# Optimizing a Trainium2 kernel written in Bass

```python
import math
import jax, jax.numpy as jnp
from jax import lax
import numpy as np

D_MODEL = 1024
BATCH = 1
SEQ = 512
DEPTH = 2

N_Q_HEADS = 8
N_KV_HEADS = 2
HEAD_DIM = 64
ATTN_WIDTH = N_Q_HEADS * HEAD_DIM
KV_WIDTH = N_KV_HEADS * HEAD_DIM
WINDOW = 128
ATTN_BLOCK = 128
GMLP_GROUPS = 4
GMLP_GROUP_DIM = 128
GMLP_WIDTH = GMLP_GROUPS * GMLP_GROUP_DIM
CHUNK = 128
SPLITS = (ATTN_WIDTH, KV_WIDTH, KV_WIDTH, ATTN_WIDTH,
          GMLP_WIDTH, GMLP_WIDTH, GMLP_WIDTH, D_MODEL, D_MODEL)
IN_WIDTH = sum(SPLITS)
ALPHA = (2 * DEPTH) ** 0.25
BETA = (8 * DEPTH) ** -0.25
LN_EPS = 1e-5


def layer_norm(x, g, b):
    xf = x.astype(jnp.float32)
    mu = xf.mean(-1, keepdims=True)
    var = jnp.square(xf - mu).mean(-1, keepdims=True)
    y = (xf - mu) * lax.rsqrt(var + LN_EPS)
    return (y * g.astype(jnp.float32) + b.astype(jnp.float32)).astype(x.dtype)

def alibi_slopes():
    h = jnp.arange(N_Q_HEADS, dtype=jnp.float32)
    return jnp.exp2(-8.0 * (h + 1.0) / N_Q_HEADS)

def split_columns(h):
    offs = [int(o) for o in np.cumsum(SPLITS)[:-1]]
    return jnp.split(h, offs, axis=-1)

def sliding_window_attention(q, k, v, sinks):
    B, S = q.shape[0], q.shape[1]
    nb = S // ATTN_BLOCK
    grp = N_Q_HEADS // N_KV_HEADS
    qb = q.reshape(B, nb, ATTN_BLOCK, N_KV_HEADS, grp, HEAD_DIM)

    def band(t):
        tb = t.reshape(B, nb, ATTN_BLOCK, N_KV_HEADS, HEAD_DIM)
        prev = jnp.pad(tb, ((0, 0), (1, 0), (0, 0), (0, 0), (0, 0)))[:, :-1]
        return jnp.concatenate([prev, tb], axis=2)

    kb, vb = band(k), band(v)
    scores = jnp.einsum('bnqhgd,bnkhd->bnhgqk', qb, kb).astype(jnp.float32) * (HEAD_DIM ** -0.5)
    qi = jnp.arange(ATTN_BLOCK)[:, None]
    kj = jnp.arange(2 * ATTN_BLOCK)[None, :]
    dist = qi + ATTN_BLOCK - kj
    blk = jnp.arange(nb)[:, None, None]
    key_pos = blk * ATTN_BLOCK + qi - dist
    valid = (dist >= 0) & (dist < WINDOW) & (key_pos >= 0)
    slopes = alibi_slopes().reshape(N_KV_HEADS, grp)
    scores = scores - slopes[:, :, None, None] * dist.astype(jnp.float32)
    scores = jnp.where(valid[None, :, None, None], scores, -jnp.inf)
    sink = sinks.astype(jnp.float32).reshape(N_KV_HEADS, grp)[None, None, :, :, None, None]
    m = jnp.maximum(scores.max(-1, keepdims=True), sink)
    p = jnp.exp(scores - m)
    denom = p.sum(-1, keepdims=True) + jnp.exp(sink - m)
    out = jnp.einsum('bnhgqk,bnkhd->bnqhgd', (p / denom).astype(v.dtype), vb)
    return out.reshape(B, S, ATTN_WIDTH)

def chunked_spatial_gating(u, v, ln_g, ln_b, w_s, b_s):
    B, S = v.shape[0], v.shape[1]
    nc = S // CHUNK
    vn = layer_norm(v, ln_g, ln_b).reshape(B, nc, CHUNK, GMLP_GROUPS, GMLP_GROUP_DIM)
    causal = jnp.tril(jnp.ones((CHUNK, CHUNK), dtype=bool))
    w = jnp.where(causal[None], w_s, jnp.zeros_like(w_s))
    mixed = jnp.einsum('gts,bcsgd->bctgd', w, vn) + b_s.T[None, None, :, :, None]
    return u * mixed.reshape(B, S, GMLP_WIDTH)

def first_inputs(seed: int = 0) -> dict:
    key = jax.random.key(seed)
    ks = jax.random.split(key, 16)
    f32 = jnp.float32
    x = jax.random.normal(ks[0], (BATCH, SEQ, D_MODEL), f32)
    w_in = jax.random.normal(ks[1], (DEPTH, D_MODEL, IN_WIDTH), f32) * D_MODEL ** -0.5
    b_in = jax.random.normal(ks[2], (DEPTH, IN_WIDTH), f32) * 0.02
    attn_sinks = jax.random.normal(ks[3], (DEPTH, N_Q_HEADS), f32) * 0.5
    gmlp_ln_g = 1.0 + 0.02 * jax.random.normal(ks[4], (DEPTH, GMLP_WIDTH), f32)
    gmlp_ln_b = 0.02 * jax.random.normal(ks[5], (DEPTH, GMLP_WIDTH), f32)
    w_spatial = jax.random.normal(ks[6], (DEPTH, GMLP_GROUPS, CHUNK, CHUNK), f32) * (0.5 * CHUNK ** -0.5)
    b_spatial = 1.0 + 0.02 * jax.random.normal(ks[7], (DEPTH, GMLP_GROUPS, CHUNK), f32)
    w_branch_attn = jax.random.normal(ks[8], (DEPTH, ATTN_WIDTH, D_MODEL), f32) * (ATTN_WIDTH ** -0.5 * BETA)
    w_branch_gmlp = jax.random.normal(ks[9], (DEPTH, GMLP_WIDTH, D_MODEL), f32) * (GMLP_WIDTH ** -0.5 * BETA)
    w_out = jax.random.normal(ks[10], (DEPTH, D_MODEL, D_MODEL), f32) * (D_MODEL ** -0.5 * BETA)
    b_out = 0.02 * jax.random.normal(ks[11], (DEPTH, D_MODEL), f32)
    ln_g = 1.0 + 0.02 * jax.random.normal(ks[12], (DEPTH, D_MODEL), f32)
    ln_b = 0.02 * jax.random.normal(ks[13], (DEPTH, D_MODEL), f32)
    return {"x": x, "w_in": w_in, "b_in": b_in, "attn_sinks": attn_sinks,
            "gmlp_ln_g": gmlp_ln_g, "gmlp_ln_b": gmlp_ln_b,
            "w_spatial": w_spatial, "b_spatial": b_spatial,
            "w_branch_attn": w_branch_attn, "w_branch_gmlp": w_branch_gmlp,
            "w_out": w_out, "b_out": b_out, "ln_g": ln_g, "ln_b": ln_b}

def first_block(x, w_in, b_in, attn_sinks, gmlp_ln_g, gmlp_ln_b, w_spatial, b_spatial,
              w_branch_attn, w_branch_gmlp, w_out, b_out, ln_g, ln_b):
    B, S = x.shape[0], x.shape[1]
    for l in range(DEPTH):
        h = jnp.einsum('bsd,de->bse', x, w_in[l]) + b_in[l]
        q, k, v, z_a, u_g, v_g, z_g, g_a, g_g = split_columns(h)
        y_a = sliding_window_attention(q.reshape(B, S, N_Q_HEADS, HEAD_DIM),
                                       k.reshape(B, S, N_KV_HEADS, HEAD_DIM),
                                       v.reshape(B, S, N_KV_HEADS, HEAD_DIM),
                                       attn_sinks[l]) * jax.nn.silu(z_a)
        y_g = chunked_spatial_gating(jax.nn.gelu(u_g, approximate=False),
                                     jax.nn.gelu(v_g, approximate=False),
                                     gmlp_ln_g[l], gmlp_ln_b[l],
                                     w_spatial[l], b_spatial[l]) * jax.nn.silu(z_g)
        br_a = jnp.einsum('bse,ed->bsd', y_a, w_branch_attn[l])
        br_g = jnp.einsum('bse,ed->bsd', y_g, w_branch_gmlp[l])
        merged = jax.nn.sigmoid(g_a) * br_a + jax.nn.sigmoid(g_g) * br_g
        out = jnp.einsum('bsd,de->bse', merged, w_out[l]) + b_out[l]
        x = layer_norm(ALPHA * x + out, ln_g[l], ln_b[l])
    return x


NSA_HEADS = 8
NSA_GROUPS = 2
NSA_HPG = NSA_HEADS // NSA_GROUPS
CMP_LEN = 32
CMP_STRIDE = 16
CMP_HIDDEN = 256
SEL_BLK = 64
N_SEL = 16
WINDOW_2 = 512
DSA_HEADS = 8
DSA_KV_RANK = 128
IDX_HEADS = 8
IDX_DIM = 64
DSA_TOPK = 256
DIFF_HEADS = 8
DIFF_DIM = 64
D_FF = 4 * D_MODEL
NUM_BUCKETS = 32
MAX_DISTANCE = 128
REL_HEADS = NSA_HEADS + DSA_HEADS
QBLK = 128
N_EVEN = (DEPTH + 1) // 2
N_ODD = DEPTH // 2
ALPHA_2 = (2 * DEPTH) ** 0.25
BETA_2 = (8 * DEPTH) ** -0.25
NEG_INF = -1e30
BIG = 1e9
EPS = 1e-5
NSA_Q = NSA_HEADS * HEAD_DIM
NSA_KV = 2 * NSA_GROUPS * HEAD_DIM
NSA_GATE = NSA_HEADS * 3
DSA_Q = DSA_HEADS * HEAD_DIM
EVEN_SIZES = (NSA_Q, NSA_KV, NSA_KV, NSA_KV, NSA_GATE, DSA_Q, DSA_KV_RANK, IDX_HEADS * IDX_DIM, IDX_DIM, IDX_HEADS)
EVEN_IN = sum(EVEN_SIZES)
EVEN_OUT = NSA_Q + DSA_HEADS * HEAD_DIM
ODD_IN = 3 * DIFF_HEADS * 2 * DIFF_DIM
ODD_OUT = DIFF_HEADS * 2 * DIFF_DIM


def _split(x, sizes):
    offs = np.cumsum(sizes)[:-1].tolist()
    return jnp.split(x, offs, axis=-1)

def layer_norm_2(x, g, b):
    xf = x.astype(jnp.float32)
    mu = jnp.mean(xf, axis=-1, keepdims=True)
    var = jnp.mean(jnp.square(xf - mu), axis=-1, keepdims=True)
    return ((xf - mu) * lax.rsqrt(var + EPS) * g + b).astype(x.dtype)

def rms_norm(x, g):
    xf = x.astype(jnp.float32)
    return (xf * lax.rsqrt(jnp.mean(jnp.square(xf), axis=-1, keepdims=True) + EPS) * g).astype(x.dtype)

def masked_softmax(logits, mask):
    z = jnp.where(mask, logits.astype(jnp.float32), NEG_INF)
    z = z - jnp.max(z, axis=-1, keepdims=True)
    e = jnp.where(mask, jnp.exp(z), 0.0)
    return e / jnp.maximum(jnp.sum(e, axis=-1, keepdims=True), 1e-30)

def t5_bucket(dist):
    n = jnp.maximum(dist, 0)
    exact = NUM_BUCKETS // 2
    nf = jnp.maximum(n, 1).astype(jnp.float32)
    large = exact + (jnp.log(nf / exact) / math.log(MAX_DISTANCE / exact) * (NUM_BUCKETS - exact)).astype(jnp.int32)
    return jnp.where(n < exact, n, jnp.minimum(large, NUM_BUCKETS - 1))

def sweep_query_blocks(fn, B, S):
    out = lax.map(fn, jnp.arange(S // QBLK))
    return jnp.moveaxis(out, 0, 1).reshape(B, S, -1)

def nsa_compress(k_raw, pe, w1, w2):
    B, S, G, Dh = k_raw.shape
    nc = (S - CMP_LEN) // CMP_STRIDE + 1
    idx = np.arange(nc)[:, None] * CMP_STRIDE + np.arange(CMP_LEN)[None, :]
    blk = k_raw[:, idx] + pe[:, None, :]
    blk = blk.transpose(0, 1, 3, 2, 4).reshape(B, nc, G, CMP_LEN * Dh)
    return jax.nn.gelu(blk @ w1) @ w2

def nsa_attention(q, kvc, kvs, kvw, gate_logits, pe_k, pe_v, w1_k, w2_k, w1_v, w2_v, bias_tab):
    B, S = q.shape[:2]
    G, HPG, Dh = NSA_GROUPS, NSA_HPG, HEAD_DIM
    q = q.reshape(B, S, G, HPG, Dh)
    kc_raw, vc_raw = [a.reshape(B, S, G, Dh) for a in jnp.split(kvc, 2, axis=-1)]
    kc = nsa_compress(kc_raw, pe_k, w1_k, w2_k)
    vc = nsa_compress(vc_raw, pe_v, w1_v, w2_v)
    ks, vs = [a.reshape(B, S, G, Dh).transpose(0, 2, 1, 3) for a in jnp.split(kvs, 2, axis=-1)]
    kw, vw = [jnp.pad(a.reshape(B, S, G, Dh), ((0, 0), (WINDOW_2, 0), (0, 0), (0, 0))) for a in jnp.split(kvw, 2, axis=-1)]
    gates = jax.nn.sigmoid(gate_logits.astype(jnp.float32)).astype(q.dtype).reshape(B, S, G, HPG, 3)
    nc = kc.shape[1]
    nb = S // SEL_BLK
    n_sel = min(N_SEL, nb)
    cs = np.arange(nc) * CMP_STRIDE
    ss = np.arange(nb) * SEL_BLK
    overlap = np.clip(np.minimum(cs[:, None] + CMP_LEN, ss[None, :] + SEL_BLK) - np.maximum(cs[:, None], ss[None, :]), 0, None)
    imp = jnp.asarray(overlap / CMP_STRIDE, dtype=jnp.float32)
    cmp_end = jnp.asarray(cs + CMP_LEN - 1, dtype=jnp.int32)
    tab = bias_tab.reshape(NUM_BUCKETS, G, HPG)
    scale = Dh ** -0.5
    bi = jnp.arange(B)[:, None, None, None]
    gi = jnp.arange(G)[None, :, None, None]
    jblk = jnp.arange(nb)

    def block(qb):
        q0 = qb * QBLK
        t = q0 + jnp.arange(QBLK)
        qq = lax.dynamic_slice_in_dim(q, q0, QBLK, axis=1)
        gg = lax.dynamic_slice_in_dim(gates, q0, QBLK, axis=1)
        dc = t[:, None] - cmp_end[None, :]
        bias_c = tab[t5_bucket(dc)].transpose(2, 3, 0, 1)
        lc = jnp.einsum('bqghd,bngd->bghqn', qq, kc) * scale + bias_c
        pc = masked_softmax(lc, dc >= 0)
        oc = jnp.einsum('bghqn,bngd->bqghd', pc.astype(vc.dtype), vc)
        score = jnp.einsum('bghqn,nj->bgqj', pc, imp)
        cb = (t // SEL_BLK)[:, None]
        allowed = jblk[None, :] * SEL_BLK <= t[:, None]
        forced = (jblk[None, :] == 0) | (jblk[None, :] == cb) | (jblk[None, :] == cb - 1)
        score = jnp.where(forced, BIG, jnp.where(allowed, score, -BIG))
        _, sel = lax.top_k(score, n_sel)
        tok = (sel[..., None] * SEL_BLK + jnp.arange(SEL_BLK)).reshape(B, G, QBLK, n_sel * SEL_BLK)
        k_sel = ks[bi, gi, tok]
        v_sel = vs[bi, gi, tok]
        dist = t[None, None, :, None] - tok
        bias_s = tab[t5_bucket(dist), gi].transpose(0, 1, 4, 2, 3)
        ls = jnp.einsum('bqghd,bgqtd->bghqt', qq, k_sel) * scale + bias_s
        ps = masked_softmax(ls, (dist >= 0)[:, :, None])
        o_s = jnp.einsum('bghqt,bgqtd->bqghd', ps.astype(v_sel.dtype), v_sel)
        kwb = lax.dynamic_slice_in_dim(kw, q0, WINDOW_2 + QBLK, axis=1)
        vwb = lax.dynamic_slice_in_dim(vw, q0, WINDOW_2 + QBLK, axis=1)
        s = q0 - WINDOW_2 + jnp.arange(WINDOW_2 + QBLK)
        dw = t[:, None] - s[None, :]
        mask_w = (dw >= 0) & (dw < WINDOW_2) & (s[None, :] >= 0)
        bias_w = tab[t5_bucket(dw)].transpose(2, 3, 0, 1)
        lw = jnp.einsum('bqghd,bsgd->bghqs', qq, kwb) * scale + bias_w
        pw = masked_softmax(lw, mask_w)
        o_w = jnp.einsum('bghqs,bsgd->bqghd', pw.astype(vwb.dtype), vwb)
        out = gg[..., 0:1] * oc + gg[..., 1:2] * o_s + gg[..., 2:3] * o_w
        return out.reshape(B, QBLK, G * HPG * Dh)

    return sweep_query_blocks(block, B, S)

def dsa_attention(q, kv_lat, iq, ik, iw, kv_norm, w_uk, w_uv, bias_tab):
    B, S = q.shape[:2]
    ckv = rms_norm(kv_lat, kv_norm)
    q_lat = jnp.einsum('bshd,rhd->bshr', q, w_uk)
    iq = iq.reshape(B, S, IDX_HEADS, IDX_DIM)
    iw = iw * (IDX_HEADS ** -0.5 * IDX_DIM ** -0.5)
    topk = min(DSA_TOPK, S // 4)
    scale = HEAD_DIM ** -0.5
    bi = jnp.arange(B)[:, None, None]
    spos = jnp.arange(S)

    def block(qb):
        q0 = qb * QBLK
        t = q0 + jnp.arange(QBLK)
        iqb = lax.dynamic_slice_in_dim(iq, q0, QBLK, axis=1)
        iwb = lax.dynamic_slice_in_dim(iw, q0, QBLK, axis=1)
        qlb = lax.dynamic_slice_in_dim(q_lat, q0, QBLK, axis=1)
        rel = jax.nn.relu(jnp.einsum('bqjd,bsd->bqjs', iqb, ik))
        isc = jnp.einsum('bqj,bqjs->bqs', iwb, rel).astype(jnp.float32)
        isc = jnp.where(spos[None, None, :] <= t[None, :, None], isc, NEG_INF)
        _, idx = lax.top_k(isc, topk)
        c_sel = ckv[bi, idx]
        dist = t[None, :, None] - idx
        bias = bias_tab[t5_bucket(dist)].transpose(0, 3, 1, 2)
        logits = jnp.einsum('bqhr,bqkr->bhqk', qlb, c_sel) * scale + bias
        p = masked_softmax(logits, (dist >= 0)[:, None])
        o_lat = jnp.einsum('bhqk,bqkr->bqhr', p.astype(c_sel.dtype), c_sel)
        o = jnp.einsum('bqhr,rhd->bqhd', o_lat, w_uv)
        return o.reshape(B, QBLK, DSA_HEADS * HEAD_DIM)

    return sweep_query_blocks(block, B, S)

def even_mixer(h, w_in, w_out, pe_k, pe_v, w1_k, w2_k, w1_v, w2_v, kv_norm, w_uk, w_uv, rel_bias):
    B, S, _ = h.shape
    nsa_q, kvc, kvs, kvw, gate, dsa_q, dsa_kv, idx_q, idx_k, idx_w = _split(h @ w_in, EVEN_SIZES)
    o_a = nsa_attention(nsa_q, kvc, kvs, kvw, gate, pe_k, pe_v, w1_k, w2_k, w1_v, w2_v, rel_bias[:, :NSA_HEADS])
    o_b = dsa_attention(dsa_q.reshape(B, S, DSA_HEADS, HEAD_DIM), dsa_kv, idx_q, idx_k, idx_w, kv_norm, w_uk, w_uv, rel_bias[:, NSA_HEADS:])
    return jnp.concatenate([o_a, o_b], axis=-1) @ w_out

def diff_mixer(h, w_in, w_out, lam, subln, rel_bias, lambda_init):
    B, S, _ = h.shape
    q, k, v = jnp.split(h @ w_in, 3, axis=-1)
    q = q.reshape(B, S, DIFF_HEADS, 2, DIFF_DIM)
    k = k.reshape(B, S, DIFF_HEADS, 2, DIFF_DIM)
    v = v.reshape(B, S, DIFF_HEADS, 2 * DIFF_DIM)
    lamf = lam.astype(jnp.float32)
    lam_full = jnp.exp(jnp.sum(lamf[0] * lamf[1])) - jnp.exp(jnp.sum(lamf[2] * lamf[3])) + lambda_init
    tab = rel_bias.reshape(NUM_BUCKETS, DIFF_HEADS, 2)
    scale = DIFF_DIM ** -0.5
    spos = jnp.arange(S)

    def block(qb):
        q0 = qb * QBLK
        t = q0 + jnp.arange(QBLK)
        qq = lax.dynamic_slice_in_dim(q, q0, QBLK, axis=1)
        dist = t[:, None] - spos[None, :]
        bias = tab[t5_bucket(dist)].transpose(2, 3, 0, 1)
        logits = jnp.einsum('bqhmd,bshmd->bhmqs', qq, k) * scale + bias
        p = masked_softmax(logits, dist >= 0)
        pd = p[:, :, 0] - lam_full * p[:, :, 1]
        o = jnp.einsum('bhqs,bshe->bqhe', pd.astype(v.dtype), v)
        o = rms_norm(o, subln) * (1.0 - lambda_init)
        return o.reshape(B, QBLK, DIFF_HEADS * 2 * DIFF_DIM)

    return sweep_query_blocks(block, B, S) @ w_out

def sq_relu_mlp(h, w1, w2):
    return jnp.square(jax.nn.relu(h @ w1)) @ w2

def modulate(x, shift, scale):
    return x * (1.0 + scale[:, None, :]) + shift[:, None, :]

def second_inputs(seed: int = 0) -> dict:
    key = jax.random.key(seed)
    ks = jax.random.split(key, 26)
    f32 = jnp.float32

    def nrm(k, shape, fan_in, s=1.0):
        return jax.random.normal(k, shape, f32) * (s * fan_in ** -0.5)

    D = D_MODEL
    return {
        "x": jax.random.normal(ks[0], (BATCH, SEQ, D), f32),
        "c": jax.random.normal(ks[1], (BATCH, D), f32),
        "rel_bias": 0.5 * jax.random.normal(ks[2], (NUM_BUCKETS, REL_HEADS), f32),
        "ada_w": nrm(ks[3], (DEPTH, D, 6 * D), D, 0.2),
        "ada_b": 0.01 * jax.random.normal(ks[4], (DEPTH, 6 * D), f32),
        "ln_g": 1.0 + 0.02 * jax.random.normal(ks[5], (DEPTH, 2, D), f32),
        "ln_b": 0.02 * jax.random.normal(ks[6], (DEPTH, 2, D), f32),
        "ev_w_in": nrm(ks[7], (N_EVEN, D, EVEN_IN), D),
        "ev_w_out": nrm(ks[8], (N_EVEN, EVEN_OUT, D), EVEN_OUT, BETA_2),
        "nsa_pe_k": 0.5 * jax.random.normal(ks[9], (N_EVEN, CMP_LEN, HEAD_DIM), f32),
        "nsa_pe_v": 0.5 * jax.random.normal(ks[10], (N_EVEN, CMP_LEN, HEAD_DIM), f32),
        "nsa_w1_k": nrm(ks[11], (N_EVEN, CMP_LEN * HEAD_DIM, CMP_HIDDEN), CMP_LEN * HEAD_DIM),
        "nsa_w2_k": nrm(ks[12], (N_EVEN, CMP_HIDDEN, HEAD_DIM), CMP_HIDDEN),
        "nsa_w1_v": nrm(ks[13], (N_EVEN, CMP_LEN * HEAD_DIM, CMP_HIDDEN), CMP_LEN * HEAD_DIM),
        "nsa_w2_v": nrm(ks[14], (N_EVEN, CMP_HIDDEN, HEAD_DIM), CMP_HIDDEN),
        "dsa_kv_norm": 1.0 + 0.02 * jax.random.normal(ks[15], (N_EVEN, DSA_KV_RANK), f32),
        "dsa_w_uk": nrm(ks[16], (N_EVEN, DSA_KV_RANK, DSA_HEADS, HEAD_DIM), DSA_KV_RANK),
        "dsa_w_uv": nrm(ks[17], (N_EVEN, DSA_KV_RANK, DSA_HEADS, HEAD_DIM), DSA_KV_RANK),
        "od_w_in": nrm(ks[18], (N_ODD, D, ODD_IN), D),
        "od_w_out": nrm(ks[19], (N_ODD, ODD_OUT, D), ODD_OUT, BETA_2),
        "diff_lam": 0.1 * jax.random.normal(ks[20], (N_ODD, 4, DIFF_DIM), f32),
        "diff_subln": 1.0 + 0.02 * jax.random.normal(ks[21], (N_ODD, 2 * DIFF_DIM), f32),
        "mlp_w1": nrm(ks[22], (DEPTH, D, D_FF), D),
        "mlp_w2": nrm(ks[23], (DEPTH, D_FF, D), D_FF, BETA_2),
    }

def second_block(x, c, rel_bias, ada_w, ada_b, ln_g, ln_b, ev_w_in, ev_w_out, nsa_pe_k, nsa_pe_v, nsa_w1_k, nsa_w2_k, nsa_w1_v, nsa_w2_v, dsa_kv_norm, dsa_w_uk, dsa_w_uv, od_w_in, od_w_out, diff_lam, diff_subln, mlp_w1, mlp_w2):
    c_act = jax.nn.silu(c)
    for l in range(DEPTH):
        ada = c_act @ ada_w[l] + ada_b[l]
        sh1, sc1, g1, sh2, sc2, g2 = jnp.split(ada, 6, axis=-1)
        h = modulate(x, sh1, sc1)
        i = l // 2
        if l % 2 == 0:
            y = even_mixer(h, ev_w_in[i], ev_w_out[i], nsa_pe_k[i], nsa_pe_v[i], nsa_w1_k[i], nsa_w2_k[i], nsa_w1_v[i], nsa_w2_v[i], dsa_kv_norm[i], dsa_w_uk[i], dsa_w_uv[i], rel_bias)
        else:
            lambda_init = 0.8 - 0.6 * math.exp(-0.3 * l)
            y = diff_mixer(h, od_w_in[i], od_w_out[i], diff_lam[i], diff_subln[i], rel_bias, lambda_init)
        x = layer_norm_2(ALPHA_2 * x + (1.0 + g1[:, None, :]) * y, ln_g[l, 0], ln_b[l, 0])
        h = modulate(x, sh2, sc2)
        y = sq_relu_mlp(h, mlp_w1[l], mlp_w2[l])
        x = layer_norm_2(ALPHA_2 * x + (1.0 + g2[:, None, :]) * y, ln_g[l, 1], ln_b[l, 1])
    return x


def setup_inputs(seed=0):
    out = dict(first_inputs(seed))
    for name, value in second_inputs(seed + 1).items():
        if name != "x":
            out[name + "_2"] = value
    return out


def reference(
    x, w_in, b_in, attn_sinks, gmlp_ln_g, gmlp_ln_b, w_spatial, b_spatial, w_branch_attn,
    w_branch_gmlp, w_out, b_out, ln_g, ln_b, c_2, rel_bias_2, ada_w_2, ada_b_2, ln_g_2, ln_b_2,
    ev_w_in_2, ev_w_out_2, nsa_pe_k_2, nsa_pe_v_2, nsa_w1_k_2, nsa_w2_k_2, nsa_w1_v_2,
    nsa_w2_v_2, dsa_kv_norm_2, dsa_w_uk_2, dsa_w_uv_2, od_w_in_2, od_w_out_2, diff_lam_2,
    diff_subln_2, mlp_w1_2, mlp_w2_2,
):
    x = first_block(
        x, w_in, b_in, attn_sinks, gmlp_ln_g, gmlp_ln_b, w_spatial, b_spatial, w_branch_attn,
        w_branch_gmlp, w_out, b_out, ln_g, ln_b,
    )
    return second_block(
        x, c_2, rel_bias_2, ada_w_2, ada_b_2, ln_g_2, ln_b_2, ev_w_in_2, ev_w_out_2, nsa_pe_k_2,
        nsa_pe_v_2, nsa_w1_k_2, nsa_w2_k_2, nsa_w1_v_2, nsa_w2_v_2, dsa_kv_norm_2, dsa_w_uk_2,
        dsa_w_uv_2, od_w_in_2, od_w_out_2, diff_lam_2, diff_subln_2, mlp_w1_2, mlp_w2_2,
    )


_drawn_inputs = setup_inputs


def setup_inputs(seed=0):
    import zlib

    import numpy as np

    out = dict(_drawn_inputs(seed))
    spreads = {}
    factors = {'b_in': 8.0,
     'attn_sinks': 8.0,
     'gmlp_ln_g': 8.0,
     'gmlp_ln_b': 8.0,
     'w_spatial': 2.811,
     'b_spatial': 8.0,
     'ada_b_2': 3.633,
     'nsa_pe_k_2': 8.0,
     'nsa_w1_k_2': 3.494,
     'nsa_w2_k_2': 3.588,
     'dsa_kv_norm_2': 8.0,
     'diff_subln_2': 8.0}
    for name, (base, spread) in spreads.items():
        noise = np.random.default_rng([zlib.crc32(name.encode()), seed]).standard_normal(out[name].shape)
        drawn = base * np.exp(spread * noise) if base else spread * noise
        out[name] = __import__('jax').numpy.asarray(drawn.astype(out[name].dtype))
    for name, factor in factors.items():
        out[name] = (out[name] * factor).astype(out[name].dtype)
    return out
```

```python
from contextlib import ExitStack
import math

import numpy as np
import concourse.bass as bass
from concourse import mybir

ALU = mybir.AluOpType
ACT = mybir.ActivationFunctionType
F32 = mybir.dt.float32
AX_X = mybir.AxisListType.X

P = 128
S = 512
NT = S // P
D = 1024
KT = D // P
DEPTH = 2
HEADS = 8
HD = 64
W1 = 4864
EVEN_IN = 2528
ODD_IN = 3072
DFF = 4096
ALPHA = float(np.float32((2 * DEPTH) ** 0.25))
EPS = 1e-5
MASKED = 1e30
HUGE = 3e38
TOPK = 128
BUCKETS = 32
NCMP = 31
CHUNK = 8 * 512
RING = 3
BANKS = 6
TW = 640
LAMBDA_INIT = 0.8 - 0.6 * math.exp(-0.3)
ORDER = (0, 2, 1, 3)
ZOFF = (0, 128, 384, 768)
KOFF = (0, 512, 896, 1152)


def buckets_of(dist):
    n = np.maximum(dist, 0)
    exact = BUCKETS // 2
    nf = np.maximum(n, 1).astype(np.float32)
    large = exact + (np.log(nf / exact) / math.log(128 / exact) * (BUCKETS - exact)).astype(np.int32)
    return np.where(n < exact, n, np.minimum(large, BUCKETS - 1))


def one_hot(dist):
    out = np.zeros((BUCKETS + 1, len(dist)), np.float32)
    b = buckets_of(dist)
    for i, d in enumerate(dist):
        if d >= 0:
            out[b[i], i] = 1.0
        else:
            out[BUCKETS, i] = 1.0
    return out


def shape_constants():
    ident = np.eye(P, dtype=np.float32)
    s, t = np.arange(P)[:, None], np.arange(P)[None, :]
    tril = (t <= s).astype(np.float32)
    dist = np.arange(P)[:, None] + P - np.arange(2 * P)[None, :]
    valid = (dist >= 0) & (dist < P)
    alibi = np.stack([np.where(valid, np.float32(2.0 ** -(h + 1)) * dist, MASKED) for h in range(HEADS)], 1)
    future = np.where(t <= s, 0.0, -1e30)
    wide = one_hot(511 - np.arange(TW))
    full = one_hot(np.arange(1024) - 511)
    return {
        "ident": ident, "tril": tril, "alibi": alibi.astype(np.float32).reshape(P, HEADS * 2 * P),
        "future": future.astype(np.float32), "hot_rev": wide, "hot": full,
    }


class Unit:
    def __init__(self, index, who, drained):
        self.index, self.who, self.drained = index, who, drained
        self.bank, self.full = index % BANKS, index + 1


class Job:
    pass


class Plan:

    def __init__(self):
        self.units, self.order, self.count = {}, [], {"act": 0, "dve": 0, "z": 0}
        self.chunks, self.chunk = [], {}
        self.jobs = []
        self.cur = {"z": 0, "p": 0, "s": 0, "m": 0, "r": 0, "pt": 0, "o": 0}

    def unit(self, key, who, n=1):
        self.count[who] += n
        u = Unit(len(self.order), who, self.count[who])
        assert key not in self.units, key
        self.units[key] = u
        self.order.append(u)
        return u

    def load(self, name, last):
        self.chunk[name] = len(self.chunks)
        self.chunks.append((name, last))

    def job(self, kind, h, l=0, m=0):
        j = Job()
        j.kind, j.h, j.l, j.m, j.J = kind, h, l, m, len(self.jobs)
        j.slot = j.J % 4
        j.key = (kind, l, h, m)
        n = 1 if kind == "cmp" else 4
        j.z0, j.p0, j.s0 = self.cur["z"], self.cur["p"], self.cur["s"]
        self.cur["z"] += n
        self.cur["p"] += n
        self.cur["s"] += 5 if kind == "diff" and m == 1 else n
        self.cur["r"] += 1
        self.cur["m"] += kind in ("swa", "cmp")
        j.mr = self.cur["m"]
        j.r_count = self.cur["r"]
        j.z, j.p, j.s = self.cur["z"], self.cur["p"], self.cur["s"]
        j.has_pt = not (kind == "diff" and m == 0)
        if j.has_pt:
            j.pt = self.cur["pt"]
            self.cur["pt"] += 1
            j.pv = self.cur["pt"]
            if kind == "swa":
                j.first_o, j.last_o = True, h >= 4
                new_o = h < 4
            elif kind in ("cmp", "sel", "win"):
                new_o = kind == "cmp" and h < 4
                j.first_o, j.last_o = kind == "cmp", kind == "win" and h >= 4
            else:
                new_o, j.first_o, j.last_o = True, True, True
            j.new_o = new_o
            if new_o:
                self.cur["o"] += 1
            j.o = self.cur["o"] - 1
        self.jobs.append(j)
        return j

    def s_units(self, j):
        if j.kind == "swa":
            for i in range(2):
                self.unit(("S", j.J, i), "z", 2)
        elif j.kind == "cmp":
            self.unit(("S", j.J, 0), "z", 1)
        else:
            for i, n in enumerate((2, 1, 1)):
                self.unit(("S", j.J, i), "z", n)

    def t_units(self, j):
        if not j.has_pt:
            return
        if j.kind == "swa":
            whos = ("act", "dve")
        elif j.kind == "cmp":
            whos = ("act",)
        else:
            whos = ("act", "dve", "act")
        for i, who in enumerate(whos):
            self.unit(("T", j.J, i), who)
        j.ptn = len(whos)


PAIRS = (0, 4, 1, 5, 2, 6, 3, 7)


def make_plan():
    pl = Plan()
    U = pl.unit
    for i in range(3):
        U(("vec", i), "dve")
    for i in range(2):
        U(("bias", i), "act")
    for k in range(KT):
        U(("xT", k), "dve" if k % 2 else "act")

    def ada(n):
        U(("ada", n), "dve")
        pl.load(("ada", n), ("ada", n))

    pl.swa = []
    for l in range(DEPTH):
        U(("wT", l), "dve")
        a = 12 * l
        pl.load(("vg", l), ("vg", l, 3))
        for t in range(4):
            U(("vg", l, t), "dve")
        ada(a)
        for i, name in enumerate(("u", "za", "zg")):
            pl.load((name, l), (name, l, 3))
            for t in range(4):
                U((name, l, t), "act")
            ada(a + 1 + i)
        pl.load(("kv", l), ("v", l))
        U(("k", l), "act")
        U(("v", l), "dve")
        ada(a + 4)
        pl.load(("q", l), ("q", l, 3))
        for t in range(4):
            U(("q", l, t), "dve")
        ada(a + 5)
        for g in range(4):
            U(("sp", l, g), "dve")
        jobs = [pl.job("swa", h, l) for h in PAIRS]
        pl.swa.append(jobs)
        pl.s_units(jobs[0])
        pl.s_units(jobs[1])
        for s in range(9):
            if s + 2 < 8:
                pl.s_units(jobs[s + 2])
            if s < 8:
                c = s // 2
                if s % 2 == 0:
                    pl.load(("g", l, c), ("g", l, 4 * c + 3))
                for t in range(2 * s, 2 * s + 2):
                    U(("g", l, t), "act")
                if s % 2 == 1:
                    ada(a + 6 + c)
                pl.t_units(jobs[s])
        pl.load(("ba", l), ("ba", l, 7))
        pl.load(("bg", l), ("bg", l, 7))
        for t in range(KT):
            U(("ba", l, t), "dve")
            U(("bg", l, t), "dve")
        ada(a + 10)
        ada(a + 11)
        for c in range(2):
            pl.load(("out", l, c), ("out", l, 4 * c + 3))
            for t in range(4 * c, 4 * c + 4):
                U(("out", l, t), "dve")

    U("biasc0", "act")
    U("biasc1", "act")
    U("ukT", "dve")
    pl.load("lat", "iw")
    U("lat", "dve")
    U("ik", "act")
    U("iw", "dve")
    pl.load("iq", ("iq", 3))
    for t in range(4):
        U(("iq", t), "act")
    U("ckvT", "dve")
    for qb in range(1, 4):
        for j in range(8):
            U(("I", qb, j), "act")
    pl.load("dq", ("dq", 3))
    for t in range(4):
        U(("dq", t), "act")
    pl.load("cs", "vs")
    for n in ("kc", "vc", "ks", "vs"):
        U(n, "act")
    pl.load("wg", "gate")
    for n in ("kw", "vw", "gate"):
        U(n, "act")
    pl.load("nq", ("nq", 3))
    for t in range(4):
        U(("nq", t), "act")
    for h in range(8):
        U(("ql", h), "act")
    for kind in range(2):
        pl.load(("w1", kind), ("hid", kind, 1))
        for half in range(2):
            U(("hid", kind, half), "act")
    U("kcT", "act")
    U("vct", "act")
    jobs = [pl.job(kind, h) for h in PAIRS for kind in ("cmp", "sel", "win")]
    jobs += [pl.job("dsa", h) for h in range(8)]
    pl.even = jobs
    steps(pl, jobs)
    mixer_out(pl, 0)
    mlp(pl, 0)
    for c in range(2):
        pl.load(("oq", c), ("oq", 4 * c + 3))
        for t in range(4 * c, 4 * c + 4):
            U(("oq", t), "act" if t % 2 else "dve")
    for c in range(2):
        pl.load(("ok", c), ("ok", 4 * c + 3))
        for t in range(4 * c, 4 * c + 4):
            U(("ok", t), "act" if t % 2 else "dve")
    for c in range(2):
        pl.load(("ov", c), ("ov", 4 * c + 3))
        for t in range(4 * c, 4 * c + 4):
            U(("ov", t), "act" if t % 2 else "dve")
    jobs = [pl.job("diff", h, m=m) for h in range(8) for m in range(2)]
    pl.odd = jobs
    steps(pl, jobs)
    mixer_out(pl, 1)
    mlp(pl, 1)
    for tt in range(NT):
        for c in range(2):
            U(("y", tt, c), "act" if c else "dve")
    return pl


def steps(pl, jobs):
    n = len(jobs)
    pl.s_units(jobs[0])
    pl.s_units(jobs[1])
    for s in range(n + 2):
        if s + 2 < n:
            pl.s_units(jobs[s + 2])
        if s < n:
            pl.t_units(jobs[s])
        if 0 <= s - 2 < n:
            j = jobs[s - 2]
            if j.kind == "dsa":
                pl.unit(("uv", j.h), "act")
            if j.kind == "diff" and j.m:
                pl.unit(("ms", j.h), "dve")


def mixer_out(pl, i):
    for c in range(2):
        pl.load(("mo", i, c), ("mo", i, 4 * c + 3))
        for t in range(4 * c, 4 * c + 4):
            pl.unit(("mo", i, t), "dve")


def mlp(pl, i):
    for c in range(8):
        pl.load(("m1", i, c), ("m1", i, 4 * c + 3))
        for t in range(4 * c, 4 * c + 4):
            pl.unit(("m1", i, t), "act")
    for c in range(2):
        for kc in range(4):
            pl.load(("m2", i, c, kc), ("m2", i, 4 * c + 3) if kc == 3 else 6 * i + 3 * c + kc + 1)
        for t in range(4 * c, 4 * c + 4):
            pl.unit(("m2", i, t), "dve")


N_VEC, N_E = 19, 9

N_A, N_B, N_C = 124, 128, 41


def vec_a(l, name, t=0):
    at = {"q": 0, "k": 4, "v": 5, "za": 6, "u": 10, "vg": 14, "zg": 18, "g": 22,
          "b_out": 38, "ln_g": 46, "ln_b": 54}[name]
    return 62 * l + at + t


def vec_b(i, name, t=0):
    if name == "ada_b":
        return N_A + 48 * i + t
    if name == "ln_g":
        return N_A + 96 + 8 * i + t
    if name == "ln_b":
        return N_A + N_B + 8 * i + t
    return N_A + N_B + {"subln": 32, "c": 33}[name] + t


ADA = {"sh1": 0, "sc1": 8, "g1": 16, "sh2": 24, "sc2": 32, "g2": 40}


class Steps:

    def __init__(self, eng, sem):
        self.eng, self.sem, self.n = eng, sem, 0

    def step(self, ins):
        self.n += 1
        return ins.then_inc(self.sem, 1)

    def settle(self):
        self.eng.wait_ge(self.sem, self.n)


def two_blocks(nc, a, out):
    pl = make_plan()
    u = pl.units
    bias_rows = nc.dram_tensor("bias_rows", (16, P, TW), F32, kind="Internal").ap()

    with ExitStack() as ctx:
        def sb(name, cols):
            return ctx.enter_context(nc.sbuf_tensor(name, [P, cols], F32))

        def sem(name):
            return ctx.enter_context(nc.semaphore(name))

        ring = sb("ring", RING * CHUNK)
        x = sb("x", KT * S)
        hreg = sb("hreg", KT * S)
        mix = sb("mix", KT * S)
        arena = sb("arena", 32 * S)
        side = sb("side", 10624)
        cols = sb("cols", N_A + N_B + N_C)
        adac = sb("adac", 2 * 48)
        ident = sb("ident", P)
        mean_w = sb("mean_w", P)
        head_w = sb("head_w", P)
        tril = sb("tril", P)
        negm = sb("negm", 16)
        sums = sb("sums", 16)
        recips = sb("recips", 16)
        esink = sb("esink", 16)
        sinks = sb("sinks", 2 * HEADS)
        nsinks = sb("nsinks", 2 * HEADS)
        stats = sb("stats", 4 * 6 + 4 * 2 + 4)
        cact = sb("cact", KT)
        small = sb("small", 8)
        eps = sb("eps", 1)
        psum = ctx.enter_context(nc.psum_tensor("psum", [P, 8, 512], F32))

        def tile(t, i, n=S):
            return t[:, i * n:(i + 1) * n]

        def X(t):
            return tile(x, t)

        def H(t):
            return tile(hreg, t)

        def M(t):
            return tile(mix, t)

        def A(off, n=S):
            return arena[:, off:off + n]

        b1_u, b1_za, b1_zg, b1_vn, b1_q = 0, 2048, 4096, 6144, 8192
        b1_k, b1_v, b1_ga, b1_tmp = 10240, 10752, 11264, 15360
        PTOFF, SWA_Z = 3584, 896
        alibi = side[:, 5376:7424]
        bv_row, bvg_row = side[:, 7424:7552], side[:, 7552:8064]
        lng_row, lnb_row = side[:, 8064:8576], side[:, 8576:9088]
        bs_row = side[:, 9088:9600]
        ws_raw, ws_t = side[:, 9600:10112], side[:, 10112:10624]

        def ga(i):
            return A(b1_ga + i * S) if i < 8 else H(i - 8)

        T_AT = 7680
        biasc = side[:, 9216:9216 + 4 * 8 * NCMP]
        e_q, e_dq, e_ql, e_ks, e_vs, e_kw, e_vw = 0, 2048, 4096, 8192, 8704, 9216, 9728
        e_ckv, e_ckvT, e_ik, e_iq, e_kc, e_vc = 10240, 10752, 11264, 11776, 13824, 14336
        kcT = A(14848, NCMP)
        vct = A(14880, P)
        hid = A(15008, 248)
        gates = A(15264, 96)
        iw = A(15360, 32)
        w2kv = A(15392, 256)
        kvnorm = A(15648, P)
        ukT = A(15776, S)
        peT = A(16288, 32)
        m8 = A(16320, 24)
        e_olat, w_uv = 2048, A(3072, S)
        hot_full, tab_full = side[:, 5120:6144], side[:, 6144:6160]
        uk_raw = side[:, 6656:7168]
        rp_at = 2560
        o_q, o_k, o_v, o_sq = 0, 4096, 8192, 12288
        lam_in = A(14336, 256)
        lam_tmp = A(14592, 128)
        lamc = small[:, 0:4]
        rstd = A(15872)
        work_at = {1: 2048, 2: 2304, 3: 2688}
        selm_at = {1: 0, 2: 256, 3: 640}

        def zbuf(j):
            n = SWA_Z if j.kind == "swa" else 1280
            return side[:, j.slot * n:(j.slot + 1) * n]

        def ptbuf(j):
            n, at = (SWA_Z, PTOFF) if j.kind == "swa" else (1280, 5120)
            return side[:, at + (j.pt % 2) * n:at + (j.pt % 2 + 1) * n]

        def stat4(t, j, i=None):
            return t[:, 4 * j.slot:4 * j.slot + 4] if i is None else t[:, 4 * j.slot + i:4 * j.slot + i + 1]

        def tbuf(ti):
            return side[:, T_AT + (ti % 3) * S:T_AT + (ti % 3 + 1) * S]

        tables = [h for h in PAIRS] + [8 + h for h in range(8)] + list(range(16))
        for i, j in enumerate(pl.even):
            j.ti = i // 3 if j.kind != "dsa" else 8 + j.h
            j.t_last = j.kind in ("win", "dsa")
        for i, j in enumerate(pl.odd):
            j.ti, j.t_last = 16 + i, True

        psum_full = sem("psum_full")
        act_drained = sem("act_drained")
        dve_drained = sem("dve_drained")
        z_ready = sem("z_ready")
        m_ready = sem("m_ready")
        p_ready = sem("p_ready")
        sink_ready = sem("sink_ready")
        r_ready = sem("r_ready")
        s_ready = sem("s_ready")
        pv_done = sem("pv_done")
        o_drained = sem("o_drained")
        landed = [sem(f"landed{i}") for i in range(RING)]
        m2_used = sem("m2_used")
        const_in, x_in, rows_in = sem("const_in"), sem("x_in"), sem("rows_in")
        vec_in, tab_in = sem("vec_in"), sem("tab_in")
        e_in, r_in, uv_in, lam_sem = sem("e_in"), sem("r_in"), sem("uv_in"), sem("lam_sem")
        t_in = [sem(f"t_in{i}") for i in range(3)]
        memsets, bias_out = sem("memsets"), sem("bias_out")
        c_ready, ada_ready = sem("c_ready"), sem("ada_ready")
        ws_masked = sem("ws_masked")
        vg_gelu, vn_norm, vn_ready = sem("vg_gelu"), sem("vn_norm"), sem("vn_ready")
        uz_ready, yg_ready = sem("uz_ready"), sem("yg_ready")
        sig_ready, merged = sem("sig_ready"), sem("merged")
        res_scaled = sem("res_scaled")
        ln_centered, ln_squared, stat_full = sem("ln_centered"), sem("ln_squared"), sem("stat_full")
        ln_scaled, x_ready, h_ready = sem("ln_scaled"), sem("x_ready"), sem("h_ready")
        nsink_ready = sem("nsink_ready")
        std_ready, var_ready = sem("std_ready"), sem("var_ready")
        lat_done, relu_ready, isc_used = sem("lat_done"), sem("relu_ready"), sem("isc_used")
        selm_ready, rp_ready = sem("selm_ready"), sem("rp_ready")
        hidden_ready = sem("hidden_ready")
        sq_ready, o_normed = sem("sq_ready"), sem("o_normed")
        lam_ready, lam_dots = sem("lam_ready"), sem("lam_dots")
        y_out = sem("y_out")
        dve_own, pool_own = sem("dve_own"), sem("pool_own")
        drained_by = {"act": act_drained, "dve": dve_drained, "z": z_ready}

        def bcast(ap, n, off=0):
            return bass.AP(tensor=ap.tensor, offset=ap.offset + off, ap=[[0, P], [1, n]])

        def full(eng, key):
            eng.wait_ge(psum_full, u[key].full)
            return psum[:, u[key].bank, :]

        def taken(eng, key):
            eng.wait_ge(drained_by[u[key].who], u[key].drained)

        block = ctx.enter_context(nc.Block())

        def pieces(name):
            kind = name[0] if isinstance(name, tuple) else name

            def plain(w, c0, n):
                return (KT, n), [(slice(0, P), slice(0, KT), slice(0, n),
                                  w.rearrange("(k p) n -> p k n", p=P)[:, :, c0:c0 + n])]

            def split(w, c0, n, kt, paired):
                out_ = []
                for hf in range(2):
                    src = w[hf * 256:hf * 256 + 256, c0:c0 + n].rearrange("(t d) n -> d t n", d=HD)
                    out_.append((slice(hf * HD, hf * HD + HD), slice(0, 4), slice(0, n), src))
                if kt > paired:
                    out_.append((slice(0, P), slice(4, kt), slice(0, n),
                                 w[512:1024, c0:c0 + n].rearrange("(k p) n -> p k n", p=P)))
                return (kt, n), out_

            if kind == "ada":
                l, c = divmod(name[1], 12)
                return plain(a["ada_w_2"][l], 512 * c, 512)
            def paired_columns(w, c0):
                src = w.rearrange("(k p) n -> p k n", p=P)[:, :, c0:c0 + 512].rearrange(
                    "p k (b t d) -> b p k t d", b=2, d=HD)
                return (KT, 512), [(k, b, None, src[b, :, k]) for b in range(2) for k in range(KT)]

            at1 = {"q": 0, "kv": 512, "za": 768, "u": 1280, "vg": 1792, "zg": 2304}
            if kind in ("q", "za"):
                return paired_columns(a["w_in"][name[1]], at1[kind])
            if kind in at1:
                return plain(a["w_in"][name[1]], at1[kind], 256 if kind == "kv" else 512)
            if kind == "g":
                return plain(a["w_in"][name[1]], 2816 + 512 * name[2], 512)
            if kind == "ba":
                return split(a["w_branch_attn"][name[1]], 0, D, 4, 4)
            if kind == "bg":
                w = a["w_branch_gmlp"][name[1]]
                return (4, D), [(slice(0, P), slice(0, 4), slice(0, D), w.rearrange("(k p) n -> p k n", p=P))]
            if kind == "out":
                return plain(a["w_out"][name[1]], 512 * name[2], 512)
            ev = a["ev_w_in_2"][0]
            if kind == "lat":
                src = ev.rearrange("(k p) n -> p k n", p=P)
                return (KT, 200), [(slice(0, P), slice(0, KT), slice(0, 128), src[:, :, 1816:1944]),
                                   (slice(0, P), slice(0, KT), slice(128, 200), src[:, :, 2456:2528])]
            ate = {"iq": (1944, 512), "dq": (1304, 512), "cs": (512, 512), "wg": (1024, 280)}
            if kind == "nq":
                return paired_columns(ev, 0)
            if kind in ate:
                return plain(ev, *ate[kind])
            if kind == "w1":
                w = (a["nsa_w1_k_2"], a["nsa_w1_v_2"])[name[1]][0]
                return (16, 256), [(slice(0, P), slice(0, 16), slice(0, 256), w.rearrange("(k p) n -> p k n", p=P))]
            if kind == "mo":
                if name[1] == 0:
                    return split(a["ev_w_out_2"][0], 512 * name[2], 512, 8, 4)
                return plain(a["od_w_out_2"][0], 512 * name[2], 512)
            if kind in ("oq", "ok", "ov"):
                return plain(a["od_w_in_2"][0], 1024 * ("oq", "ok", "ov").index(kind) + 512 * name[1], 512)
            if kind == "m1":
                return plain(a["mlp_w1_2"][name[1]], 512 * name[2], 512)
            if kind == "m2":
                _, i, c, kc = name
                w = a["mlp_w2_2"][i][kc * D:(kc + 1) * D, :]
                return plain(w, 512 * c, 512)
            raise KeyError(name)

        def slot_view(i, shape):
            kt, n = shape
            return ring[:, (i % RING) * CHUNK:(i % RING) * CHUNK + kt * n].rearrange("p (k n) -> p k n", k=kt)

        arrival, reached = {}, [0] * RING
        for i, (name, _) in enumerate(pl.chunks):
            reached[i % RING] += 16 * len(pieces(name)[1])
            arrival[name] = (i, reached[i % RING])

        @block.sync
        def _(sp):
            for i, (name, _) in enumerate(pl.chunks):
                if i >= RING:
                    last = pl.chunks[i - RING][1]
                    if isinstance(last, int):
                        sp.wait_ge(m2_used, last)
                    else:
                        sp.wait_ge(psum_full, u[last].full)
                shape, loads = pieces(name)
                v = slot_view(i, shape)
                for ps, ks, ns, src in loads:
                    dst = v[ps, ks, ns] if ns else v[:, ps].rearrange("p (t b d) -> p t b d", b=2, d=HD)[:, :, ks]
                    sp.dma_start(dst, src).then_inc(landed[i % RING], 16)
            for tt in range(NT):
                taken(sp, ("y", tt, 0))
                taken(sp, ("y", tt, 1))
                sp.dma_start(out[0, tt * P:(tt + 1) * P, :], hreg[:, tt * D:(tt + 1) * D]).then_inc(y_out, 16)
            sp.wait_ge(y_out, 16 * NT)

        @block.tensor
        def _(pe):
            made = [0]

            def begin(key):
                unit = u[key]
                assert unit.index == made[0], (key, unit.index, made[0])
                made[0] += 1
                if unit.index >= BANKS:
                    before = pl.order[unit.index - BANKS]
                    pe.wait_ge(drained_by[before.who], before.drained)
                return psum[:, unit.bank, :]

            def weights(name):
                i, n = arrival[name]
                pe.wait_ge(landed[i % RING], n)
                return slot_view(i, pieces(name)[0])

            def dense(key, w, c0, rhs, m=P, kt=KT):
                o = begin(key)
                for k in range(kt):
                    mm = nc.tensor.matmul(o[0:m, :], w[:, k, c0:c0 + m], rhs(k), start=k == 0, stop=k == kt - 1)
                mm.then_inc(psum_full, 1)

            def dense_tokens(key, w, c0, n, lhs):
                o = begin(key)
                for tt in range(NT):
                    for k in range(KT):
                        mm = nc.tensor.matmul(o[:, tt * n:(tt + 1) * n], lhs(k)[:, tt * P:(tt + 1) * P],
                                              w[:, k, c0:c0 + n], start=k == 0, stop=k == KT - 1)
                mm.then_inc(psum_full, 1)

            def ada(n):
                w = weights(("ada", n))
                o = begin(("ada", n))
                for t in range(4):
                    for k in range(KT):
                        mm = nc.tensor.matmul(o[:, t:t + 1], w[:, k, t * P:(t + 1) * P], cact[:, k:k + 1],
                                              start=k == 0, stop=k == KT - 1)
                mm.then_inc(psum_full, 1)

            def wait_x(i, first=None):
                for k in range(KT):
                    if i == 0:
                        taken(pe, ("xT", k))
                    else:
                        pe.wait_ge(x_ready, 8 * (i - 1) + k + 1)

            def scores(j):
                def emit(o, c, lhs, rhs, n):
                    return nc.tensor.matmul(o[:, c:c + n], lhs, rhs, start=True, stop=True)

                hf = slice((j.h >= 4) * HD, (j.h >= 4) * HD + HD)
                t = j.h % 4
                if j.kind == "swa":
                    q, k = A(b1_q + t * S)[hf, :], A(b1_k)[hf, :]
                    for i in range(2):
                        o = begin(("S", j.J, i))
                        c = 0
                        for qb in (2 * i, 2 * i + 1):
                            k0 = max(0, qb - 1) * P
                            n = (qb + 1) * P - k0
                            mm = emit(o, c, q[:, qb * P:(qb + 1) * P], k[:, k0:k0 + n], n)
                            c += n
                        mm.then_inc(psum_full, 1)
                elif j.kind == "cmp":
                    o = begin(("S", j.J, 0))
                    q = A(e_q + t * S)[hf, :]
                    for qb in range(4):
                        mm = emit(o, qb * NCMP, q[:, qb * P:(qb + 1) * P], kcT[hf, :], NCMP)
                    mm.then_inc(psum_full, 1)
                else:
                    if j.kind in ("sel", "win"):
                        q = A(e_q + t * S)[hf, :]
                        k = A(e_ks if j.kind == "sel" else e_kw)[hf, :]
                    elif j.kind == "dsa":
                        q, k = A(e_ql + j.h * S), A(e_ckvT)
                    else:
                        q, k = A(o_q + j.h * S)[j.m * HD:(j.m + 1) * HD, :], A(o_k + j.h * S)[j.m * HD:(j.m + 1) * HD, :]
                    for i, qbs in enumerate(((0, 2), (1,), (3,))):
                        o = begin(("S", j.J, i))
                        c = 0
                        for qb in qbs:
                            n = (qb + 1) * P
                            mm = emit(o, c, q[:, qb * P:(qb + 1) * P], k[:, 0:n], n)
                            c += n
                        mm.then_inc(psum_full, 1)

            def transposes(j):
                if not j.has_pt:
                    return
                pe.wait_ge(s_ready, j.s)
                z = zbuf(j)
                if j.kind == "swa":
                    plan = [[(768 * 0 + (0 if qb == 0 else 256 * qb), qb * P) for qb in range(4)],
                            [(256 * qb - 128, (qb - 1) * P) for qb in range(1, 4)]]
                elif j.kind == "cmp":
                    plan = [[(qb * NCMP, qb * P) for qb in range(4)]]
                else:
                    plan = [[(ZOFF[qb], qb * P) for qb in range(4)],
                            [(ZOFF[qb] + P, (qb - 1) * P) for qb in range(1, 4)],
                            [(ZOFF[2] + 2 * P, 0), (ZOFF[3] + 2 * P, P), (ZOFF[3] + 3 * P, 2 * P)]]
                for i, moves in enumerate(plan):
                    o = begin(("T", j.J, i))
                    for src, dst in moves:
                        n = NCMP if j.kind == "cmp" else P
                        mm = nc.tensor.transpose(o[0:n, dst:dst + P], z[:, src:src + n], ident[:, :])
                    mm.then_inc(psum_full, 1)

            def values(j):
                if not j.has_pt:
                    return
                if j.new_o and j.o >= 2:
                    pe.wait_ge(o_drained, j.o - 1)
                for i in range(j.ptn):
                    taken(pe, ("T", j.J, i))
                pt = ptbuf(j)
                bank = psum[:, 6 + j.o % 2, :]
                hf = slice((j.h >= 4) * HD, (j.h >= 4) * HD + HD)
                if j.kind == "swa":
                    v = A(b1_v).rearrange("p (b f) -> p b f", b=4)
                    for qb in range(4):
                        mm = nc.tensor.matmul(bank[hf, qb * P:(qb + 1) * P], v[:, qb, hf], pt[:, qb * P:(qb + 1) * P],
                                              start=True, stop=qb == 0)
                        if qb:
                            mm = nc.tensor.matmul(bank[hf, qb * P:(qb + 1) * P], v[:, qb - 1, hf],
                                                  pt[:, 512 + (qb - 1) * P:512 + qb * P], start=False, stop=True)
                elif j.kind == "cmp":
                    mm = nc.tensor.matmul(bank[hf, :], vct[0:NCMP, hf], pt[0:NCMP, 0:512], start=True, stop=False,
                                          skip_group_check=True)
                else:
                    for kb in range(4):
                        n = (4 - kb) * P
                        if j.kind in ("sel", "win"):
                            v = A(e_vs if j.kind == "sel" else e_vw).rearrange("p (b f) -> p b f", b=4)[:, kb, hf]
                            o = bank[hf, kb * P:512]
                            start, stop = False, j.kind == "win" and kb == 3
                        elif j.kind == "dsa":
                            v = A(e_ckv).rearrange("p (b f) -> p b f", b=4)[:, kb, :]
                            o, start, stop = bank[:, kb * P:512], kb == 0, kb == 3
                        else:
                            v = arena[:, o_v + kb * D + j.h * P:o_v + kb * D + (j.h + 1) * P]
                            o, start, stop = bank[:, kb * P:512], kb == 0, kb == 3
                        mm = nc.tensor.matmul(o, v, pt[:, KOFF[kb]:KOFF[kb] + n], start=start, stop=stop,
                                              skip_group_check=True)
                mm.then_inc(pv_done, 1)

            def after(j):
                if j.kind == "dsa":
                    pe.wait_ge(o_drained, j.o + 1)
                    pe.wait_ge(uv_in, 16)
                    o = begin(("uv", j.h))
                    hf = (j.h % 2) * HD
                    nc.tensor.matmul(o[hf:hf + HD, :], w_uv[:, j.h * HD:(j.h + 1) * HD], A(e_olat + (j.h % 2) * S),
                                     start=True, stop=True).then_inc(psum_full, 1)
                if j.kind == "diff" and j.m:
                    pe.wait_ge(sq_ready, j.h + 1)
                    o = begin(("ms", j.h))
                    nc.tensor.matmul(o, head_w[:, :], A(o_sq + (j.h % 2) * S), start=True, stop=True)\
                        .then_inc(psum_full, 1)

            def attention(jobs):
                scores(jobs[0])
                scores(jobs[1])
                for s in range(len(jobs) + 2):
                    if s + 2 < len(jobs):
                        scores(jobs[s + 2])
                    if s < len(jobs):
                        transposes(jobs[s])
                    if 0 <= s - 1 < len(jobs):
                        values(jobs[s - 1])
                    if 0 <= s - 2 < len(jobs):
                        after(jobs[s - 2])

            def mean(n, key, tiles):
                for t in tiles:
                    taken(pe, key + (t,))
                    mm = nc.tensor.matmul(psum[:, 6, :], mean_w[:, :], X(t), start=t == 0, stop=t == KT - 1,
                                          skip_group_check=True)
                if tiles[-1] == KT - 1:
                    mm.then_inc(stat_full, 1)

            def variance(n):
                for t in range(KT):
                    pe.wait_ge(ln_squared, 8 * n + t + 1)
                    mm = nc.tensor.matmul(psum[:, 7, :], mean_w[:, :], H(t), start=t == 0, stop=t == KT - 1)
                mm.then_inc(stat_full, 1)

            pe.wait_ge(memsets, 4)
            pe.wait_ge(const_in, 64)
            pe.wait_ge(vec_in, 16 * N_VEC)
            for i, n in enumerate((N_A, N_B, N_C)):
                o = begin(("vec", i))
                nc.tensor.transpose(o[:, 0:n], mix[0:n, i * P:(i + 1) * P], ident[0:n, 0:n]).then_inc(psum_full, 1)
            pe.wait_ge(tab_in, 32)
            tab, hot = mix[0:BUCKETS + 1, 384:400], mix[0:BUCKETS + 1, 512:512 + TW]
            for i, (c, n) in enumerate(((0, 512), (512, 128))):
                o = begin(("bias", i))
                nc.tensor.matmul(o[0:16, 0:n], tab, hot[:, c:c + n], start=True, stop=True).then_inc(psum_full, 1)
            pe.wait_ge(x_in, 64)
            for k in range(KT):
                o = begin(("xT", k))
                for tt in range(NT):
                    mm = nc.tensor.transpose(o[:, tt * P:(tt + 1) * P],
                                             hreg[:, tt * D + k * P:tt * D + (k + 1) * P], ident[:, :])
                mm.then_inc(psum_full, 1)

            for l in range(DEPTH):
                ad = 12 * l
                pe.wait_ge(ws_masked, l + 1)
                o = begin(("wT", l))
                for g in range(4):
                    mm = nc.tensor.transpose(o[:, g * P:(g + 1) * P], ws_raw[:, g * P:(g + 1) * P], ident[:, :])
                mm.then_inc(psum_full, 1)
                wait_x(l)
                w = weights(("vg", l))
                for tt in range(NT):
                    o = begin(("vg", l, tt))
                    for k in range(KT):
                        mm = nc.tensor.matmul(o, X(k)[:, tt * P:(tt + 1) * P], w[:, k, :], start=k == 0, stop=k == KT - 1)
                    mm.then_inc(psum_full, 1)
                if l == 0:
                    pe.wait_ge(c_ready, 1)
                ada(ad)
                for i, name in enumerate(("u", "za", "zg")):
                    w = weights((name, l))
                    for t in range(4):
                        dense((name, l, t), w, t * P, X)
                    ada(ad + 1 + i)
                w = weights(("kv", l))
                dense(("k", l), w, 0, X)
                dense_tokens(("v", l), w, P, P, X)
                ada(ad + 4)
                w = weights(("q", l))
                for t in range(4):
                    dense(("q", l, t), w, t * P, X)
                ada(ad + 5)
                pe.wait_ge(vn_ready, 4 * l + 4)
                taken(pe, ("wT", l))
                for g in range(4):
                    o = begin(("sp", l, g))
                    for c in range(NT):
                        vn = A(b1_vn + c * S)
                        mm = nc.tensor.matmul(o[:, c * P:(c + 1) * P], vn[:, g * P:(g + 1) * P],
                                              ws_t[:, g * P:(g + 1) * P], start=True, stop=True)
                    mm.then_inc(psum_full, 1)
                jobs = pl.swa[l]
                taken(pe, ("k", l))
                taken(pe, ("v", l))
                taken(pe, ("q", l, 3))
                scores(jobs[0])
                scores(jobs[1])
                for s in range(9):
                    if s + 2 < 8:
                        scores(jobs[s + 2])
                    if s < 8:
                        w = weights(("g", l, s // 2))
                        for t in range(2 * s, 2 * s + 2):
                            dense(("g", l, t), w, (t % 4) * P, X)
                        if s % 2 == 1:
                            ada(ad + 6 + s // 2)
                        transposes(jobs[s])
                    if s >= 1:
                        values(jobs[s - 1])
                pe.wait_ge(yg_ready, 4 * l + 4)
                pe.wait_ge(o_drained, 4 * l + 4)
                wa, wg = weights(("ba", l)), weights(("bg", l))
                for t in range(KT):
                    dense(("ba", l, t), wa, t * P, M, kt=4)
                    dense(("bg", l, t), wg, t * P, lambda k: M(4 + k), kt=4)
                ada(ad + 10)
                ada(ad + 11)
                pe.wait_ge(merged, 8 * l + 8)
                for c in range(2):
                    w = weights(("out", l, c))
                    for t in range(4):
                        dense(("out", l, 4 * c + t), w, t * P, lambda k: ga(k))
                    if c:
                        mean(l, ("out", l), range(KT))
                variance(l)

            def wait_h(i):
                for k in range(KT):
                    pe.wait_ge(h_ready, 8 * i + k + 1)

            def mixer_out_pe(i):
                for c in range(2):
                    w = weights(("mo", i, c))
                    for t in range(4):
                        dense(("mo", i, 4 * c + t), w, t * P, M)
                mean(2 + 2 * i, ("mo", i), range(KT))
                variance(2 + 2 * i)

            def mlp_pe(i):
                wait_h(2 * i + 1)
                for c in range(8):
                    w = weights(("m1", i, c))
                    for t in range(4):
                        dense(("m1", i, 4 * c + t), w, t * P, H)
                for c in range(2):
                    banks = None
                    for kc in range(4):
                        w = weights(("m2", i, c, kc))
                        if banks is None:
                            banks = [begin(("m2", i, 4 * c + t)) for t in range(4)]
                        for t in range(4):
                            for k in range(KT):
                                if c == 0 and t == 0:
                                    pe.wait_ge(hidden_ready, 32 * i + 8 * kc + k + 1)
                                mm = nc.tensor.matmul(banks[t], w[:, k, t * P:(t + 1) * P], A((8 * kc + k) * S),
                                                      start=kc == 0 and k == 0, stop=kc == 3 and k == KT - 1)
                            if kc == 3:
                                mm.then_inc(psum_full, 1)
                        if kc < 3:
                            mm.then_inc(m2_used, 1)
                mean(3 + 2 * i, ("m2", i), range(KT))
                variance(3 + 2 * i)

            pe.wait_ge(e_in, 16 * N_E)
            pe.wait_ge(memsets, 5)
            for i in range(2):
                o = begin(f"biasc{i}")
                for b in range(2):
                    for n in range(NCMP):
                        d0 = (2 * i + b) * P - 16 * n - 31 + 511
                        c = (b * NCMP + n) * 8
                        mm = nc.tensor.matmul(o[:, c:c + 8], hot_full[0:33, d0:d0 + P], tab_full[0:33, 0:8],
                                              start=True, stop=True)
                mm.then_inc(psum_full, 1)
            o = begin("ukT")
            for t in range(4):
                mm = nc.tensor.transpose(o[:, t * P:(t + 1) * P], uk_raw[:, t * P:(t + 1) * P], ident[:, :])
            mm.then_inc(psum_full, 1)
            wait_h(0)
            w = weights("lat")
            dense_tokens("lat", w, 0, P, H)
            o = begin("ik")
            for hf in range(2):
                for k in range(KT):
                    mm = nc.tensor.matmul(o[hf * HD:(hf + 1) * HD, :], w[:, k, 128:192], H(k),
                                          start=k == 0, stop=k == KT - 1)
            mm.then_inc(psum_full, 1)
            dense_tokens("iw", w, 192, 8, H)
            w = weights("iq")
            for t in range(4):
                dense(("iq", t), w, t * P, H)
            pe.wait_ge(lat_done, 4)
            o = begin("ckvT")
            for tt in range(NT):
                mm = nc.tensor.transpose(o[:, tt * P:(tt + 1) * P], A(e_ckv + tt * P, P), ident[:, :])
            mm.then_inc(psum_full, 1)
            taken(pe, ("iq", 3))
            for qb in range(1, 4):
                for j in range(8):
                    hf = slice((j % 2) * HD, (j % 2) * HD + HD)
                    n = (qb + 1) * P
                    o = begin(("I", qb, j))
                    nc.tensor.matmul(o[:, 0:n], A(e_iq + (j // 2) * S)[hf, qb * P:(qb + 1) * P], A(e_ik)[hf, 0:n],
                                     start=True, stop=True).then_inc(psum_full, 1)
            w = weights("dq")
            for t in range(4):
                dense(("dq", t), w, t * P, H)
            w = weights("cs")
            dense("kc", w, 0, H)
            dense("vc", w, 128, H)
            dense("ks", w, 256, H)
            dense_tokens("vs", w, 384, P, H)
            w = weights("wg")
            dense("kw", w, 0, H)
            dense_tokens("vw", w, 128, P, H)
            dense_tokens("gate", w, 256, 24, H)
            w = weights("nq")
            for t in range(4):
                dense(("nq", t), w, t * P, H)
            taken(pe, "ukT")
            taken(pe, ("dq", 3))
            for h in range(8):
                hf = slice((h % 2) * HD, (h % 2) * HD + HD)
                o = begin(("ql", h))
                nc.tensor.matmul(o, ukT[hf, (h // 2) * P:(h // 2 + 1) * P], A(e_dq + (h // 2) * S)[hf, :],
                                 start=True, stop=True).then_inc(psum_full, 1)
            pe.wait_ge(rp_ready, 8)
            for kind in range(2):
                w = weights(("w1", kind))
                for half in range(2):
                    o = begin(("hid", kind, half))
                    for jj in range(16):
                        mm = nc.tensor.matmul(o[:, 0:62], w[:, jj, half * P:(half + 1) * P],
                                              side[:, rp_at + kind * 992 + jj * 62:rp_at + kind * 992 + jj * 62 + 62],
                                              start=jj == 0, stop=jj == 15)
                    mm.then_inc(psum_full, 1)
            taken(pe, ("hid", 1, 1))
            o = begin("kcT")
            for g in range(2):
                for half in range(2):
                    mm = nc.tensor.matmul(o[g * HD:(g + 1) * HD, 0:NCMP], w2kv[:, half * HD:(half + 1) * HD],
                                          hid[:, half * 62 + g * NCMP:half * 62 + (g + 1) * NCMP],
                                          start=half == 0, stop=half == 1)
            mm.then_inc(psum_full, 1)
            o = begin("vct")
            for g in range(2):
                for half in range(2):
                    mm = nc.tensor.matmul(o[0:NCMP, g * HD:(g + 1) * HD],
                                          hid[:, 124 + half * 62 + g * NCMP:124 + half * 62 + (g + 1) * NCMP],
                                          w2kv[:, 128 + half * HD:128 + (half + 1) * HD],
                                          start=half == 0, stop=half == 1)
            mm.then_inc(psum_full, 1)
            taken(pe, "vct")
            taken(pe, "ckvT")
            attention(pl.even)
            taken(pe, ("uv", 7))
            mixer_out_pe(0)
            mlp_pe(0)

            wait_h(2)
            for name in ("oq", "ok"):
                for c in range(2):
                    w = weights((name, c))
                    for t in range(4):
                        dense((name, 4 * c + t), w, t * P, H)
            for c in range(2):
                w = weights(("ov", c))
                for tt in range(NT):
                    o = begin(("ov", 4 * c + tt))
                    for k in range(KT):
                        mm = nc.tensor.matmul(o, H(k)[:, tt * P:(tt + 1) * P], w[:, k, :], start=k == 0, stop=k == KT - 1)
                    mm.then_inc(psum_full, 1)
            for i in (6, 7):
                taken(pe, ("ov", i))
            attention(pl.odd)
            pe.wait_ge(o_normed, 8)
            mixer_out_pe(1)
            mlp_pe(1)
            for k in range(KT):
                pe.wait_ge(x_ready, 8 * 5 + k + 1)
            for tt in range(NT):
                for c in range(2):
                    o = begin(("y", tt, c))
                    for k in range(4):
                        mm = nc.tensor.transpose(o[:, k * P:(k + 1) * P], X(4 * c + k)[:, tt * P:(tt + 1) * P], ident[:, :])
                    mm.then_inc(psum_full, 1)
            assert made[0] == len(pl.order)

        def load_rows(eng, l):
            for dst, src in ((bv_row, bcast(a["b_in"], P, l * W1 + 640)),
                             (bvg_row, bcast(a["b_in"], 512, l * W1 + 1792)),
                             (lng_row, bcast(a["gmlp_ln_g"], 512, l * 512)),
                             (lnb_row, bcast(a["gmlp_ln_b"], 512, l * 512)),
                             (bs_row, bcast(a["b_spatial"], 512, l * 512))):
                eng.dma_start(dst, src).then_inc(rows_in, 16)
            eng.dma_start(ws_raw.rearrange("p (g s) -> p g s", g=4), a["w_spatial"][l].rearrange("g t s -> t g s"))\
                .then_inc(rows_in, 16)

        @block.scalar
        def _(act):

            def sqrt(out_, in_, bias):
                nc.scalar.activation(out_, in_, ACT.Sqrt, bias=bias).then_inc(std_ready, 1)

            def drain(key, dst, func=ACT.Copy, bias=0.0, scale=1.0, m=slice(0, P), n=slice(0, S)):
                o = full(act, key)
                nc.scalar.activation(dst, o[m, n], func, bias=bias, scale=scale).then_inc(act_drained, 1)

            act.wait_ge(memsets, 3)
            for dst, src in ((ident[:, :], a["ident"]), (tril[:, :], a["tril"]), (alibi, a["alibi"]),
                             (sinks[:, :], bcast(a["attn_sinks"], 2 * HEADS))):
                act.dma_start(dst, src).then_inc(const_in, 16)
            for tt in range(NT):
                act.dma_start(hreg[:, tt * D:(tt + 1) * D], a["x"][0, tt * P:(tt + 1) * P, :]).then_inc(x_in, 16)
            load_rows(act, 0)

            def rows(ap, off, n):
                return bass.AP(tensor=ap.tensor, offset=ap.offset + off, ap=[[P, n], [1, P]])

            def paired_rows(ap, off):
                return bass.AP(tensor=ap.tensor, offset=ap.offset + off, ap=[[HD, 4], [256, 2], [1, HD]])

            vecs = []
            for l in range(DEPTH):
                r, b = 62 * l, l * W1
                for row, off in ((r, b), (r + 6, b + 768)):
                    vecs.append((mix[row:row + 4, 0:P].rearrange("p (b d) -> p b d", b=2), paired_rows(a["b_in"], off)))
                vecs.append((mix[r + 4:r + 6, 0:P], rows(a["b_in"], b + 512, 2)))
                vecs.append((mix[r + 10:r + 38, 0:P], rows(a["b_in"], b + 1280, 28)))
                for i, name in enumerate(("b_out", "ln_g", "ln_b")):
                    vecs.append((mix[r + 38 + 8 * i:r + 46 + 8 * i, 0:P], rows(a[name], l * D, 8)))
            vecs.append((mix[0:96, P:2 * P], rows(a["ada_b_2"], 0, 96)))
            vecs.append((mix[96:128, P:2 * P], rows(a["ln_g_2"], 0, 32)))
            vecs.append((mix[0:32, 2 * P:3 * P], rows(a["ln_b_2"], 0, 32)))
            vecs.append((mix[32:33, 2 * P:3 * P], rows(a["diff_subln_2"], 0, 1)))
            vecs.append((mix[33:41, 2 * P:3 * P], rows(a["c_2"], 0, 8)))
            assert len(vecs) == N_VEC
            for dst, src in vecs:
                act.dma_start(dst, src).then_inc(vec_in, 16)
            act.dma_start(mix[0:BUCKETS, 384:400], a["rel_bias_2"]).then_inc(tab_in, 16)
            act.dma_start(mix[0:BUCKETS + 1, 512:512 + TW], a["hot_rev"]).then_inc(tab_in, 16)
            bias_sb = mix[0:16, 2048:2048 + TW]
            drain(("bias", 0), bias_sb[:, 0:512], scale=-1.0, m=slice(0, 16))
            drain(("bias", 1), bias_sb[:, 512:TW], scale=-1.0, m=slice(0, 16), n=slice(0, TW - 512))
            act.wait_ge(act_drained, 2)
            act.dma_start(bias_rows, bias_sb.unsqueeze(1).to_broadcast([16, P, TW])).then_inc(bias_out, 16)
            for k in range(0, KT, 2):
                drain(("xT", k), X(k))
            taken(act, ("vec", 2))
            c0 = vec_b(0, "c")
            nc.scalar.activation(cact[:, :], cols[:, c0:c0 + KT], ACT.Silu).then_inc(c_ready, 1)

            def load_table(ti):
                h = tables[ti]
                src = bass.AP(tensor=bias_rows.tensor, offset=bias_rows.offset + h * P * TW + P - 1,
                              ap=[[TW - 1, P], [1, S]])
                act.dma_start(tbuf(ti), src).then_inc(t_in[ti % 3], 16)

            def exps(j):
                z = zbuf(j)
                if j.kind == "cmp":
                    act.wait_ge(m_ready, j.mr)
                    nc.scalar.activation(z[:, 0:4 * NCMP], z[:, 0:4 * NCMP], ACT.Exp, scale=-1.0).then_inc(p_ready, 1)
                    return
                if j.kind == "swa":
                    act.wait_ge(m_ready, j.mr)
                    spans = [(qb, (0, 128, 384, 640)[qb], 256 if qb else 128) for qb in range(4)]
                else:
                    spans = [(qb, ZOFF[qb], (qb + 1) * P) for qb in ORDER]
                for i, (qb, c, n) in enumerate(spans):
                    if j.kind != "swa":
                        act.wait_ge(z_ready, j.z0 + i + 1)
                    nc.scalar.activation(z[:, c:c + n], z[:, c:c + n], ACT.Exp, bias=stat4(negm, j, qb), scale=-1.0,
                                         accum_out=stat4(sums, j, qb)).then_inc(p_ready, 1)
                if j.kind == "swa":
                    h = HEADS * j.l + j.h
                    nc.scalar.activation(stat4(esink, j), stat4(negm, j), ACT.Exp, bias=sinks[:, h:h + 1])\
                        .then_inc(sink_ready, 1)
                if j.kind not in ("swa", "cmp") and j.t_last and j.ti + 3 < len(tables):
                    load_table(j.ti + 3)

            def drain_t(j):
                if not j.has_pt:
                    return
                pt = ptbuf(j)
                if j.pt >= 2:
                    act.wait_ge(pv_done, j.pt - 1)
                if j.kind == "cmp":
                    drain(("T", j.J, 0), pt[0:NCMP, 0:512], m=slice(0, NCMP))
                else:
                    drain(("T", j.J, 0), pt[:, 0:512])
                    if j.kind != "swa":
                        drain(("T", j.J, 2), pt[:, 896:1280], n=slice(0, 384))

            def squares(n):
                for t in range(KT):
                    act.wait_ge(ln_centered, 8 * n + t + 1)
                    nc.scalar.activation(H(t), X(t), ACT.Square).then_inc(ln_squared, 1)

            def affine(n, g, b):
                act.wait_ge(stat_full, 2 * n + 2)
                sqrt(rstd, psum[:, 7, :], eps[:, :])
                for t in range(KT):
                    act.wait_ge(ln_scaled, 8 * n + t + 1)
                    nc.scalar.activation(X(t), X(t), ACT.Identity, bias=cols[:, b + t:b + t + 1],
                                         scale=cols[:, g + t:g + t + 1]).then_inc(x_ready, 1)

            for l in range(DEPTH):
                for tt in range(NT):
                    taken(act, ("vg", l, tt))
                    nc.scalar.activation(A(b1_vn + tt * S), A(b1_vn + tt * S), ACT.Gelu).then_inc(vg_gelu, 1)
                for name, at, func in (("u", b1_u, ACT.Gelu), ("za", b1_za, ACT.Silu), ("zg", b1_zg, ACT.Silu)):
                    if name == "za":
                        act.wait_ge(var_ready, l + 1)
                        sqrt(stats[:, 32:36], stats[:, 32:36], eps[:, :])
                    for t in range(4):
                        c = vec_a(l, name, t)
                        drain((name, l, t), A(at + t * S), func, bias=cols[:, c:c + 1])
                c = vec_a(l, "k")
                drain(("k", l), A(b1_k), ACT.Identity, bias=cols[:, c:c + 1])
                jobs = pl.swa[l]
                exps(jobs[0])
                exps(jobs[1])
                for s in range(8):
                    for t in range(2 * s, 2 * s + 2):
                        c = vec_a(l, "g", t)
                        drain(("g", l, t), ga(t), ACT.Identity, bias=cols[:, c:c + 1])
                    if s + 2 < 8:
                        exps(jobs[s + 2])
                    drain_t(jobs[s])
                act.wait_ge(act_drained, u[("T", jobs[7].J, 0)].drained)
                for i in range(4):
                    for v in (A(b1_ga + 2 * i * S, 2 * S), hreg[:, 2 * i * S:2 * (i + 1) * S]):
                        nc.scalar.activation(v, v, ACT.Sigmoid).then_inc(sig_ready, 1)
                if l + 1 < DEPTH:
                    taken(act, ("sp", l, 3))
                    load_rows(act, l + 1)
                squares(l)
                affine(l, vec_a(l, "ln_g"), vec_a(l, "ln_b"))

            e_loads = [(hot_full[0:33, :], a["hot"]), (tab_full[0:32, :], a["rel_bias_2"]),
                       (uk_raw, a["dsa_w_uk_2"][0].rearrange("r h d -> r (h d)")),
                       (side[:, 7168:7296], a["future"]), (kvnorm, bcast(a["dsa_kv_norm_2"], P))]
            for i, name in enumerate(("nsa_w2_k_2", "nsa_w2_v_2")):
                e_loads.append((w2kv[:, 128 * i:128 * i + 128].rearrange("p (k n) -> p k n", k=2),
                                a[name][0].rearrange("(k p) n -> p k n", p=P)))
            for dst, src in e_loads:
                act.dma_start(dst, src).then_inc(e_in, 16)
            with nc.allow_non_contiguous_dma("positional embeddings of 16 KB"):
                for i, name in enumerate(("nsa_pe_k_2", "nsa_pe_v_2")):
                    src = bass.AP(tensor=a[name].tensor, offset=a[name].offset, ap=[[1, P], [P, 16]])
                    act.dma_start(peT[:, 16 * i:16 * i + 16], src).then_inc(e_in, 16)
            act.wait_ge(bias_out, 16)
            for ti in range(3):
                load_table(ti)
            for i in range(2):
                o = full(act, f"biasc{i}")
                nc.scalar.activation(
                    biasc[:, i * 2 * 248:(i + 1) * 2 * 248].rearrange("p (b h n) -> p b h n", b=2, h=8),
                    o[:, 0:496].rearrange("p (b n h) -> p b h n", b=2, h=8), ACT.Copy, scale=-1.0)\
                    .then_inc(act_drained, 1)
            drain("ik", A(e_ik))
            act.wait_ge(var_ready, DEPTH + 1)
            sqrt(stats[:, 0:4], stats[:, 0:4], eps[:, :])
            for t in range(4):
                drain(("iq", t), A(e_iq + t * S))
            i = 0
            for qb in range(1, 4):
                n = (qb + 1) * P
                for j in range(8):
                    if i >= 2:
                        act.wait_ge(isc_used, i - 1)
                    drain(("I", qb, j), side[:, (i % 2) * S:(i % 2) * S + n], ACT.Relu, n=slice(0, n))
                    i += 1
            for t in range(4):
                drain(("dq", t), A(e_dq + t * S), scale=-HD ** -0.5)
            drain("kc", A(e_kc))
            drain("vc", A(e_vc))
            act.wait_ge(act_drained, u["vc"].drained)
            for kind, at in enumerate((e_kc, e_vc)):
                for g in range(2):
                    dst = tile(mix, 2 * kind + g)
                    src = A(at)[g * HD:(g + 1) * HD, :]
                    act.dma_start(dst[0:HD, :], src).then_inc(r_in, 16)
                    act.dma_start(dst[HD:P, 0:S - 1], src[:, 1:S]).then_inc(r_in, 16)
            for key, at in (("ks", e_ks), ("vs", e_vs), ("kw", e_kw), ("vw", e_vw)):
                drain(key, A(at))
            drain("gate", gates, ACT.Sigmoid, n=slice(0, 96))
            for t in range(4):
                drain(("nq", t), A(e_q + t * S), scale=-HD ** -0.5)
            for h in range(8):
                drain(("ql", h), A(e_ql + h * S))
            act.wait_ge(psum_full, u[("ql", 7)].full)
            act.dma_start(w_uv, a["dsa_w_uv_2"][0].rearrange("r h d -> r (h d)")).then_inc(uv_in, 16)
            for kind in range(2):
                for half in range(2):
                    c = (2 * kind + half) * 62
                    drain(("hid", kind, half), hid[:, c:c + 62], ACT.Gelu_apprx_tanh, n=slice(0, 62))
            drain("kcT", kcT, n=slice(0, NCMP))
            drain("vct", vct[0:NCMP, :], m=slice(0, NCMP), n=slice(0, P))

            def attention(jobs):
                exps(jobs[0])
                exps(jobs[1])
                for s in range(len(jobs) + 2):
                    if s + 2 < len(jobs):
                        exps(jobs[s + 2])
                    if s < len(jobs):
                        drain_t(jobs[s])
                    if 0 <= s - 1 < len(jobs) and jobs[s - 1].kind == "diff" and jobs[s - 1].m:
                        h = jobs[s - 1].h
                        act.wait_ge(o_drained, jobs[s - 1].o + 1)
                        if h >= 2:
                            act.wait_ge(psum_full, u[("ms", h - 2)].full)
                        nc.scalar.activation(A(o_sq + (h % 2) * S), M(h), ACT.Square).then_inc(sq_ready, 1)
                    if 0 <= s - 2 < len(jobs) and jobs[s - 2].kind == "dsa":
                        h = jobs[s - 2].h
                        m = slice((h % 2) * HD, (h % 2) * HD + HD)
                        drain(("uv", h), M(4 + h // 2)[m, :], m=m)

            attention(pl.even)

            def norms(n):
                squares(n)
                affine(n, vec_b(n - 2, "ln_g"), vec_b(n - 2, "ln_b"))

            def relus(i):
                for t in range(32):
                    drain(("m1", i, t), A(t * S), ACT.Relu)

            norms(2)
            relus(0)
            norms(3)
            for i, at in ((0, o_q), (1, o_k), (2, o_v)):
                for t in range(1, 8, 2):
                    name = ("oq", "ok", "ov")[i]
                    if name == "ov":
                        c, tt = divmod(t, 4)
                        drain((name, t), arena[:, at + tt * D + c * S:at + tt * D + (c + 1) * S])
                    else:
                        drain((name, t), A(at + t * S), scale=-HD ** -0.5 if i == 0 else 1.0)
            act.wait_ge(lam_dots, 2)
            nc.scalar.activation(lamc[:, 2:4], lamc[:, 0:2], ACT.Exp).then_inc(lam_ready, 1)
            attention(pl.odd)
            for h in range(HEADS):
                taken(act, ("ms", h))
                sqrt(H(h), H(h), eps[:, :])
            norms(4)
            relus(1)
            norms(5)
            for tt in range(NT):
                drain(("y", tt, 1), hreg[:, tt * D + S:(tt + 1) * D])

        @block.vector
        def _(dve):
            own = Steps(dve, dve_own)
            v = nc.vector
            stds = [0]

            def drain(key, dst, m=slice(0, P), n=slice(0, S)):
                o = full(dve, key)
                v.tensor_copy(dst, o[m, n]).then_inc(dve_drained, 1)

            def ada(n):
                o = full(dve, ("ada", n))
                b = N_A + 4 * n
                v.tensor_tensor(adac[:, 4 * n:4 * n + 4], o[:, 0:4], cols[:, b:b + 4], ALU.add).then_inc(dve_drained, 1)

            def biased(j):
                z = zbuf(j)
                if j.J >= 4:
                    before = pl.jobs[j.J - 4]
                    if not before.has_pt:
                        before = pl.jobs[j.J - 3]
                    dve.wait_ge(psum_full, u[("T", before.J, before.ptn - 1)].full)
                if j.kind == "cmp":
                    o = full(dve, ("S", j.J, 0))[:, 0:4 * NCMP].rearrange("p (b n) -> p b n", b=4)
                    zz = z[:, 0:4 * NCMP].rearrange("p (b n) -> p b n", b=4)
                    bias = biasc.rearrange("p (b h n) -> p b h n", b=4, h=8)[:, :, j.h, :]
                    v.tensor_tensor(zz, o, bias, ALU.add).then_inc(z_ready, 1)
                    dve.wait_ge(z_ready, j.z)
                    own.step(v.tensor_reduce(stat4(negm, j), zz, AX_X, ALU.min))
                    own.settle()
                    own.step(v.tensor_scalar(stat4(negm, j), stat4(negm, j), 0.1 * MASKED, None, ALU.min))
                    own.settle()
                    v.tensor_tensor(zz, zz, stat4(negm, j).unsqueeze(2).to_broadcast([P, 4, NCMP]),
                                    ALU.subtract).then_inc(m_ready, 1)
                    return
                if j.kind == "swa":
                    for i in range(2):
                        o = full(dve, ("S", j.J, i))
                        c = 0
                        for qb in (2 * i, 2 * i + 1):
                            n = 256 if qb else 128
                            at = (0, 128, 384, 640)[qb]
                            v.tensor_tensor_reduce(
                                out=z[:, at:at + n], in0=o[:, c:c + n],
                                in1=alibi[:, j.h * 256 + 256 - n:(j.h + 1) * 256], scale=1.0, scalar=HUGE,
                                op0=ALU.add, op1=ALU.min, accum_out=stat4(negm, j, qb)).then_inc(z_ready, 1)
                            c += n
                    dve.wait_ge(z_ready, j.z)
                    h = HEADS * j.l + j.h
                    v.tensor_scalar(stat4(negm, j), stat4(negm, j), nsinks[:, h:h + 1], None, ALU.min)\
                        .then_inc(m_ready, 1)
                    return
                dve.wait_ge(t_in[j.ti % 3], 16 * (j.ti // 3 + 1))
                table = tbuf(j.ti)
                for i, qbs in enumerate(((0, 2), (1,), (3,))):
                    o = full(dve, ("S", j.J, i))
                    c = 0
                    for qb in qbs:
                        n, at = (qb + 1) * P, ZOFF[qb]
                        zz, bias = z[:, at:at + n], table[:, S - n:S]
                        first, second = o[:, c:c + n], bias
                        if j.kind == "dsa" and qb:
                            own.step(v.tensor_tensor(zz, o[:, c:c + n], bias, ALU.add))
                            own.settle()
                            first, second = zz, hreg[:, selm_at[qb]:selm_at[qb] + n]
                        v.tensor_tensor_reduce(out=zz, in0=first, in1=second, scale=1.0, scalar=HUGE,
                                               op0=ALU.add, op1=ALU.min, accum_out=stat4(negm, j, qb))\
                            .then_inc(z_ready, 1)
                        c += n

            def row_factors(j):
                dve.wait_ge(p_ready, j.p)
                den, r = stat4(sums, j), stat4(recips, j)
                if j.kind == "swa":
                    dve.wait_ge(sink_ready, HEADS * j.l + pl.swa[j.l].index(j) + 1)
                    own.step(v.tensor_tensor(den, den, stat4(esink, j), ALU.add))
                    own.settle()
                    v.reciprocal(r, den).then_inc(r_ready, 1)
                    return
                if j.kind == "cmp":
                    zz = zbuf(j)[:, 0:4 * NCMP].rearrange("p (b n) -> p b n", b=4)
                    own.step(v.tensor_reduce(den, zz, AX_X, ALU.add))
                    own.settle()
                own.step(v.tensor_scalar(den, den, 1e-30, None, ALU.max))
                own.settle()
                if j.kind == "dsa" or (j.kind == "diff" and j.m == 0):
                    v.reciprocal(r, den).then_inc(r_ready, 1)
                    return
                own.step(v.reciprocal(r, den))
                own.settle()
                if j.kind == "diff":
                    v.tensor_scalar(r, r, small[:, 6:7], None, ALU.mult).then_inc(r_ready, 1)
                else:
                    i = ("cmp", "sel", "win").index(j.kind)
                    g = gates.rearrange("p (b f) -> p b f", b=4)[:, :, 3 * j.h + i]
                    v.tensor_tensor(r, r, g, ALU.mult).then_inc(r_ready, 1)

            def drain_t(j):
                if not j.has_pt or j.kind == "cmp":
                    return
                if j.pt >= 2:
                    dve.wait_ge(pv_done, j.pt - 1)
                drain(("T", j.J, 1), ptbuf(j)[:, 512:896], n=slice(0, 384))

            def outputs(j):
                if not (j.has_pt and j.last_o):
                    return
                dve.wait_ge(pv_done, j.pv)
                bank = psum[:, 6 + j.o % 2, :]
                if j.kind == "swa":
                    t = j.h % 4
                    v.tensor_tensor(M(t), bank, A(b1_za + t * S), ALU.mult).then_inc(o_drained, 1)
                elif j.kind == "win":
                    v.tensor_copy(M(j.h % 4), bank).then_inc(o_drained, 1)
                elif j.kind == "dsa":
                    if j.h >= 2:
                        dve.wait_ge(psum_full, u[("uv", j.h - 2)].full)
                    v.tensor_copy(A(e_olat + (j.h % 2) * S), bank).then_inc(o_drained, 1)
                else:
                    v.tensor_copy(M(j.h), bank).then_inc(o_drained, 1)

            def head_norm(h):
                stds[0] += 1
                dve.wait_ge(std_ready, stds[0])
                own.step(v.reciprocal(H(h), H(h)))
                own.settle()
                v.scalar_tensor_tensor(M(h), M(h), small[:, 7:8], H(h), ALU.mult, ALU.mult).then_inc(o_normed, 1)

            def attention(jobs):
                biased(jobs[0])
                biased(jobs[1])
                row_factors(jobs[0])
                for s in range(len(jobs) + 2):
                    if s + 2 < len(jobs):
                        biased(jobs[s + 2])
                    if s + 1 < len(jobs):
                        row_factors(jobs[s + 1])
                    if s < len(jobs):
                        drain_t(jobs[s])
                    if 0 <= s - 1 < len(jobs):
                        outputs(jobs[s - 1])
                    if 0 <= s - 2 < len(jobs) and jobs[s - 2].kind == "diff" and jobs[s - 2].m:
                        drain(("ms", jobs[s - 2].h), H(jobs[s - 2].h))

            def layer_norm(n):
                dve.wait_ge(stat_full, 2 * n + 1)
                for t in range(KT):
                    v.tensor_tensor(X(t), X(t), psum[:, 6, :], ALU.subtract).then_inc(ln_centered, 1)
                stds[0] += 1
                dve.wait_ge(std_ready, stds[0])
                own.step(v.reciprocal(rstd, rstd))
                own.settle()
                for t in range(KT):
                    dve.wait_ge(ln_centered, 8 * n + t + 1)
                    v.tensor_tensor(X(t), X(t), rstd, ALU.mult).then_inc(ln_scaled, 1)

            for i, (c, n) in enumerate(((0, N_A), (N_A, N_B), (N_A + N_B, N_C))):
                drain(("vec", i), cols[:, c:c + n], n=slice(0, n))
            dve.wait_ge(const_in, 64)
            v.tensor_scalar(nsinks[:, :], sinks[:, :], -1.0, None, ALU.mult).then_inc(nsink_ready, 1)
            for k in range(1, KT, 2):
                drain(("xT", k), X(k))
            dve.wait_ge(nsink_ready, 1)

            for l in range(DEPTH):
                ad = 12 * l
                dve.wait_ge(rows_in, 96 * (l + 1))
                if l:
                    dve.wait_ge(psum_full, u[("wT", l - 1)].full)
                ws3 = ws_raw.rearrange("p (g s) -> p g s", g=4)
                v.tensor_tensor(ws3, ws3, tril[:, :].unsqueeze(1).to_broadcast([P, 4, P]), ALU.mult)\
                    .then_inc(ws_masked, 1)
                drain(("wT", l), ws_t)
                for tt in range(NT):
                    o = full(dve, ("vg", l, tt))
                    v.tensor_tensor(A(b1_vn + tt * S), o, bvg_row, ALU.add).then_inc(dve_drained, 1)
                ada(ad)
                bn = stats[:, 0:24].rearrange("p (t s) -> p t s", t=4)
                mv = stats[:, 24:32].rearrange("p (t s) -> p t s", t=4)
                rs = stats[:, 32:36]
                for tt in range(NT):
                    dve.wait_ge(vg_gelu, 4 * l + tt + 1)
                    own.step(v.bn_stats(bn[:, tt, :], A(b1_vn + tt * S)))
                    own.settle()
                    own.step(v.bn_aggr(mv[:, tt, :], bn[:, tt, :]))
                own.settle()
                v.tensor_copy(rs, mv[:, :, 1]).then_inc(var_ready, 1)
                stds[0] += 1
                dve.wait_ge(std_ready, stds[0])
                own.step(v.reciprocal(rs, rs))
                own.settle()
                for tt in range(NT):
                    v.tensor_scalar(A(b1_vn + tt * S), A(b1_vn + tt * S), mv[:, tt, 0:1], rs[:, tt:tt + 1],
                                    ALU.subtract, ALU.mult).then_inc(vn_norm, 1)
                for i in range(1, 4):
                    ada(ad + i)
                o = full(dve, ("v", l))
                v.tensor_tensor(A(b1_v).rearrange("p (b f) -> p b f", b=4), o.rearrange("p (b f) -> p b f", b=4),
                                bv_row.unsqueeze(1).to_broadcast([P, 4, P]), ALU.add).then_inc(dve_drained, 1)
                ada(ad + 4)
                for t in range(4):
                    c = vec_a(l, "q", t)
                    o = full(dve, ("q", l, t))
                    v.tensor_scalar(A(b1_q + t * S), o, cols[:, c:c + 1], -HD ** -0.5, ALU.add, ALU.mult)\
                        .then_inc(dve_drained, 1)
                ada(ad + 5)
                dve.wait_ge(bias_out, 16)
                for g in range(4):
                    o = full(dve, ("sp", l, g))
                    tmp = A(b1_tmp + (g % 2) * S)
                    bs = bs_row[:, g * P:(g + 1) * P].unsqueeze(1).to_broadcast([P, 4, P])
                    v.tensor_tensor(tmp.rearrange("p (b t) -> p b t", b=4), o.rearrange("p (b t) -> p b t", b=4),
                                    bs, ALU.add).then_inc(dve_drained, 1)
                    dve.wait_ge(dve_drained, u[("sp", l, g)].drained)
                    dve.wait_ge(uz_ready, 4 * l + g + 1)
                    v.tensor_tensor(M(4 + g), tmp, A(b1_zg + g * S), ALU.mult).then_inc(yg_ready, 1)
                jobs = pl.swa[l]
                biased(jobs[0])
                biased(jobs[1])
                row_factors(jobs[0])
                for s in range(9):
                    if s + 2 < 8:
                        biased(jobs[s + 2])
                    if s + 1 < 8:
                        row_factors(jobs[s + 1])
                    if s < 8:
                        if s % 2 == 1:
                            ada(ad + 6 + s // 2)
                        drain_t(jobs[s])
                    if s >= 1:
                        outputs(jobs[s - 1])
                for t in range(KT):
                    dve.wait_ge(sig_ready, 8 * l + 2 * (t // 2) + 2)
                    o = full(dve, ("ba", l, t))
                    v.tensor_tensor(ga(t), ga(t), o, ALU.mult).then_inc(dve_drained, 1)
                    o = full(dve, ("bg", l, t))
                    v.tensor_tensor(ga(8 + t), ga(8 + t), o, ALU.mult).then_inc(dve_drained, 1)
                    taken(dve, ("bg", l, t))
                    v.tensor_tensor(ga(t), ga(t), ga(8 + t), ALU.add).then_inc(merged, 1)
                ada(ad + 10)
                ada(ad + 11)
                dve.wait_ge(dve_drained, u[("ada", ad + 11)].drained)
                for c in (ADA["sc1"], ADA["sc2"]):
                    one = adac[:, 48 * l + c:48 * l + c + 16]
                    v.tensor_scalar(one, one, 1.0, None, ALU.add).then_inc(ada_ready, 1)
                for t in range(KT):
                    o = full(dve, ("out", l, t))
                    dve.wait_ge(res_scaled, 8 * l + t + 1)
                    v.tensor_tensor(X(t), X(t), o, ALU.add).then_inc(dve_drained, 1)
                layer_norm(l)

            drain("ukT", ukT)
            drain("lat", A(e_ckv))
            taken(dve, "lat")
            dve.wait_ge(e_in, 16 * N_E)
            for tt in range(NT):
                own.step(v.tensor_tensor_reduce(out=side[:, 6144 + 16:6144 + 16 + P], in0=A(e_ckv + tt * P, P),
                                                in1=A(e_ckv + tt * P, P), scale=1.0, scalar=0.0, op0=ALU.mult,
                                                op1=ALU.add, accum_out=stats[:, tt:tt + 1]))
                own.settle()
            v.tensor_scalar(stats[:, 0:4], stats[:, 0:4], 1.0 / P, None, ALU.mult).then_inc(var_ready, 1)
            stds[0] += 1
            dve.wait_ge(std_ready, stds[0])
            own.step(v.reciprocal(stats[:, 0:4], stats[:, 0:4]))
            own.settle()
            for tt in range(NT):
                c = A(e_ckv + tt * P, P)
                v.scalar_tensor_tensor(c, c, stats[:, tt:tt + 1], kvnorm, ALU.mult, ALU.mult).then_inc(lat_done, 1)
            o = full(dve, "iw")
            v.tensor_scalar(iw, o[:, 0:32], 8 ** -0.5 * 64 ** -0.5, None, ALU.mult).then_inc(dve_drained, 1)
            drain("ckvT", A(e_ckvT))
            taken(dve, "ckvT")
            i = 0
            for qb in range(1, 4):
                n = (qb + 1) * P
                work = mix[:, work_at[qb]:work_at[qb] + n]
                for j in range(8):
                    dve.wait_ge(act_drained, u[("I", qb, j)].drained)
                    relu = side[:, (i % 2) * S:(i % 2) * S + n]
                    w = iw[:, 8 * qb + j:8 * qb + j + 1]
                    if j == 0:
                        v.tensor_scalar(work, relu, w, None, ALU.mult).then_inc(isc_used, 1)
                    else:
                        dve.wait_ge(isc_used, i)
                        v.scalar_tensor_tensor(work, relu, w, work, ALU.mult, ALU.add).then_inc(isc_used, 1)
                    i += 1
                dve.wait_ge(isc_used, i)
                diag = work[:, n - P:n]
                own.step(v.tensor_tensor(diag, diag, side[:, 7168:7296], ALU.add))
            for _ in range(TOPK // 8):
                own.settle()
                for qb in range(1, 4):
                    work = mix[:, work_at[qb]:work_at[qb] + (qb + 1) * P]
                    own.step(v.max(m8[:, 8 * qb - 8:8 * qb], work))
                own.settle()
                for qb in range(1, 4):
                    work = mix[:, work_at[qb]:work_at[qb] + (qb + 1) * P]
                    own.step(v.match_replace(work, m8[:, 8 * qb - 8:8 * qb], work, -HUGE))
            own.settle()
            dve.wait_ge(r_in, 128)
            for kind in range(2):
                rp = side[:, rp_at + kind * 992:rp_at + (kind + 1) * 992].rearrange("p (j g n) -> p j g n", j=16, g=2)
                for g in range(2):
                    src = tile(mix, 2 * kind + g).rearrange("p (n r) -> p r n", r=16)
                    for half in range(2):
                        pe_ = peT[:, 16 * kind + 8 * half:16 * kind + 8 * half + 8]
                        v.tensor_tensor(rp[:, 8 * half:8 * half + 8, g, :], src[:, 0:16:2, half:half + NCMP],
                                        pe_.unsqueeze(2).to_broadcast([P, 8, NCMP]), ALU.add).then_inc(rp_ready, 1)
            dve.wait_ge(psum_full, u[("nq", 3)].full)
            for qb in range(1, 4):
                n = (qb + 1) * P
                v.tensor_scalar(hreg[:, selm_at[qb]:selm_at[qb] + n], mix[:, work_at[qb]:work_at[qb] + n],
                                -0.5 * HUGE, MASKED, ALU.is_gt, ALU.mult).then_inc(selm_ready, 1)
            dve.wait_ge(selm_ready, 3)
            attention(pl.even)

            def residual(key, n, gate):
                for t in range(KT):
                    o = full(dve, key + (t,))
                    dve.wait_ge(res_scaled, 8 * n + t + 1)
                    v.scalar_tensor_tensor(X(t), o, adac[:, gate + t:gate + t + 1], X(t), ALU.mult, ALU.add)\
                        .then_inc(dve_drained, 1)
                layer_norm(n)

            def mlp_dve(i):
                for t in range(32):
                    taken(dve, ("m1", i, t))
                    v.tensor_tensor(A(t * S), A(t * S), A(t * S), ALU.mult).then_inc(hidden_ready, 1)
                residual(("m2", i), 3 + 2 * i, 48 * i + ADA["g2"])

            residual(("mo", 0), 2, ADA["g1"])
            mlp_dve(0)

            dve.wait_ge(ada_ready, 4)
            for i, at in ((0, o_q), (1, o_k), (2, o_v)):
                for t in range(0, 8, 2):
                    name = ("oq", "ok", "ov")[i]
                    if name == "oq":
                        o = full(dve, (name, t))
                        v.tensor_scalar(A(at + t * S), o, -HD ** -0.5, None, ALU.mult).then_inc(dve_drained, 1)
                    elif name == "ok":
                        drain((name, t), A(at + t * S))
                    else:
                        c, tt = divmod(t, 4)
                        drain((name, t), arena[:, at + tt * D + c * S:at + tt * D + (c + 1) * S])
            dve.wait_ge(lam_sem, 16)
            for i in range(2):
                v.tensor_tensor_reduce(out=lam_tmp[:, i * HD:(i + 1) * HD],
                                       in0=lam_in[:, 2 * i * HD:(2 * i + 1) * HD],
                                       in1=lam_in[:, (2 * i + 1) * HD:(2 * i + 2) * HD], scale=1.0, scalar=0.0,
                                       op0=ALU.mult, op1=ALU.add, accum_out=lamc[:, i:i + 1]).then_inc(lam_dots, 1)
            c = vec_b(0, "subln")
            own.step(v.tensor_scalar(small[:, 7:8], cols[:, c:c + 1], 1.0 - LAMBDA_INIT, None, ALU.mult))
            own.settle()
            dve.wait_ge(lam_ready, 1)
            own.step(v.tensor_tensor(small[:, 6:7], lamc[:, 3:4], lamc[:, 2:3], ALU.subtract))
            own.settle()
            own.step(v.tensor_scalar(small[:, 6:7], small[:, 6:7], -LAMBDA_INIT, None, ALU.add))
            own.settle()
            attention(pl.odd)
            for h in range(HEADS):
                head_norm(h)
            residual(("mo", 1), 4, 48 + ADA["g1"])
            mlp_dve(1)
            for tt in range(NT):
                drain(("y", tt, 0), hreg[:, tt * D:tt * D + S])

        @block.gpsimd
        def _(pool):
            g = nc.gpsimd

            def scale_rows(j):
                pool.wait_ge(r_ready, j.r_count)
                z = zbuf(j)
                if j.kind == "cmp":
                    zz = z[:, 0:4 * NCMP].rearrange("p (b n) -> p b n", b=4)
                    r = stat4(recips, j).unsqueeze(2).to_broadcast([P, 4, NCMP])
                    g.tensor_tensor(zz, zz, r, ALU.mult).then_inc(s_ready, 1)
                    return
                if j.kind == "swa":
                    spans = [(qb, (0, 128, 384, 640)[qb], 256 if qb else 128) for qb in range(4)]
                else:
                    spans = [(qb, ZOFF[qb], (qb + 1) * P) for qb in range(4)]
                for qb, c, n in spans:
                    g.tensor_scalar(z[:, c:c + n], z[:, c:c + n], stat4(recips, j, qb), None, ALU.mult)\
                        .then_inc(s_ready, 1)
                if j.kind == "diff" and j.m:
                    pool.wait_ge(s_ready, j.s - 1)
                    z0 = zbuf(pl.jobs[j.J - 1])
                    g.tensor_tensor(z, z, z0, ALU.add).then_inc(s_ready, 1)

            def modulate(i, n):
                pool.wait_ge(ada_ready, 2 * (i // 2) + 2)
                c = 48 * (i // 2) + (ADA["sc1"] if i % 2 == 0 else ADA["sc2"])
                sh = 48 * (i // 2) + (ADA["sh1"] if i % 2 == 0 else ADA["sh2"])
                for t in range(KT):
                    pool.wait_ge(x_ready, 8 * (i + 1) + t + 1)
                    g.tensor_scalar(H(t), X(t), adac[:, c + t:c + t + 1], adac[:, sh + t:sh + t + 1],
                                    ALU.mult, ALU.add).then_inc(h_ready, 1)
                for t in range(KT):
                    pool.wait_ge(h_ready, 8 * i + t + 1)
                    g.tensor_scalar(X(t), X(t), ALPHA, None, ALU.mult).then_inc(res_scaled, 1)

            g.memset(mean_w[:, :], 1.0 / D).then_inc(memsets, 1)
            g.memset(head_w[:, :], 1.0 / P).then_inc(memsets, 1)
            g.memset(eps[:, :], EPS).then_inc(memsets, 1)
            pool.wait_ge(memsets, 3)
            g.memset(mix[BUCKETS:BUCKETS + 1, 384:400], -MASKED).then_inc(memsets, 1)
            pool.wait_ge(memsets, 4)
            for l in range(DEPTH):
                for tt in range(NT):
                    vn = A(b1_vn + tt * S)
                    pool.wait_ge(vn_norm, 4 * l + tt + 1)
                    g.tensor_tensor(vn, vn, lng_row, ALU.mult).then_inc(pool_own, 1)
                for tt in range(NT):
                    vn = A(b1_vn + tt * S)
                    pool.wait_ge(pool_own, 4 * l + tt + 1)
                    g.tensor_tensor(vn, vn, lnb_row, ALU.add).then_inc(vn_ready, 1)
                for t in range(4):
                    taken(pool, ("zg", l, t))
                    zg = A(b1_zg + t * S)
                    g.tensor_tensor(zg, zg, A(b1_u + t * S), ALU.mult).then_inc(uz_ready, 1)
                for j in pl.swa[l]:
                    scale_rows(j)
                pool.wait_ge(psum_full, u[("g", l, 15)].full)
                for t in range(KT):
                    c = vec_a(l, "b_out", t)
                    g.tensor_scalar(X(t), X(t), ALPHA, cols[:, c:c + 1], ALU.mult, ALU.add).then_inc(res_scaled, 1)
            pool.wait_ge(x_ready, 16)
            g.memset(tab_full[BUCKETS:BUCKETS + 1, :], -MASKED).then_inc(memsets, 1)
            pool.wait_ge(memsets, 5)
            modulate(0, 2)
            for j in pl.even:
                scale_rows(j)
            modulate(1, 3)
            modulate(2, 4)
            pool.wait_ge(psum_full, u[("oq", 0)].full)
            pool.dma_start(lam_in, bcast(a["diff_lam_2"], 256)).then_inc(lam_sem, 16)
            for j in pl.odd:
                scale_rows(j)
            modulate(3, 5)


_INS = ["x", "w_in", "b_in", "attn_sinks", "gmlp_ln_g", "gmlp_ln_b", "w_spatial", "b_spatial", "w_branch_attn",
        "w_branch_gmlp", "w_out", "b_out", "ln_g", "ln_b", "c_2", "rel_bias_2", "ada_w_2", "ada_b_2", "ln_g_2",
        "ln_b_2", "ev_w_in_2", "ev_w_out_2", "nsa_pe_k_2", "nsa_pe_v_2", "nsa_w1_k_2", "nsa_w2_k_2", "nsa_w1_v_2",
        "nsa_w2_v_2", "dsa_kv_norm_2", "dsa_w_uk_2", "dsa_w_uv_2", "od_w_in_2", "od_w_out_2", "diff_lam_2",
        "diff_subln_2", "mlp_w1_2", "mlp_w2_2"]


def kernel(**inputs):
    import concourse.bacc as bacc
    from concourse.bass_utils import run_bass_kernel_spmd

    nc = bacc.Bacc("TRN2", target_bir_lowering=False, num_devices=1)
    given = {name: np.ascontiguousarray(inputs[name]) for name in _INS}
    given.update(shape_constants())
    arrays, a = {}, {}
    for name, value in given.items():
        arrays[f"in_{name}"] = value
        a[name] = nc.dram_tensor(f"in_{name}", value.shape, mybir.dt.from_np(value.dtype), kind="ExternalInput").ap()
    out = nc.dram_tensor("out_0", (1, S, D), F32, kind="ExternalOutput").ap()
    two_blocks(nc, a, out)
    r = run_bass_kernel_spmd(nc, [arrays], core_ids=[0])
    return r.results[0]["out_0"]
```

```python
from contextlib import ExitStack
import math

import numpy as np
import concourse.bass as bass
from concourse import mybir

ALU = mybir.AluOpType
ACT = mybir.ActivationFunctionType
F32 = mybir.dt.float32
F32R = mybir.dt.float32r
AX_X = mybir.AxisListType.X

P = 128
S = 512
NT = S // P
D = 1024
KT = D // P
DEPTH = 2
HEADS = 8
HD = 64
W1 = 4864
EVEN_IN = 2528
ODD_IN = 3072
DFF = 4096
ALPHA = float(np.float32((2 * DEPTH) ** 0.25))
EPS = 1e-5
MASKED = 1e30
HUGE = 3e38
TOPK = 128
BUCKETS = 32
NCMP = 31
CHUNK = 8 * 256
RING = 4
PART = 8 * 128
SPLITS = 3
BANKS = 6
TW = 640
LAMBDA_INIT = 0.8 - 0.6 * math.exp(-0.3)
ADAS = 12
ZSLOTS = 6
AHEAD = 3
ORDER = (0, 2, 1, 3)
ZOFF = (0, 128, 384, 768)
KOFF = (0, 512, 896, 1152)


def buckets_of(dist):
    n = np.maximum(dist, 0)
    exact = BUCKETS // 2
    nf = np.maximum(n, 1).astype(np.float32)
    large = exact + (np.log(nf / exact) / math.log(128 / exact) * (BUCKETS - exact)).astype(np.int32)
    return np.where(n < exact, n, np.minimum(large, BUCKETS - 1))


def one_hot(dist):
    out = np.zeros((BUCKETS + 1, len(dist)), np.float32)
    b = buckets_of(dist)
    for i, d in enumerate(dist):
        if d >= 0:
            out[b[i], i] = 1.0
        else:
            out[BUCKETS, i] = 1.0
    return out


def shape_constants():
    ident = np.eye(P, dtype=np.float32)
    s, t = np.arange(P)[:, None], np.arange(P)[None, :]
    tril = (t <= s).astype(np.float32)
    dist = np.arange(P)[:, None] + P - np.arange(2 * P)[None, :]
    valid = (dist >= 0) & (dist < P)
    alibi = np.stack([np.where(valid, np.float32(2.0 ** -(h + 1)) * dist, MASKED) for h in range(HEADS)], 1)
    future = np.where(t <= s, 0.0, -1e30)
    wide = one_hot(511 - np.arange(TW))
    full = one_hot(np.arange(1024) - 511)
    return {
        "ident": ident, "tril": tril, "alibi": alibi.astype(np.float32).reshape(P, HEADS * 2 * P),
        "future": future.astype(np.float32), "hot_rev": wide, "hot": full,
    }


class Unit:
    def __init__(self, index, who, drained):
        self.index, self.who, self.drained = index, who, drained
        self.bank, self.full = index % BANKS, index + 1


class Job:
    pass


class Plan:

    def __init__(self):
        self.units, self.order, self.count = {}, [], {"act": 0, "dve": 0, "z": 0}
        self.chunks, self.parts, self.part_of, self.used = [], [], {}, 0
        self.jobs = []
        self.cur = {"z": 0, "p": 0, "s": 0, "m": 0, "r": 0, "pt": 0, "o": 0}

    def unit(self, key, who, n=1):
        self.count[who] += n
        u = Unit(len(self.order), who, self.count[who])
        assert key not in self.units, key
        self.units[key] = u
        self.order.append(u)
        return u

    def load(self, name, free):
        self.chunks.append([name, free])

    def part(self, chunk, key, src=("plain", 0), kt=KT, used=None):
        self.parts.append((chunk, src, kt, ("unit", key) if used is None else ("used", used)))
        for c in self.chunks:
            if c[0] == chunk:
                c[1] = ("split", len(self.parts))
        self.part_of[key] = len(self.parts) - 1

    def dense(self, key, who, chunk, src=("plain", 0), kt=KT):
        self.unit(key, who)
        self.part(chunk, key, src, kt)

    def job(self, kind, h, l=0, m=0):
        j = Job()
        j.kind, j.h, j.l, j.m, j.J = kind, h, l, m, len(self.jobs)
        j.slot = j.J % 4 if kind == "swa" else (j.J - 2 * HEADS) % ZSLOTS
        j.key = (kind, l, h, m)
        n = 1 if kind == "cmp" else 4
        j.z0, j.p0, j.s0 = self.cur["z"], self.cur["p"], self.cur["s"]
        self.cur["z"] += n
        self.cur["p"] += n
        self.cur["s"] += n
        self.cur["r"] += 1
        self.cur["m"] += kind in ("swa", "cmp")
        j.before = None
        j.mr = self.cur["m"]
        j.r_count = self.cur["r"]
        j.z, j.p, j.s = self.cur["z"], self.cur["p"], self.cur["s"]
        j.has_pt = not (kind == "diff" and m == 0)
        if j.has_pt:
            j.pt = self.cur["pt"]
            self.cur["pt"] += 1
            j.pv = self.cur["pt"]
            if kind == "swa":
                j.first_o, j.last_o = True, h >= 4
                new_o = h < 4
            elif kind in ("cmp", "sel", "win"):
                new_o = kind == "cmp" and h < 4
                j.first_o, j.last_o = kind == "cmp", kind == "win" and h >= 4
            else:
                new_o, j.first_o, j.last_o = True, True, True
            j.new_o = new_o
            if new_o:
                self.cur["o"] += 1
            j.o = self.cur["o"] - 1
        self.jobs.append(j)
        return j

    def s_units(self, j):
        if j.kind == "swa":
            for i in range(2):
                self.unit(("S", j.J, i), "z", 2)
        elif j.kind == "cmp":
            self.unit(("S", j.J, 0), "z", 1)
        else:
            for i, n in enumerate((2, 1, 1)):
                self.unit(("S", j.J, i), "z", n)

    def t_units(self, j):
        if not j.has_pt:
            return
        if j.kind == "swa":
            whos = ("act", "dve")
        elif j.kind == "cmp":
            whos = ("act",)
        else:
            whos = ("act", "dve", "act")
        for i, who in enumerate(whos):
            self.unit(("T", j.J, i), who)
        j.ptn = len(whos)


PAIRS = (0, 4, 1, 5, 2, 6, 3, 7)


def make_plan():
    pl = Plan()
    U, DN = pl.unit, pl.dense
    for k in range(KT):
        U(("xT", k), "dve" if k % 2 else "act")
    for i in range(3):
        U(("vec", i), "dve")
    for i in range(2):
        U(("bias", i), "act")

    pl.swa = []
    for l in range(DEPTH):
        a = [ADAS * l]

        def next_ada():
            if a[0] < ADAS * (l + 1):
                ada(pl, a[0])
                a[0] += 1

        def two(name, c, who="act", paired=False):
            pl.load((name, l, c), None)
            for t in (2 * c, 2 * c + 1):
                DN((name, l, t), who, (name, l, c), ("paired" if paired else "plain", t % 2))
            next_ada()

        two("vg", 0)
        two("vg", 1)
        two("u", 0)
        U(("wT", l), "dve")
        for tt in range(4):
            U(("vgT", l, tt), "dve")
        two("u", 1)
        pl.load(("kv", l, 0), None)
        DN(("v", l), "act", ("kv", l, 0), ("plain", 1))
        DN(("k", l), "act", ("kv", l, 0), ("plain", 0))
        next_ada()
        two("za", 0, paired=True)
        two("za", 1, paired=True)
        U(("vT", l), "dve")
        two("zg", 0)
        two("zg", 1)
        two("q", 0, "dve", True)
        two("q", 1, "dve", True)
        for g in range(4):
            U(("sp", l, g), "dve")
        jobs = [pl.job("swa", h, l) for h in PAIRS]
        pl.swa.append(jobs)
        pl.s_units(jobs[0])
        pl.s_units(jobs[1])
        for s in range(8):
            if s + 2 < 8:
                pl.s_units(jobs[s + 2])
            two("g", s)
            pl.t_units(jobs[s])
        for c in range(2):
            pl.load(("ba", l, c), None)
            pl.load(("bg", l, c), None)
            for t in range(4 * c, 4 * c + 4):
                DN(("ba", l, t), "dve", ("ba", l, c), ("plain", t % 4), 4)
                DN(("bg", l, t), "dve", ("bg", l, c), ("plain", t % 4), 4)
        for c in range(4):
            pl.load(("out", l, c), None)
            for t in (2 * c, 2 * c + 1):
                DN(("out", l, t), "dve", ("out", l, c), ("plain", t % 2))

    pl.load("lat", None)
    DN("lat", "act", "lat", ("plain", 0))
    DN("ik", "act", "lat", ("twice", 2))
    pl.load("misc", None)
    DN("misc", "act", "misc", ("plain", 0))
    U("latT", "dve")
    for c in range(2):
        pl.load(("iq", c), None)
        for t in (2 * c, 2 * c + 1):
            DN(("iq", t), "act", ("iq", c), ("plain", t % 2))
        if c == 0:
            U("miscT", "dve")
    U("ckvT", "dve")
    pl.load(("dq", 0), None)
    pl.load(("dq", 1), None)
    for qb in range(1, 4):
        for j in range(8):
            U(("I", qb, j), "act")
            if qb < 3 and j % 4 == 3:
                t = (qb - 1) * 2 + j // 4
                DN(("dq", t), "act", ("dq", t // 2), ("plain", t % 2))
    for name, one, two_ in (("c", "kc", "vc"), ("s", "vs", "ks"), ("w", "vw", "kw")):
        pl.load(("kv2", name), None)
        DN(one, "act", ("kv2", name), ("plain", 1 if name != "c" else 0))
        DN(two_, "act", ("kv2", name), ("plain", 0 if name != "c" else 1))
        if name != "c":
            U(one + "T", "act")
    U("biasc0", "act")
    U("biasc1", "act")
    U("ukT", "dve")
    for c in range(2):
        pl.load(("nq", c), None)
        for t in (2 * c, 2 * c + 1):
            DN(("nq", t), "act", ("nq", c), ("paired", t % 2))
    for h in range(8):
        U(("ql", h), "act")
    pl.phase = [len(pl.parts)]
    for kind in range(2):
        pl.used += 1
        pl.load(("w1", kind, 0), ("used", pl.used))
        pl.load(("w1", kind, 1), ("unit", ("hid", kind, 1)))
        for half in range(2):
            U(("hid", kind, half), "act")
    U("kcT", "act")
    U("vct", "act")
    jobs = [pl.job(kind, h) for h in PAIRS for kind in ("cmp", "sel", "win")]
    jobs += [pl.job("dsa", h) for h in range(8)]
    pl.even = jobs
    steps(pl, jobs)
    mixer_out(pl, 0)
    mlp(pl, 0)
    for name in ("oq", "ok", "ov"):
        for c in range(4):
            pl.load((name, c), None)
            for t in (2 * c, 2 * c + 1):
                DN((name, t), "act", (name, c), ("plain", t % 2))
                if name == "ov" and t:
                    U(("ovT", t - 1), "dve")
    U(("ovT", 7), "dve")
    pl.phase.append(len(pl.parts))
    jobs = [pl.job("diff", h, m=m) for h in range(8) for m in range(2)]
    pl.odd = jobs
    steps(pl, jobs)
    mixer_out(pl, 1)
    mlp(pl, 1)
    for tt in range(NT):
        for c in range(2):
            U(("y", tt, c), "act" if c else "dve")
    return pl


def ada(pl, n):
    pl.load(("ada", n), ("acc", n + 1))
    pl.unit(("ada", n), "dve")


def steps(pl, jobs):
    n = len(jobs)
    for i, j in enumerate(jobs):
        j.before = None
        if i >= ZSLOTS:
            j.before = jobs[i - ZSLOTS] if jobs[i - ZSLOTS].has_pt else jobs[i - ZSLOTS + 1]
    for i in range(AHEAD):
        pl.s_units(jobs[i])
    for s in range(n + 2):
        if s + AHEAD < n:
            pl.s_units(jobs[s + AHEAD])
        if s < n:
            pl.t_units(jobs[s])
        if 0 <= s - 2 < n:
            j = jobs[s - 2]
            if j.kind == "dsa":
                pl.unit(("uv", j.h), "act")
            if j.kind == "diff" and j.m:
                pl.unit(("ms", j.h), "dve")


def mixer_out(pl, i):
    for c in range(4):
        pl.load(("mo", i, c), None)
        for t in (2 * c, 2 * c + 1):
            pl.dense(("mo", i, t), "dve", ("mo", i, c), ("plain", t % 2))


def mlp(pl, i):
    for half in range(2):
        for c in range(8 * half, 8 * half + 8):
            pl.load(("m1", i, c), None)
            for t in (2 * c, 2 * c + 1):
                pl.dense(("m1", i, t), "act", ("m1", i, c), ("plain", t % 2))
            if i == 0:
                ada(pl, 24 + 8 * half + c)
        for c in range(4):
            for t in (2 * c, 2 * c + 1):
                pl.unit(("m2", i, half, t), "dve")
            for kc in range(2):
                name = ("m2", i, half, c, kc)
                pl.load(name, None)
                for t in (2 * c, 2 * c + 1):
                    key = ("m2", i, half, t)
                    if kc == 0:
                        pl.used += 1
                    pl.part(name, key, ("plain", t % 2), used=pl.used if kc == 0 else None)
            if i == 0 and half == 0:
                ada(pl, 32 + 2 * c)
                ada(pl, 33 + 2 * c)


N_VEC, N_E = 19, 7

N_A, N_B, N_C = 124, 128, 41


def vec_a(l, name, t=0):
    at = {"q": 0, "k": 4, "v": 5, "za": 6, "u": 10, "vg": 14, "zg": 18, "g": 22,
          "b_out": 38, "ln_g": 46, "ln_b": 54}[name]
    return 62 * l + at + t


def vec_b(i, name, t=0):
    if name == "ada_b":
        return N_A + 48 * i + t
    if name == "ln_g":
        return N_A + 96 + 8 * i + t
    if name == "ln_b":
        return N_A + N_B + 8 * i + t
    return N_A + N_B + {"subln": 32, "c": 33}[name] + t


ADA = {"sh1": 0, "sc1": 8, "g1": 16, "sh2": 24, "sc2": 32, "g2": 40}


class Steps:

    def __init__(self, eng, sem):
        self.eng, self.sem, self.n = eng, sem, 0

    def step(self, ins):
        self.n += 1
        return ins.then_inc(self.sem, 1)

    def settle(self):
        self.eng.wait_ge(self.sem, self.n)


def two_blocks(nc, a, out):
    pl = make_plan()
    u = pl.units
    bias_rows = nc.dram_tensor("bias_rows", (16, P, TW), F32, kind="Internal").ap()

    with ExitStack() as ctx:
        def sb(name, cols):
            return ctx.enter_context(nc.sbuf_tensor(name, [P, cols], F32))

        def sem(name):
            return ctx.enter_context(nc.semaphore(name))

        cols = sb("cols", N_A + N_B + N_C)
        adac = sb("adac", 2 * 48)
        ident = sb("ident", P)
        mean_w = sb("mean_w", P)
        head_w = sb("head_w", P)
        tril = sb("tril", P)
        negm = sb("negm", 4 * ZSLOTS)
        sums = sb("sums", 4 * ZSLOTS)
        recips = sb("recips", 4 * ZSLOTS)
        esink = sb("esink", 4 * ZSLOTS)
        sinks = sb("sinks", 2 * HEADS)
        nsinks = sb("nsinks", 2 * HEADS)
        stats = sb("stats", 4 * 6 + 4 * 2 + 4)
        cact = sb("cact", KT)
        ones = sb("ones", 1)
        ccols = sb("ccols", 4 * 32)
        small = sb("small", 8)
        eps = sb("eps", 1)
        base = -(-nc.sbuf_base // 64) * 64

        def at(name, off, n, dt=F32):
            return nc.alloc_sbuf_tensor_at(name, [P, n], dt, offset=base + 4 * off)

        X0, HH0, HL0, MIX0, RAW0, W0 = 0, 4096, 8192, 12288, 16384, 24576
        REST = W0 + 2 * SPLITS * PART
        raw = at("raw", RAW0, RING * CHUNK)
        w_hi = at("w_hi", W0, SPLITS * PART, F32R)
        w_lo = at("w_lo", W0 + SPLITS * PART, SPLITS * PART, F32R)
        zarea = at("zarea", W0, 4 * 1280)
        x = at("x", X0, KT * S)
        x_lo = at("x_lo", X0, KT * S, F32R)
        hi32, hi_r = at("hi32", HH0, KT * S), at("hi_r", HH0, KT * S, F32R)
        lo32, lo_r = at("lo32", HL0, KT * S), at("lo_r", HL0, KT * S, F32R)
        mix = at("mix", MIX0, KT * S)
        rest = at("rest", REST, 21248)
        psum = ctx.enter_context(nc.psum_tensor("psum", [P, 8, 512], F32))

        def tile(t, i, n=S):
            return t[:, i * n:(i + 1) * n]

        def X(t):
            return tile(x, t)

        def H(t):
            return tile(lo32, t)

        def HI(t):
            return tile(hi_r, t).bitcast(F32)

        def M(t):
            return tile(mix, t)

        def R(off, n=S):
            return rest[:, off:off + n]

        alibi = R(0, 2048)
        lng_row, lnb_row, bs_row = R(5632), R(6144), R(6656)
        ws_raw, ws_t = R(7168), R(7680)
        b1_z, b1_pt, acc_at, b1_vn, b1_zg, b1_q = 2048, 8704, 20480, 8704, 10752, 12800
        b1_k, b1_v, b1_ga, b1_vT = 14848, 15360, 15872, 19968
        za, ug = mix[:, 0:2048], mix[:, 2048:4096]
        za_lo = at("za_lo", MIX0, 4 * S, F32R)
        q_hi = at("q_hi", REST + b1_q, 4 * S, F32R)
        u_hi = at("u_hi", MIX0 + 2048, 4 * S, F32R)
        zg_lo = at("zg_lo", REST + b1_zg, 4 * S, F32R)
        ga_lo = at("ga_lo", REST + b1_ga, KT * S, F32R)
        SWA_Z = 896

        def ga(i):
            return R(b1_ga + i * S) if i < 8 else H(i - 8)

        T_AT, PT_AT, A0 = 0, 1536, 5088
        biasc = R(4096, 4 * 8 * NCMP)

        def A(off, n=S):
            return R(A0 + off, n)

        e_q, e_dq, e_ql, e_ks, e_vs, e_kw, e_vw = 0, 2048, 4096, 8192, 8704, 9216, 9728
        e_ckv, e_ckvT, e_ik, e_kc, e_vc, e_iq = 10240, 10752, 11264, 11776, 12288, 6144
        small0 = 12800
        kcT = A(small0, NCMP)
        vct = A(small0 + 32, P)
        hid = A(small0 + 160, 248)
        gates = A(small0 + 416, 96)
        iw = A(small0 + 512, 32)
        w2kv = A(small0 + 544, 256)
        kvnorm = A(small0 + 800, P)
        ukT = A(small0 + 928, S)
        peT = A(small0 + 1440, 32)
        m8 = A(small0 + 1472, 24)
        e_tmp = small0 + 1504
        e_olat, w_uv = 2048, A(3072, S)
        hot_full, tab_full, uk_raw, future = A(0, 1024), A(1024, 16), A(1040, 512), A(1552, P)
        rp_at, relu_at = 2048, 2048
        o_q, o_k, o_v, o_sq = 0, 4096, 8192, 12288
        o_tmp = 13312
        lam_in = A(14336, 256)
        lam_tmp = A(14592, 128)
        lamc = small[:, 0:4]
        rstd = mix[:, 0:S]
        work_at = {1: PT_AT, 2: PT_AT + 256, 3: PT_AT + 640}
        selm_at = {1: 2560, 2: 2816, 3: 3200}
        hid_hi = at("hid_hi", REST + PT_AT, 16 * S, F32R)
        hid_lo = at("hid_lo", REST + PT_AT + 16 * S, 16 * S, F32R)

        def work(qb):
            return R(work_at[qb], (qb + 1) * P)

        def selm(qb):
            return lo32[:, selm_at[qb]:selm_at[qb] + (qb + 1) * P]

        def zbuf(j):
            if j.kind == "swa":
                return R(b1_z + j.slot * SWA_Z, SWA_Z)
            if j.slot >= 4:
                return hi32[:, (j.slot - 4) * 1280:(j.slot - 3) * 1280]
            return zarea[:, j.slot * 1280:(j.slot + 1) * 1280]

        def ptbuf(j):
            n, at_ = (SWA_Z, b1_pt) if j.kind == "swa" else (1280, PT_AT)
            return R(at_ + (j.pt % 2) * n, n)

        def stat4(t, j, i=None):
            return t[:, 4 * j.slot:4 * j.slot + 4] if i is None else t[:, 4 * j.slot + i:4 * j.slot + i + 1]

        def tbuf(ti):
            return R(T_AT + (ti % 3) * S)

        def operand(hi, lo):
            return (lambda k: tile(hi, k)), (lambda k: tile(lo, k))

        tables = [h for h in PAIRS] + [8 + h for h in range(8)] + list(range(16))
        for i, j in enumerate(pl.even):
            j.ti = i // 3 if j.kind != "dsa" else 8 + j.h
            j.t_last = j.kind in ("win", "dsa")
        for i, j in enumerate(pl.odd):
            j.ti, j.t_last = 16 + i, True

        psum_full = sem("psum_full")
        act_drained = sem("act_drained")
        dve_drained = sem("dve_drained")
        z_ready = sem("z_ready")
        m_ready = sem("m_ready")
        p_ready = sem("p_ready")
        sink_ready = sem("sink_ready")
        s_ready = sem("s_ready")
        pv_done = sem("pv_done")
        o_drained = sem("o_drained")
        landed = [sem(f"landed{i}") for i in range(RING)]
        part_used = sem("part_used")
        w_hi_ready = sem("w_hi_ready")
        w_lo_ready = sem("w_lo_ready")
        hi_ready = sem("hi_ready")
        op_ready = sem("op_ready")
        acc_ready = sem("acc_ready")
        const_in, x_in, rows_in = sem("const_in"), sem("x_in"), sem("rows_in")
        vec_in, tab_in = sem("vec_in"), sem("tab_in")
        e_in, r_in, uv_in, lam_sem = sem("e_in"), sem("r_in"), sem("uv_in"), sem("lam_sem")
        t_in = [sem(f"t_in{i}") for i in range(3)]
        memsets, bias_out = sem("memsets"), sem("bias_out")
        c_ready, ada_ready = sem("c_ready"), sem("ada_ready")
        ws_masked = sem("ws_masked")
        vg_gelu, vn_norm, vn_ready = sem("vg_gelu"), sem("vn_norm"), sem("vn_ready")
        uz_ready, yg_ready = sem("uz_ready"), sem("yg_ready")
        sig_ready, merged = sem("sig_ready"), sem("merged")
        res_scaled = sem("res_scaled")
        ln_centered, ln_squared, stat_full = sem("ln_centered"), sem("ln_squared"), sem("stat_full")
        ln_scaled, x_ready, h_ready = sem("ln_scaled"), sem("x_ready"), sem("h_ready")
        nsink_ready = sem("nsink_ready")
        std_ready, var_ready = sem("std_ready"), sem("var_ready")
        lat_done, relu_ready, isc_used = sem("lat_done"), sem("relu_ready"), sem("isc_used")
        future_used, iw_ready, gates_ready = sem("future_used"), sem("iw_ready"), sem("gates_ready")
        mask_in, x_whole = sem("mask_in"), sem("x_whole")
        ya_ready, ccols_ready = sem("ya_ready"), sem("ccols_ready")
        selm_ready, rp_ready = sem("selm_ready"), sem("rp_ready")
        hidden_ready = sem("hidden_ready")
        sq_ready, o_normed = sem("sq_ready"), sem("o_normed")
        lam_ready, lam_dots = sem("lam_ready"), sem("lam_dots")
        y_out = sem("y_out")
        dve_own, pool_own = sem("dve_own"), sem("pool_own")
        drained_by = {"act": act_drained, "dve": dve_drained, "z": z_ready}

        def freed(eng, token):
            kind, n = token
            if kind == "unit":
                eng.wait_ge(psum_full, u[n].full)
            else:
                eng.wait_ge({"used": part_used, "split": w_lo_ready, "acc": acc_ready}[kind], n)

        def bcast(ap, n, off=0):
            return bass.AP(tensor=ap.tensor, offset=ap.offset + off, ap=[[0, P], [1, n]])

        def full(eng, key):
            eng.wait_ge(psum_full, u[key].full)
            return psum[:, u[key].bank, :]

        def taken(eng, key):
            eng.wait_ge(drained_by[u[key].who], u[key].drained)

        block = ctx.enter_context(nc.Block())

        ev = a["ev_w_in_2"][0]
        at1 = {"q": 0, "kv": 512, "za": 768, "u": 1280, "vg": 1792, "zg": 2304, "g": 2816}
        ate = {"iq": 1944, "dq": 1304, "nq": 0, "c": 512, "s": 768, "w": 1024}

        def pieces(name):
            kind = name[0] if isinstance(name, tuple) else name
            every, ks = slice(0, P), slice(0, KT)

            def plain(w, c0, n, kt=KT):
                return (kt, n), [(every, slice(0, kt), slice(0, n),
                                  w.rearrange("(k p) n -> p k n", p=P)[:, :, c0:c0 + n])]

            def joined(w, parts):
                loads, c = [], 0
                for c0, n in parts:
                    loads.append((every, ks, slice(c, c + n), w.rearrange("(k p) n -> p k n", p=P)[:, :, c0:c0 + n]))
                    c += n
                return (KT, c), loads

            def split(w, c0, n, kt):
                loads = []
                for hf in range(2):
                    src = w[hf * 256:hf * 256 + 256, c0:c0 + n].rearrange("(t d) n -> d t n", d=HD)
                    loads.append((slice(hf * HD, hf * HD + HD), slice(0, 4), slice(0, n), src))
                if kt > 4:
                    loads.append((every, slice(4, kt), slice(0, n),
                                  w[512:1024, c0:c0 + n].rearrange("(k p) n -> p k n", p=P)))
                return (kt, n), loads

            if kind == "ada":
                l, c = divmod(name[1], 24)
                return plain(a["ada_w_2"][l], 256 * c, 256)
            if kind in ("q", "za"):
                c0 = at1[kind] + P * name[2]
                return joined(a["w_in"][name[1]], ((c0, P), (c0 + 256, P)))
            if kind in at1:
                return plain(a["w_in"][name[1]], at1[kind] + 256 * name[2], 256)
            if kind == "ba":
                return split(a["w_branch_attn"][name[1]], 512 * name[2], 512, 4)
            if kind == "bg":
                return plain(a["w_branch_gmlp"][name[1]], 512 * name[2], 512, 4)
            if kind == "out":
                return plain(a["w_out"][name[1]], 256 * name[2], 256)
            if kind == "lat":
                return joined(ev, ((1816, 128), (2456, 64)))
            if kind == "misc":
                return joined(ev, ((1280, 96), (2496, 32)))
            if kind == "nq":
                return joined(ev, ((P * name[1], P), (P * name[1] + 256, P)))
            if kind in ("iq", "dq"):
                return plain(ev, ate[kind] + 256 * name[1], 256)
            if kind == "kv2":
                return plain(ev, ate[name[1]], 256)
            if kind == "w1":
                w = (a["nsa_w1_k_2"], a["nsa_w1_v_2"])[name[1]][0]
                return plain(w[name[2] * D:(name[2] + 1) * D, :], 0, 256)
            if kind == "mo":
                if name[1] == 0:
                    return split(a["ev_w_out_2"][0], 256 * name[2], 256, 8)
                return plain(a["od_w_out_2"][0], 256 * name[2], 256)
            if kind in ("oq", "ok", "ov"):
                return plain(a["od_w_in_2"][0], 1024 * ("oq", "ok", "ov").index(kind) + 256 * name[1], 256)
            if kind == "m1":
                return plain(a["mlp_w1_2"][name[1]], 256 * name[2], 256)
            if kind == "m2":
                _, i, half, c, kc = name
                r0 = (2 * half + kc) * D
                return plain(a["mlp_w2_2"][i][r0:r0 + D, :], 256 * c, 256)
            raise KeyError(name)

        def slot_view(i, shape):
            kt, n = shape
            return raw[:, (i % RING) * CHUNK:(i % RING) * CHUNK + kt * n].rearrange("p (k n) -> p k n", k=kt)

        arrival, reached = {}, [0] * RING
        for i, (name, _) in enumerate(pl.chunks):
            reached[i % RING] += 16 * len(pieces(name)[1])
            arrival[name] = (i, reached[i % RING])

        def arrived(eng, name):
            i, n = arrival[name]
            eng.wait_ge(landed[i % RING], n)
            return slot_view(i, pieces(name)[0])

        def part_source(view, src):
            how, c = src
            if how == "plain":
                return view[:, :, c * P:(c + 1) * P]
            if how == "paired":
                return view.rearrange("p k (b t d) -> p k b t d", b=2, d=HD)[:, :, :, c, :]
            return view[:, :, c * HD:(c + 1) * HD].unsqueeze(2).to_broadcast([P, view.shape[1], 2, HD])

        def part_view(ring, q):
            _, src, kt, _ = pl.parts[q]
            v = ring[:, (q % SPLITS) * PART:(q % SPLITS) * PART + kt * P]
            if src[0] == "plain":
                return v.rearrange("p (k n) -> p k n", k=kt)
            return v.rearrange("p (k b d) -> p k b d", k=kt, b=2)

        @block.sync
        def _(sp):
            def rows(ap, off, n):
                return bass.AP(tensor=ap.tensor, offset=ap.offset + off, ap=[[P, n], [1, P]])

            def paired_rows(ap, off):
                return bass.AP(tensor=ap.tensor, offset=ap.offset + off, ap=[[HD, 4], [256, 2], [1, HD]])

            vecs = []
            for l in range(DEPTH):
                r, b = 62 * l, l * W1
                for row, off in ((r, b), (r + 6, b + 768)):
                    vecs.append((mix[row:row + 4, 0:P].rearrange("p (b d) -> p b d", b=2), paired_rows(a["b_in"], off)))
                vecs.append((mix[r + 4:r + 6, 0:P], rows(a["b_in"], b + 512, 2)))
                vecs.append((mix[r + 10:r + 38, 0:P], rows(a["b_in"], b + 1280, 28)))
                for i, name in enumerate(("b_out", "ln_g", "ln_b")):
                    vecs.append((mix[r + 38 + 8 * i:r + 46 + 8 * i, 0:P], rows(a[name], l * D, 8)))
            vecs.append((mix[0:96, P:2 * P], rows(a["ada_b_2"], 0, 96)))
            vecs.append((mix[96:128, P:2 * P], rows(a["ln_g_2"], 0, 32)))
            vecs.append((mix[0:32, 2 * P:3 * P], rows(a["ln_b_2"], 0, 32)))
            vecs.append((mix[32:33, 2 * P:3 * P], rows(a["diff_subln_2"], 0, 1)))
            vecs.append((mix[33:41, 2 * P:3 * P], rows(a["c_2"], 0, 8)))
            assert len(vecs) == N_VEC

            def vectors():
                for dst, src in vecs:
                    sp.dma_start(dst, src).then_inc(vec_in, 16)
                sp.dma_start(mix[0:BUCKETS, 384:400], a["rel_bias_2"]).then_inc(tab_in, 16)
                sp.dma_start(mix[0:BUCKETS + 1, 512:512 + TW], a["hot_rev"]).then_inc(tab_in, 16)

            for i, (name, _) in enumerate(pl.chunks):
                if i == 2:
                    vectors()
                if i >= RING:
                    freed(sp, pl.chunks[i - RING][1])
                shape, loads = pieces(name)
                v = slot_view(i, shape)
                for ps, ks, ns, src in loads:
                    sp.dma_start(v[ps, ks, ns], src).then_inc(landed[i % RING], 16)
            for tt in range(NT):
                taken(sp, ("y", tt, 0))
                taken(sp, ("y", tt, 1))
                sp.dma_start(out[0, tt * P:(tt + 1) * P, :], hi32[:, tt * D:(tt + 1) * D]).then_inc(y_out, 16)
            sp.wait_ge(y_out, 16 * NT)

        @block.tensor
        def _(pe):
            made = [0]

            def begin(key):
                unit = u[key]
                assert unit.index == made[0], (key, unit.index, made[0])
                made[0] += 1
                if unit.index >= BANKS:
                    before = pl.order[unit.index - BANKS]
                    pe.wait_ge(drained_by[before.who], before.drained)
                return psum[:, unit.bank, :]

            part = [0]

            def multiply(o, chunk, op, first=True, last=True):
                q = part[0]
                part[0] += 1
                name, _, kt, token = pl.parts[q]
                assert name == chunk, (name, chunk)
                pe.wait_ge(w_lo_ready, q + 1)
                hi, lo = (r[:, (q % SPLITS) * PART:(q % SPLITS + 1) * PART] for r in (w_hi, w_lo))
                for k in range(kt):
                    w = slice(k * P, (k + 1) * P)
                    nc.tensor.matmul(o, hi[:, w], op[0](k), start=first and k == 0, stop=False)
                    nc.tensor.matmul(o, hi[:, w], op[1](k), start=False, stop=False)
                    mm = nc.tensor.matmul(o, lo[:, w], op[0](k), start=False, stop=last and k == kt - 1)
                mm.then_inc(psum_full if token[0] == "unit" else part_used, 1)

            def dense(key, chunk, op):
                multiply(begin(key), chunk, op)

            def ada(n):
                o = begin(("ada", n))
                pe.wait_ge(acc_ready, n + 1)
                acc = R(acc_at + (n % 2) * 256, 256)
                for t in range(2):
                    mm = nc.tensor.matmul(o[:, t:t + 1], acc[:, t * P:(t + 1) * P], ones[:, :], start=True, stop=True)
                mm.then_inc(psum_full, 1)

            def wait_op(i):
                for k in range(KT):
                    pe.wait_ge(op_ready, 8 * i + k + 1)

            def turn(key, src):
                o = begin(key)
                for tt in range(NT):
                    mm = nc.tensor.transpose(o[:, tt * P:(tt + 1) * P], src[:, tt * P:(tt + 1) * P], ident[:, :])
                mm.then_inc(psum_full, 1)

            def scores(j):
                def emit(o, c, lhs, rhs, n):
                    return nc.tensor.matmul(o[:, c:c + n], lhs, rhs, start=True, stop=True)

                hf = slice((j.h >= 4) * HD, (j.h >= 4) * HD + HD)
                t = j.h % 4
                if j.kind == "swa":
                    q, k = R(b1_q + t * S)[hf, :], R(b1_k)[hf, :]
                    for i in range(2):
                        o = begin(("S", j.J, i))
                        c = 0
                        for qb in (2 * i, 2 * i + 1):
                            k0 = max(0, qb - 1) * P
                            n = (qb + 1) * P - k0
                            mm = emit(o, c, q[:, qb * P:(qb + 1) * P], k[:, k0:k0 + n], n)
                            c += n
                        mm.then_inc(psum_full, 1)
                elif j.kind == "cmp":
                    o = begin(("S", j.J, 0))
                    q = A(e_q + t * S)[hf, :]
                    for qb in range(4):
                        mm = emit(o, qb * NCMP, q[:, qb * P:(qb + 1) * P], kcT[hf, :], NCMP)
                    mm.then_inc(psum_full, 1)
                else:
                    if j.kind in ("sel", "win"):
                        q = A(e_q + t * S)[hf, :]
                        k = A(e_ks if j.kind == "sel" else e_kw)[hf, :]
                    elif j.kind == "dsa":
                        q, k = A(e_ql + j.h * S), A(e_ckvT)
                    else:
                        q, k = A(o_q + j.h * S)[j.m * HD:(j.m + 1) * HD, :], A(o_k + j.h * S)[j.m * HD:(j.m + 1) * HD, :]
                    for i, qbs in enumerate(((0, 2), (1,), (3,))):
                        o = begin(("S", j.J, i))
                        c = 0
                        for qb in qbs:
                            n = (qb + 1) * P
                            mm = emit(o, c, q[:, qb * P:(qb + 1) * P], k[:, 0:n], n)
                            c += n
                        mm.then_inc(psum_full, 1)

            def transposes(j):
                if not j.has_pt:
                    return
                pe.wait_ge(s_ready, j.s)
                z = zbuf(j)
                if j.kind == "swa":
                    plan = [[(768 * 0 + (0 if qb == 0 else 256 * qb), qb * P) for qb in range(4)],
                            [(256 * qb - 128, (qb - 1) * P) for qb in range(1, 4)]]
                elif j.kind == "cmp":
                    plan = [[(qb * NCMP, qb * P) for qb in range(4)]]
                else:
                    plan = [[(ZOFF[qb], qb * P) for qb in range(4)],
                            [(ZOFF[qb] + P, (qb - 1) * P) for qb in range(1, 4)],
                            [(ZOFF[2] + 2 * P, 0), (ZOFF[3] + 2 * P, P), (ZOFF[3] + 3 * P, 2 * P)]]
                for i, moves in enumerate(plan):
                    o = begin(("T", j.J, i))
                    for src, dst in moves:
                        n = NCMP if j.kind == "cmp" else P
                        mm = nc.tensor.transpose(o[0:n, dst:dst + P], z[:, src:src + n], ident[:, :])
                    mm.then_inc(psum_full, 1)

            def values(j):
                if not j.has_pt:
                    return
                if j.new_o and j.o >= 2:
                    pe.wait_ge(o_drained, j.o - 1)
                for i in range(j.ptn):
                    taken(pe, ("T", j.J, i))
                pt = ptbuf(j)
                bank = psum[:, 6 + j.o % 2, :]
                hf = slice((j.h >= 4) * HD, (j.h >= 4) * HD + HD)
                if j.kind == "swa":
                    v = R(b1_v).rearrange("p (b f) -> p b f", b=4)
                    for qb in range(4):
                        mm = nc.tensor.matmul(bank[hf, qb * P:(qb + 1) * P], v[:, qb, hf], pt[:, qb * P:(qb + 1) * P],
                                              start=True, stop=qb == 0)
                        if qb:
                            mm = nc.tensor.matmul(bank[hf, qb * P:(qb + 1) * P], v[:, qb - 1, hf],
                                                  pt[:, 512 + (qb - 1) * P:512 + qb * P], start=False, stop=True)
                elif j.kind == "cmp":
                    mm = nc.tensor.matmul(bank[hf, :], vct[0:NCMP, hf], pt[0:NCMP, 0:512], start=True, stop=False,
                                          skip_group_check=True)
                else:
                    for kb in range(4):
                        n = (4 - kb) * P
                        if j.kind in ("sel", "win"):
                            v = A(e_vs if j.kind == "sel" else e_vw).rearrange("p (b f) -> p b f", b=4)[:, kb, hf]
                            o = bank[hf, kb * P:512]
                            start, stop = False, j.kind == "win" and kb == 3
                        elif j.kind == "dsa":
                            v = A(e_ckv).rearrange("p (b f) -> p b f", b=4)[:, kb, :]
                            o, start, stop = bank[:, kb * P:512], kb == 0, kb == 3
                        else:
                            v = A(o_v + j.h * S + kb * P, P)
                            o, start, stop = bank[:, kb * P:512], kb == 0, kb == 3
                        mm = nc.tensor.matmul(o, v, pt[:, KOFF[kb]:KOFF[kb] + n], start=start, stop=stop,
                                              skip_group_check=True)
                mm.then_inc(pv_done, 1)

            def after(j):
                if j.kind == "dsa":
                    pe.wait_ge(o_drained, j.o + 1)
                    pe.wait_ge(uv_in, 16)
                    o = begin(("uv", j.h))
                    hf = (j.h % 2) * HD
                    nc.tensor.matmul(o[hf:hf + HD, :], w_uv[:, j.h * HD:(j.h + 1) * HD], A(e_olat + (j.h % 2) * S),
                                     start=True, stop=True).then_inc(psum_full, 1)
                if j.kind == "diff" and j.m:
                    pe.wait_ge(sq_ready, j.h + 1)
                    o = begin(("ms", j.h))
                    nc.tensor.matmul(o, head_w[:, :], A(o_sq + (j.h % 2) * S), start=True, stop=True)\
                        .then_inc(psum_full, 1)

            def attention(jobs):
                for j in jobs[:AHEAD]:
                    scores(j)
                for s in range(len(jobs) + 2):
                    if s + AHEAD < len(jobs):
                        scores(jobs[s + AHEAD])
                    if s < len(jobs):
                        transposes(jobs[s])
                    if 0 <= s - 1 < len(jobs):
                        values(jobs[s - 1])
                    if 0 <= s - 2 < len(jobs):
                        after(jobs[s - 2])

            def mean(n, key, tiles):
                for t in tiles:
                    taken(pe, key + (t,))
                    mm = nc.tensor.matmul(psum[:, 6, :], mean_w[:, :], X(t), start=t == 0, stop=t == KT - 1,
                                          skip_group_check=True)
                if tiles[-1] == KT - 1:
                    mm.then_inc(stat_full, 1)

            def variance(n):
                for t in range(KT):
                    pe.wait_ge(ln_squared, 8 * n + t + 1)
                    mm = nc.tensor.matmul(psum[:, 7, :], mean_w[:, :], H(t), start=t == 0, stop=t == KT - 1)
                mm.then_inc(stat_full, 1)

            pe.wait_ge(x_in, 80)
            for k in range(KT):
                o = begin(("xT", k))
                for tt in range(NT):
                    mm = nc.tensor.transpose(o[:, tt * P:(tt + 1) * P],
                                             lo32[:, tt * D + k * P:tt * D + (k + 1) * P], ident[:, :])
                mm.then_inc(psum_full, 1)
            pe.wait_ge(memsets, 5)
            pe.wait_ge(vec_in, 16 * N_VEC)
            for i, n in enumerate((N_A, N_B, N_C)):
                o = begin(("vec", i))
                nc.tensor.transpose(o[:, 0:n], mix[0:n, i * P:(i + 1) * P], ident[0:n, 0:n]).then_inc(psum_full, 1)
            pe.wait_ge(tab_in, 32)
            tab, hot = mix[0:BUCKETS + 1, 384:400], mix[0:BUCKETS + 1, 512:512 + TW]
            for i, (c, n) in enumerate(((0, 512), (512, 128))):
                o = begin(("bias", i))
                nc.tensor.matmul(o[0:16, 0:n], tab, hot[:, c:c + n], start=True, stop=True).then_inc(psum_full, 1)
            X_OP, H_OP = operand(hi_r, x_lo), operand(hi_r, lo_r)
            for l in range(DEPTH):
                next_ada = [ADAS * l]

                def one_ada():
                    if next_ada[0] < ADAS * (l + 1):
                        ada(next_ada[0])
                        next_ada[0] += 1

                def two(name, c):
                    for t in (2 * c, 2 * c + 1):
                        dense((name, l, t), (name, l, c), X_OP)
                    one_ada()

                wait_op(l)
                two("vg", 0)
                two("vg", 1)
                two("u", 0)
                pe.wait_ge(ws_masked, l + 1)
                o = begin(("wT", l))
                for g in range(4):
                    mm = nc.tensor.transpose(o[:, g * P:(g + 1) * P], ws_raw[:, g * P:(g + 1) * P], ident[:, :])
                mm.then_inc(psum_full, 1)
                pe.wait_ge(act_drained, u[("vg", l, 3)].drained)
                for tt in range(NT):
                    o = begin(("vgT", l, tt))
                    for t in range(4):
                        mm = nc.tensor.transpose(o[:, t * P:(t + 1) * P], ga(t)[:, tt * P:(tt + 1) * P], ident[:, :])
                    mm.then_inc(psum_full, 1)
                two("u", 1)
                for name in ("v", "k"):
                    dense((name, l), ("kv", l, 0), X_OP)
                one_ada()
                two("za", 0)
                two("za", 1)
                taken(pe, ("v", l))
                turn(("vT", l), R(b1_vT))
                for name in ("zg", "q"):
                    two(name, 0)
                    two(name, 1)
                pe.wait_ge(vn_ready, 4 * l + 4)
                taken(pe, ("wT", l))
                for g in range(4):
                    o = begin(("sp", l, g))
                    for c in range(NT):
                        vn = R(b1_vn + c * S)
                        mm = nc.tensor.matmul(o[:, c * P:(c + 1) * P], vn[:, g * P:(g + 1) * P],
                                              ws_t[:, g * P:(g + 1) * P], start=True, stop=True)
                    mm.then_inc(psum_full, 1)
                jobs = pl.swa[l]
                taken(pe, ("k", l))
                taken(pe, ("vT", l))
                taken(pe, ("q", l, 3))
                scores(jobs[0])
                scores(jobs[1])
                for s in range(9):
                    if s + 2 < 8:
                        scores(jobs[s + 2])
                    if s < 8:
                        two("g", s)
                        transposes(jobs[s])
                    if s >= 1:
                        values(jobs[s - 1])
                pe.wait_ge(yg_ready, 4 * l + 4)
                pe.wait_ge(ya_ready, 4 * l + 4)
                for t in range(KT):
                    dense(("ba", l, t), ("ba", l, t // 4), operand(q_hi, za_lo))
                    dense(("bg", l, t), ("bg", l, t // 4), operand(u_hi, zg_lo))
                pe.wait_ge(merged, 8 * l + 8)
                for t in range(KT):
                    dense(("out", l, t), ("out", l, t // 2), operand(hi_r, ga_lo))
                mean(l, ("out", l), range(KT))
                variance(l)

            def mixer_out_pe(i, op):
                wait_op(op)
                for t in range(KT):
                    dense(("mo", i, t), ("mo", i, t // 2), H_OP)
                mean(2 + 2 * i, ("mo", i), range(KT))
                variance(2 + 2 * i)

            def mlp_pe(i, op):
                wait_op(op)
                for half in range(2):
                    for t in range(16 * half, 16 * half + 16):
                        dense(("m1", i, t), ("m1", i, t // 2), H_OP)
                        if i == 0 and t % 2:
                            ada(24 + 8 * half + t // 2)
                    for c in range(4):
                        banks = [begin(("m2", i, half, t)) for t in (2 * c, 2 * c + 1)]
                        for kc in range(2):
                            if c == 0:
                                pe.wait_ge(hidden_ready, 32 * i + 16 * half + 8 * kc + 8)
                            op_ = [lambda k, r=r: tile(r, 8 * kc + k) for r in (hid_hi, hid_lo)]
                            for bank in banks:
                                multiply(bank, ("m2", i, half, c, kc), op_, first=kc == 0, last=kc == 1)
                        if i == 0 and half == 0:
                            ada(32 + 2 * c)
                            ada(33 + 2 * c)
                mean(3 + 2 * i, ("m2", i, 1), range(KT))
                variance(3 + 2 * i)

            wait_op(2)
            dense("lat", "lat", H_OP)
            dense("ik", "lat", H_OP)
            dense("misc", "misc", H_OP)
            taken(pe, "lat")
            turn("latT", A(e_tmp))
            for t in range(4):
                dense(("iq", t), ("iq", t // 2), H_OP)
                if t == 1:
                    taken(pe, "misc")
                    turn("miscT", A(e_tmp + S))
            pe.wait_ge(lat_done, 4)
            turn("ckvT", A(e_ckv))
            taken(pe, ("iq", 3))
            for qb in range(1, 4):
                for j in range(8):
                    hf = slice((j % 2) * HD, (j % 2) * HD + HD)
                    n = (qb + 1) * P
                    o = begin(("I", qb, j))
                    nc.tensor.matmul(o[:, 0:n], A(e_iq + (j // 2) * S)[hf, qb * P:(qb + 1) * P], A(e_ik)[hf, 0:n],
                                     start=True, stop=True).then_inc(psum_full, 1)
                    if qb < 3 and j % 4 == 3:
                        t = (qb - 1) * 2 + j // 4
                        dense(("dq", t), ("dq", t // 2), H_OP)
            dense("kc", ("kv2", "c"), H_OP)
            dense("vc", ("kv2", "c"), H_OP)
            for name, v_, k_, tmp in (("s", "vs", "ks", e_tmp), ("w", "vw", "kw", e_tmp + S)):
                dense(v_, ("kv2", name), H_OP)
                dense(k_, ("kv2", name), H_OP)
                taken(pe, v_)
                turn(v_ + "T", A(tmp))
            pe.wait_ge(e_in, 16 * N_E)
            pe.wait_ge(memsets, 6)
            for i in range(2):
                o = begin(f"biasc{i}")
                for b in range(2):
                    for n in range(NCMP):
                        d0 = (2 * i + b) * P - 16 * n - 31 + 511
                        c = (b * NCMP + n) * 8
                        mm = nc.tensor.matmul(o[:, c:c + 8], hot_full[0:33, d0:d0 + P], tab_full[0:33, 0:8],
                                              start=True, stop=True)
                mm.then_inc(psum_full, 1)
            turn("ukT", uk_raw)
            for t in range(4):
                dense(("nq", t), ("nq", t // 2), H_OP)
            taken(pe, "ukT")
            taken(pe, ("dq", 3))
            for h in range(8):
                hf = slice((h % 2) * HD, (h % 2) * HD + HD)
                o = begin(("ql", h))
                nc.tensor.matmul(o, ukT[hf, (h // 2) * P:(h // 2 + 1) * P], A(e_dq + (h // 2) * S)[hf, :],
                                 start=True, stop=True).then_inc(psum_full, 1)
            pe.wait_ge(rp_ready, 8)
            for kind in range(2):
                halves = [begin(("hid", kind, half)) for half in range(2)]
                for kc in range(2):
                    w = arrived(pe, ("w1", kind, kc))
                    for half in range(2):
                        for k in range(KT):
                            c = rp_at + kind * 992 + (8 * kc + k) * 62
                            mm = nc.tensor.matmul(halves[half][:, 0:62], w[:, k, half * P:(half + 1) * P],
                                                  mix[:, c:c + 62], start=kc == 0 and k == 0,
                                                  stop=kc == 1 and k == KT - 1)
                        if kc == 1:
                            mm.then_inc(psum_full, 1)
                    if kc == 0:
                        mm.then_inc(part_used, 1)
            taken(pe, ("hid", 1, 1))
            o = begin("kcT")
            for g in range(2):
                for half in range(2):
                    mm = nc.tensor.matmul(o[g * HD:(g + 1) * HD, 0:NCMP], w2kv[:, half * HD:(half + 1) * HD],
                                          hid[:, half * 62 + g * NCMP:half * 62 + (g + 1) * NCMP],
                                          start=half == 0, stop=half == 1)
            mm.then_inc(psum_full, 1)
            o = begin("vct")
            for g in range(2):
                for half in range(2):
                    mm = nc.tensor.matmul(o[0:NCMP, g * HD:(g + 1) * HD],
                                          hid[:, 124 + half * 62 + g * NCMP:124 + half * 62 + (g + 1) * NCMP],
                                          w2kv[:, 128 + half * HD:128 + (half + 1) * HD],
                                          start=half == 0, stop=half == 1)
            mm.then_inc(psum_full, 1)
            taken(pe, "vct")
            taken(pe, "ckvT")
            attention(pl.even)
            mixer_out_pe(0, 3)
            mlp_pe(0, 4)

            wait_op(5)
            for name in ("oq", "ok", "ov"):
                for t in range(KT):
                    dense((name, t), (name, t // 2), H_OP)
                    if name == "ov" and t:
                        taken(pe, ("ov", t - 1))
                        turn(("ovT", t - 1), A(o_tmp + ((t - 1) % 2) * S))
            taken(pe, ("ov", 7))
            turn(("ovT", 7), A(o_tmp + S))
            taken(pe, ("ovT", 7))
            attention(pl.odd)
            mixer_out_pe(1, 6)
            mlp_pe(1, 7)
            for k in range(KT):
                pe.wait_ge(x_ready, 8 + k + 1)
            for tt in range(NT):
                for c in range(2):
                    o = begin(("y", tt, c))
                    for k in range(4):
                        mm = nc.tensor.transpose(o[:, k * P:(k + 1) * P], X(4 * c + k)[:, tt * P:(tt + 1) * P], ident[:, :])
                    mm.then_inc(psum_full, 1)
            assert made[0] == len(pl.order) and part[0] == len(pl.parts)

        def load_rows(eng, l):
            for dst, src in ((lng_row, bcast(a["gmlp_ln_g"], 512, l * 512)),
                             (lnb_row, bcast(a["gmlp_ln_b"], 512, l * 512)),
                             (bs_row, bcast(a["b_spatial"], 512, l * 512))):
                eng.dma_start(dst, src).then_inc(rows_in, 16)
            eng.dma_start(ws_raw.rearrange("p (g s) -> p g s", g=4), a["w_spatial"][l].rearrange("g t s -> t g s"))\
                .then_inc(rows_in, 16)

        @block.scalar
        def _(act):

            def sqrt(out_, in_, bias):
                nc.scalar.activation(out_, in_, ACT.Sqrt, bias=bias).then_inc(std_ready, 1)

            def drain(key, dst, func=ACT.Copy, bias=0.0, scale=1.0, m=slice(0, P), n=slice(0, S)):
                o = full(act, key)
                nc.scalar.activation(dst, o[m, n], func, bias=bias, scale=scale).then_inc(act_drained, 1)

            fed = [0]

            def feed(upto, limit):
                while fed[0] < min(upto, limit, len(pl.parts)):
                    q = fed[0]
                    name, src, _, _ = pl.parts[q]
                    view = arrived(act, name)
                    if q >= SPLITS:
                        freed(act, pl.parts[q - SPLITS][3])
                    nc.scalar.activation(part_view(w_hi, q), part_source(view, src), ACT.Copy).then_inc(w_hi_ready, 1)
                    fed[0] += 1

            limit = [pl.phase[0]]

            def pace(key):
                feed(pl.part_of[key] + 1 + SPLITS, limit[0])

            def dense(key, dst, func=ACT.Copy, bias=0.0, scale=1.0):
                pace(key)
                drain(key, dst, func, bias, scale)

            def round_tiles(src, tiles=range(KT), ready=None):
                for t in tiles:
                    if ready:
                        ready(t)
                    nc.scalar.activation(tile(hi_r, t), src(t), ACT.Copy).then_inc(hi_ready, 1)

            act.dma_start(ident[:, :], a["ident"]).then_inc(x_in, 16)
            for tt in range(NT):
                act.dma_start(lo32[:, tt * D:(tt + 1) * D], a["x"][0, tt * P:(tt + 1) * P, :]).then_inc(x_in, 16)
            for dst, src in ((tril[:, :], a["tril"]), (sinks[:, :], bcast(a["attn_sinks"], 2 * HEADS)),
                             (alibi, a["alibi"])):
                act.dma_start(dst, src).then_inc(const_in, 16)
            load_rows(act, 0)
            for k in range(0, KT, 2):
                drain(("xT", k), X(k))
                if k == 0:
                    feed(1, limit[0])
            round_tiles(X, ready=lambda t: taken(act, ("xT", t)))
            feed(SPLITS, limit[0])
            act.wait_ge(memsets, 4)

            bias_sb = R(b1_q, TW)[0:16, :]
            drain(("bias", 0), bias_sb[:, 0:512], scale=-1.0, m=slice(0, 16))
            drain(("bias", 1), bias_sb[:, 512:TW], scale=-1.0, m=slice(0, 16), n=slice(0, TW - 512))
            taken(act, ("bias", 1))
            act.dma_start(bias_rows, bias_sb.unsqueeze(1).to_broadcast([16, P, TW])).then_inc(bias_out, 16)
            taken(act, ("vec", 2))
            c0 = vec_b(0, "c")
            nc.scalar.activation(cact[:, :], cols[:, c0:c0 + KT], ACT.Silu).then_inc(c_ready, 1)

            def load_table(ti):
                h = tables[ti]
                src = bass.AP(tensor=bias_rows.tensor, offset=bias_rows.offset + h * P * TW + P - 1,
                              ap=[[TW - 1, P], [1, S]])
                act.dma_start(tbuf(ti), src).then_inc(t_in[ti % 3], 16)

            def exps(j):
                z = zbuf(j)
                if j is pl.even[0]:
                    taken(act, "miscT")
                    nc.scalar.activation(gates, gates, ACT.Sigmoid).then_inc(gates_ready, 1)
                if j.kind == "cmp":
                    act.wait_ge(m_ready, j.mr)
                    nc.scalar.activation(z[:, 0:4 * NCMP], z[:, 0:4 * NCMP], ACT.Exp, scale=-1.0).then_inc(p_ready, 1)
                    return
                if j.kind == "swa":
                    act.wait_ge(m_ready, j.mr)
                    spans = [(qb, (0, 128, 384, 640)[qb], 256 if qb else 128) for qb in range(4)]
                else:
                    spans = [(qb, ZOFF[qb], (qb + 1) * P) for qb in ORDER]
                for i, (qb, c, n) in enumerate(spans):
                    if j.kind != "swa":
                        act.wait_ge(z_ready, j.z0 + i + 1)
                    nc.scalar.activation(z[:, c:c + n], z[:, c:c + n], ACT.Exp, bias=stat4(negm, j, qb), scale=-1.0,
                                         accum_out=stat4(sums, j, qb)).then_inc(p_ready, 1)
                if j.kind == "swa":
                    h = HEADS * j.l + j.h
                    nc.scalar.activation(stat4(esink, j), stat4(negm, j), ACT.Exp, bias=sinks[:, h:h + 1])\
                        .then_inc(sink_ready, 1)
                if j.kind not in ("swa", "cmp") and j.t_last and j.ti + 3 < len(tables):
                    load_table(j.ti + 3)

            def drain_t(j):
                if not j.has_pt:
                    return
                pt = ptbuf(j)
                if j.pt >= 2:
                    act.wait_ge(pv_done, j.pt - 1)
                if j.kind == "cmp":
                    drain(("T", j.J, 0), pt[0:NCMP, 0:512], m=slice(0, NCMP))
                else:
                    drain(("T", j.J, 0), pt[:, 0:512])
                    if j.kind != "swa":
                        drain(("T", j.J, 2), pt[:, 896:1280], n=slice(0, 384))

            def squares(n):
                for t in range(KT):
                    act.wait_ge(ln_centered, 8 * n + t + 1)
                    nc.scalar.activation(H(t), X(t), ACT.Square).then_inc(ln_squared, 1)

            def deviation(n):
                act.wait_ge(stat_full, 2 * n + 2)
                sqrt(rstd, psum[:, 7, :], eps[:, :])

            def affine(n, g, b, ready):
                for t in range(KT):
                    act.wait_ge(ln_scaled, 8 * n + t + 1)
                    nc.scalar.activation(X(t), X(t), ACT.Identity, bias=cols[:, b + t:b + t + 1],
                                         scale=cols[:, g + t:g + t + 1]).then_inc(x_ready, 1)
                    if ready:
                        act.wait_ge(x_ready, 8 * 0 + t + 1)
                        nc.scalar.activation(tile(hi_r, t), X(t), ACT.Copy).then_inc(hi_ready, 1)

            def modulated(n):
                act.wait_ge(ccols_ready, 4 * n)
                c = 32 * (n - 1)
                for t in range(KT):
                    act.wait_ge(ln_scaled, 8 * n + t + 1)
                    nc.scalar.activation(H(t), X(t), ACT.Identity, bias=ccols[:, c + 8 + t:c + 9 + t],
                                         scale=ccols[:, c + t:c + t + 1]).then_inc(h_ready, 1)
                    act.wait_ge(h_ready, 8 * (n - 1) + t + 1)
                    nc.scalar.activation(tile(hi_r, t), H(t), ACT.Copy).then_inc(hi_ready, 1)

            def block_2_loads():
                for dst, src in ((kvnorm, bcast(a["dsa_kv_norm_2"], P)), (future, a["future"])):
                    act.dma_start(dst, src).then_inc(mask_in, 16)
                e_loads = [(hot_full[0:33, :], a["hot"]), (tab_full[0:32, :], a["rel_bias_2"]),
                           (uk_raw, a["dsa_w_uk_2"][0].rearrange("r h d -> r (h d)"))]
                for i, name in enumerate(("nsa_w2_k_2", "nsa_w2_v_2")):
                    e_loads.append((w2kv[:, 128 * i:128 * i + 128].rearrange("p (k n) -> p k n", k=2),
                                    a[name][0].rearrange("(k p) n -> p k n", p=P)))
                for dst, src in e_loads:
                    act.dma_start(dst, src).then_inc(e_in, 16)
                with nc.allow_non_contiguous_dma("positional embeddings of 16 KB"):
                    for i, name in enumerate(("nsa_pe_k_2", "nsa_pe_v_2")):
                        src = bass.AP(tensor=a[name].tensor, offset=a[name].offset, ap=[[1, P], [P, 16]])
                        act.dma_start(peT[:, 16 * i:16 * i + 16], src).then_inc(e_in, 16)
                act.wait_ge(bias_out, 16)
                for ti in range(3):
                    load_table(ti)

            for l in range(DEPTH):
                def biased_tile(name, t, dst, func):
                    c = vec_a(l, name, t)
                    dense((name, l, t) if name not in ("k", "v") else (name, l), dst, func, bias=cols[:, c:c + 1])

                for t in range(4):
                    biased_tile("vg", t, ga(t), ACT.Gelu)
                for t in range(4):
                    biased_tile("u", t, ug[:, t * S:(t + 1) * S], ACT.Gelu)
                biased_tile("v", 0, R(b1_vT), ACT.Identity)
                biased_tile("k", 0, R(b1_k), ACT.Identity)
                act.wait_ge(var_ready, l + 1)
                sqrt(stats[:, 32:36], stats[:, 32:36], eps[:, :])
                for t in range(4):
                    biased_tile("za", t, za[:, t * S:(t + 1) * S], ACT.Silu)
                for t in range(4):
                    biased_tile("zg", t, R(b1_zg + t * S), ACT.Silu)
                for t in range(4):
                    pace(("q", l, t))
                jobs = pl.swa[l]
                exps(jobs[0])
                exps(jobs[1])
                for s in range(8):
                    for t in range(2 * s, 2 * s + 2):
                        biased_tile("g", t, ga(t), ACT.Identity)
                    if s + 2 < 8:
                        exps(jobs[s + 2])
                    drain_t(jobs[s])
                act.wait_ge(act_drained, u[("T", jobs[7].J, 0)].drained)
                for i in range(4):
                    for v in (R(b1_ga + 2 * i * S, 2 * S), lo32[:, 2 * i * S:2 * (i + 1) * S]):
                        nc.scalar.activation(v, v, ACT.Sigmoid).then_inc(sig_ready, 1)
                if l + 1 < DEPTH:
                    taken(act, ("sp", l, 3))
                    load_rows(act, l + 1)
                for t in range(KT):
                    pace(("ba", l, t))
                    pace(("bg", l, t))
                for t in range(KT):
                    pace(("out", l, t))
                squares(l)
                if l == 1:
                    block_2_loads()
                deviation(l)
                if l == 0:
                    affine(0, vec_a(0, "ln_g"), vec_a(0, "ln_b"), True)
                else:
                    modulated(1)

            dense("lat", A(e_tmp))
            dense("ik", A(e_ik))
            dense("misc", A(e_tmp + S))
            for t in range(4):
                dense(("iq", t), A(e_iq + t * S))
            act.wait_ge(var_ready, DEPTH + 1)
            sqrt(stats[:, 0:4], stats[:, 0:4], eps[:, :])
            i = 0
            for qb in range(1, 4):
                n = (qb + 1) * P
                for j in range(8):
                    if i >= 2:
                        act.wait_ge(isc_used, i - 1)
                    c = relu_at + (i % 2) * S
                    drain(("I", qb, j), mix[:, c:c + n], ACT.Relu, n=slice(0, n))
                    if qb < 3 and j % 4 == 3:
                        t = (qb - 1) * 2 + j // 4
                        dense(("dq", t), A(e_dq + t * S), scale=-HD ** -0.5)
                    i += 1
            dense("kc", A(e_kc))
            dense("vc", A(e_vc))
            act.wait_ge(act_drained, u["vc"].drained)
            for kind, at_ in enumerate((e_kc, e_vc)):
                for g in range(2):
                    dst = tile(mix, 2 * kind + g)
                    src = A(at_)[g * HD:(g + 1) * HD, :]
                    act.dma_start(dst[0:HD, :], src).then_inc(r_in, 16)
                    act.dma_start(dst[HD:P, 0:S - 1], src[:, 1:S]).then_inc(r_in, 16)
            for v_, k_, tmp, at_v, at_k in (("vs", "ks", e_tmp, e_vs, e_ks), ("vw", "kw", e_tmp + S, e_vw, e_kw)):
                dense(v_, A(tmp))
                dense(k_, A(at_k))
                drain(v_ + "T", A(at_v))
            for i in range(2):
                o = full(act, f"biasc{i}")
                nc.scalar.activation(
                    biasc[:, i * 2 * 248:(i + 1) * 2 * 248].rearrange("p (b h n) -> p b h n", b=2, h=8),
                    o[:, 0:496].rearrange("p (b n h) -> p b h n", b=2, h=8), ACT.Copy, scale=-1.0)\
                    .then_inc(act_drained, 1)
            act.wait_ge(future_used, 3)
            for t in range(4):
                dense(("nq", t), A(e_q + t * S), scale=-HD ** -0.5)
            for h in range(8):
                drain(("ql", h), A(e_ql + h * S))
            act.wait_ge(psum_full, u[("ql", 7)].full)
            act.dma_start(w_uv, a["dsa_w_uv_2"][0].rearrange("r h d -> r (h d)")).then_inc(uv_in, 16)
            for kind in range(2):
                for half in range(2):
                    c = (2 * kind + half) * 62
                    drain(("hid", kind, half), hid[:, c:c + 62], ACT.Gelu_apprx_tanh, n=slice(0, 62))
            drain("kcT", kcT, n=slice(0, NCMP))
            drain("vct", vct[0:NCMP, :], m=slice(0, NCMP), n=slice(0, P))

            def attention(jobs):
                for j in jobs[:AHEAD]:
                    exps(j)
                for s in range(len(jobs) + 2):
                    if s + AHEAD < len(jobs):
                        exps(jobs[s + AHEAD])
                    if s < len(jobs):
                        drain_t(jobs[s])
                    if 0 <= s - 1 < len(jobs) and jobs[s - 1].kind == "diff" and jobs[s - 1].m:
                        h = jobs[s - 1].h
                        act.wait_ge(o_drained, jobs[s - 1].o + 1)
                        if h >= 2:
                            act.wait_ge(psum_full, u[("ms", h - 2)].full)
                        nc.scalar.activation(A(o_sq + (h % 2) * S), M(h), ACT.Square).then_inc(sq_ready, 1)
                    if 0 <= s - 2 < len(jobs) and jobs[s - 2].kind == "dsa":
                        h = jobs[s - 2].h
                        m = slice((h % 2) * HD, (h % 2) * HD + HD)
                        drain(("uv", h), M(4 + h // 2)[m, :], m=m)

            attention(pl.even)

            def mixed(i, key, ready):
                act.wait_ge(psum_full, u[key].full)
                limit[0] = pl.phase[1] if i == 0 else len(pl.parts)
                feed(pl.phase[i] + SPLITS, limit[0])
                round_tiles(M, ready=ready)
                for t in range(KT):
                    pace(("mo", i, t))
                squares(2 + 2 * i)
                deviation(2 + 2 * i)
                modulated(2 + 2 * i)

            def mlp_act(i):
                for half in range(2):
                    for t in range(16 * half, 16 * half + 16):
                        pace(("m1", i, t))
                        if t >= 8:
                            act.wait_ge(hidden_ready, 32 * i + t - 7)
                        drain(("m1", i, t), M(t % 8), ACT.Relu)
                    for t in range(0, 8, 2):
                        last = pl.part_of[("m2", i, half, t + 1)]
                        for q in range(last - 3, last + 1):
                            feed(q + 1 + SPLITS, limit[0])
                squares(3 + 2 * i)
                deviation(3 + 2 * i)

            def even_ready(t):
                if t < 4:
                    act.wait_ge(o_drained, pl.even[6 * t + 5].o + 1)
                elif t % 2 == 0:
                    taken(act, ("uv", 7))

            mixed(0, ("uv", 7), even_ready)
            mlp_act(0)
            modulated(3)
            for i, at_ in ((0, o_q), (1, o_k), (2, o_v)):
                name = ("oq", "ok", "ov")[i]
                for t in range(KT):
                    if name == "ov" and t >= 2:
                        act.wait_ge(psum_full, u[("ovT", t - 2)].full)
                    dst = A(at_ + t * S) if name != "ov" else A(o_tmp + (t % 2) * S)
                    dense((name, t), dst, scale=-HD ** -0.5 if i == 0 else 1.0)
            act.wait_ge(lam_dots, 2)
            nc.scalar.activation(lamc[:, 2:4], lamc[:, 0:2], ACT.Exp).then_inc(lam_ready, 1)
            attention(pl.odd)
            for h in range(HEADS):
                taken(act, ("ms", h))
                sqrt(H(h), H(h), eps[:, :])
            mixed(1, ("ms", 7), lambda t: act.wait_ge(o_normed, t + 1))
            mlp_act(1)
            affine(5, vec_b(3, "ln_g"), vec_b(3, "ln_b"), False)
            for tt in range(NT):
                drain(("y", tt, 1), hi32[:, tt * D + S:(tt + 1) * D])

        @block.vector
        def _(dve):
            own = Steps(dve, dve_own)
            v = nc.vector
            stds = [0]

            def drain(key, dst, m=slice(0, P), n=slice(0, S)):
                o = full(dve, key)
                v.tensor_copy(dst, o[m, n]).then_inc(dve_drained, 1)

            def ada_sum(n):
                w = arrived(dve, ("ada", n))
                if n >= 2:
                    dve.wait_ge(psum_full, u[("ada", n - 2)].full)
                acc = R(acc_at + (n % 2) * 256, 256)
                own.step(v.tensor_scalar(acc, w[:, 0, :], cact[:, 0:1], None, ALU.mult))
                for k in range(1, KT):
                    own.settle()
                    ins = v.scalar_tensor_tensor(acc, w[:, k, :], cact[:, k:k + 1], acc, ALU.mult, ALU.add)
                    if k < KT - 1:
                        own.step(ins)
                    else:
                        ins.then_inc(acc_ready, 1)

            def ada_drain(n):
                o = full(dve, ("ada", n))
                b = N_A + 2 * n
                v.tensor_tensor(adac[:, 2 * n:2 * n + 2], o[:, 0:2], cols[:, b:b + 2], ALU.add).then_inc(dve_drained, 1)

            def modulations(i):
                taken(dve, ("ada", 24 * i + 23))
                for c in (ADA["sc1"], ADA["sc2"]):
                    one = adac[:, 48 * i + c:48 * i + c + 16]
                    v.tensor_scalar(one, one, 1.0, None, ALU.add).then_inc(ada_ready, 1)

            fed = [0]
            limit = [pl.phase[0]]

            def feed(upto):
                while fed[0] < min(upto, limit[0], len(pl.parts)):
                    q = fed[0]
                    name, src, _, _ = pl.parts[q]
                    i, _ = arrival[name]
                    view = slot_view(i, pieces(name)[0])
                    dve.wait_ge(w_hi_ready, q + 1)
                    v.tensor_tensor(part_view(w_lo, q), part_source(view, src), part_view(w_hi, q).bitcast(F32),
                                    ALU.subtract).then_inc(w_lo_ready, 1)
                    fed[0] += 1

            def pace(key):
                feed(pl.part_of[key] + 1 + SPLITS)

            def rest_tiles(i, src, dst, tiles=range(KT)):
                for t in tiles:
                    dve.wait_ge(hi_ready, 8 * i + t + 1)
                    v.tensor_tensor(tile(dst, t), src(t), HI(t), ALU.subtract).then_inc(op_ready, 1)

            def both_parts(src, hi, lo):
                own.settle()
                own.step(v.tensor_copy(hi, src))
                own.settle()
                return v.tensor_tensor(lo, src, hi.bitcast(F32), ALU.subtract)

            def biased(j):
                z = zbuf(j)
                before = pl.jobs[j.J - 4] if j.kind == "swa" and j.J >= 4 else j.before
                if before:
                    dve.wait_ge(psum_full, u[("T", before.J, before.ptn - 1)].full)
                if j.kind == "cmp":
                    o = full(dve, ("S", j.J, 0))[:, 0:4 * NCMP].rearrange("p (b n) -> p b n", b=4)
                    zz = z[:, 0:4 * NCMP].rearrange("p (b n) -> p b n", b=4)
                    bias = biasc.rearrange("p (b h n) -> p b h n", b=4, h=8)[:, :, j.h, :]
                    v.tensor_tensor(zz, o, bias, ALU.add).then_inc(z_ready, 1)
                    dve.wait_ge(z_ready, j.z)
                    own.step(v.tensor_reduce(stat4(negm, j), zz, AX_X, ALU.min))
                    own.settle()
                    own.step(v.tensor_scalar(stat4(negm, j), stat4(negm, j), 0.1 * MASKED, None, ALU.min))
                    own.settle()
                    v.tensor_tensor(zz, zz, stat4(negm, j).unsqueeze(2).to_broadcast([P, 4, NCMP]),
                                    ALU.subtract).then_inc(m_ready, 1)
                    return
                if j.kind == "swa":
                    for i in range(2):
                        o = full(dve, ("S", j.J, i))
                        c = 0
                        for qb in (2 * i, 2 * i + 1):
                            n = 256 if qb else 128
                            at = (0, 128, 384, 640)[qb]
                            v.tensor_tensor_reduce(
                                out=z[:, at:at + n], in0=o[:, c:c + n],
                                in1=alibi[:, j.h * 256 + 256 - n:(j.h + 1) * 256], scale=1.0, scalar=HUGE,
                                op0=ALU.add, op1=ALU.min, accum_out=stat4(negm, j, qb)).then_inc(z_ready, 1)
                            c += n
                    dve.wait_ge(z_ready, j.z)
                    h = HEADS * j.l + j.h
                    v.tensor_scalar(stat4(negm, j), stat4(negm, j), nsinks[:, h:h + 1], None, ALU.min)\
                        .then_inc(m_ready, 1)
                    return
                dve.wait_ge(t_in[j.ti % 3], 16 * (j.ti // 3 + 1))
                table = tbuf(j.ti)
                for i, qbs in enumerate(((0, 2), (1,), (3,))):
                    o = full(dve, ("S", j.J, i))
                    c = 0
                    for qb in qbs:
                        n, at = (qb + 1) * P, ZOFF[qb]
                        zz, bias = z[:, at:at + n], table[:, S - n:S]
                        first, second = o[:, c:c + n], bias
                        if j.kind == "dsa" and qb:
                            own.step(v.tensor_tensor(zz, o[:, c:c + n], bias, ALU.add))
                            own.settle()
                            first, second = zz, selm(qb)
                        v.tensor_tensor_reduce(out=zz, in0=first, in1=second, scale=1.0, scalar=HUGE,
                                               op0=ALU.add, op1=ALU.min, accum_out=stat4(negm, j, qb))\
                            .then_inc(z_ready, 1)
                        c += n

            def normalise(j):
                dve.wait_ge(p_ready, j.p)
                z, den, r = zbuf(j), stat4(sums, j), stat4(recips, j)
                cmp = z[:, 0:4 * NCMP].rearrange("p (b n) -> p b n", b=4)
                if j.kind == "swa":
                    dve.wait_ge(sink_ready, HEADS * j.l + pl.swa[j.l].index(j) + 1)
                    own.step(v.tensor_tensor(den, den, stat4(esink, j), ALU.add))
                else:
                    if j.kind == "cmp":
                        own.step(v.tensor_reduce(den, cmp, AX_X, ALU.add))
                        own.settle()
                    own.step(v.tensor_scalar(den, den, 1e-30, None, ALU.max))
                own.settle()
                own.step(v.reciprocal(r, den))
                own.settle()
                if j.kind == "diff" and j.m:
                    own.step(v.tensor_scalar(r, r, small[:, 6:7], None, ALU.mult))
                    own.settle()
                elif j.kind in ("cmp", "sel", "win"):
                    i = ("cmp", "sel", "win").index(j.kind)
                    dve.wait_ge(gates_ready, 1)
                    g = gates.rearrange("p (b f) -> p b f", b=4)[:, :, 3 * j.h + i]
                    own.step(v.tensor_tensor(r, r, g, ALU.mult))
                    own.settle()
                if j.kind == "cmp":
                    v.tensor_tensor(cmp, cmp, r.unsqueeze(2).to_broadcast([P, 4, NCMP]), ALU.mult)\
                        .then_inc(s_ready, 1)
                    return
                if j.kind == "swa":
                    spans = [(qb, (0, 128, 384, 640)[qb], 256 if qb else 128) for qb in range(4)]
                else:
                    spans = [(qb, ZOFF[qb], (qb + 1) * P) for qb in range(4)]
                if j.kind == "diff" and j.m:
                    dve.wait_ge(s_ready, j.s0)
                for qb, c, n in spans:
                    zz, rr = z[:, c:c + n], stat4(recips, j, qb)
                    if j.kind == "diff" and j.m:
                        z0 = zbuf(pl.jobs[j.J - 1])[:, c:c + n]
                        v.scalar_tensor_tensor(zz, zz, rr, z0, ALU.mult, ALU.add).then_inc(s_ready, 1)
                    else:
                        v.tensor_scalar(zz, zz, rr, None, ALU.mult).then_inc(s_ready, 1)

            def drain_t(j):
                if not j.has_pt or j.kind == "cmp":
                    return
                if j.pt >= 2:
                    dve.wait_ge(pv_done, j.pt - 1)
                drain(("T", j.J, 1), ptbuf(j)[:, 512:896], n=slice(0, 384))

            def outputs(j):
                if not (j.has_pt and j.last_o):
                    return
                dve.wait_ge(pv_done, j.pv)
                bank = psum[:, 6 + j.o % 2, :]
                if j.kind == "swa":
                    t = j.h % 4
                    zt = za[:, t * S:(t + 1) * S]
                    v.tensor_tensor(zt, zt, bank, ALU.mult).then_inc(o_drained, 1)
                    dve.wait_ge(o_drained, j.o + 1)
                    both_parts(zt, tile(q_hi, t), tile(za_lo, t)).then_inc(ya_ready, 1)
                elif j.kind == "win":
                    v.tensor_copy(M(j.h % 4), bank).then_inc(o_drained, 1)
                elif j.kind == "dsa":
                    if j.h >= 2:
                        dve.wait_ge(psum_full, u[("uv", j.h - 2)].full)
                    v.tensor_copy(A(e_olat + (j.h % 2) * S), bank).then_inc(o_drained, 1)
                else:
                    v.tensor_copy(M(j.h), bank).then_inc(o_drained, 1)

            def head_norm(h):
                stds[0] += 1
                dve.wait_ge(std_ready, stds[0])
                own.step(v.reciprocal(H(h), H(h)))
                own.settle()
                v.scalar_tensor_tensor(M(h), M(h), small[:, 7:8], H(h), ALU.mult, ALU.mult).then_inc(o_normed, 1)

            def attention(jobs):
                biased(jobs[0])
                for i in range(1, AHEAD):
                    biased(jobs[i])
                    normalise(jobs[i - 1])
                for s in range(len(jobs) + 2):
                    if s + AHEAD < len(jobs):
                        biased(jobs[s + AHEAD])
                    if s + AHEAD - 1 < len(jobs):
                        normalise(jobs[s + AHEAD - 1])
                    if s < len(jobs):
                        drain_t(jobs[s])
                    if 0 <= s - 1 < len(jobs):
                        outputs(jobs[s - 1])
                    if 0 <= s - 2 < len(jobs) and jobs[s - 2].kind == "diff" and jobs[s - 2].m:
                        drain(("ms", jobs[s - 2].h), H(jobs[s - 2].h))

            def layer_norm(n):
                dve.wait_ge(stat_full, 2 * n + 1)
                for t in range(KT):
                    v.tensor_tensor(X(t), X(t), psum[:, 6, :], ALU.subtract).then_inc(ln_centered, 1)
                stds[0] += 1
                dve.wait_ge(std_ready, stds[0])
                own.step(v.reciprocal(rstd, rstd))
                own.settle()
                for t in range(KT):
                    dve.wait_ge(ln_centered, 8 * n + t + 1)
                    v.tensor_tensor(X(t), X(t), rstd, ALU.mult).then_inc(ln_scaled, 1)

            for k in range(1, KT, 2):
                drain(("xT", k), X(k))
            feed(1)
            rest_tiles(0, X, x_lo)
            feed(SPLITS)
            for i, (c, n) in enumerate(((0, N_A), (N_A, N_B), (N_A + N_B, N_C))):
                drain(("vec", i), cols[:, c:c + n], n=slice(0, n))
            dve.wait_ge(const_in, 48)
            v.tensor_scalar(nsinks[:, :], sinks[:, :], -1.0, None, ALU.mult).then_inc(nsink_ready, 1)
            dve.wait_ge(nsink_ready, 1)
            dve.wait_ge(c_ready, 1)

            for l in range(DEPTH):
                next_ada = [ADAS * l]

                def one_sum():
                    if next_ada[0] < ADAS * (l + 1):
                        ada_sum(next_ada[0])
                        next_ada[0] += 1
                        return next_ada[0] - 1
                    return None

                def two(name, c, act=None):
                    n = one_sum()
                    for t in (2 * c, 2 * c + 1):
                        pace((name, l, t))
                        if act:
                            act(t)
                    if n is not None:
                        ada_drain(n)

                two("vg", 0)
                two("vg", 1)
                two("u", 0)
                dve.wait_ge(rows_in, 64 * (l + 1))
                if l:
                    dve.wait_ge(psum_full, u[("wT", l - 1)].full)
                ws3 = ws_raw.rearrange("p (g s) -> p g s", g=4)
                v.tensor_tensor(ws3, ws3, tril[:, :].unsqueeze(1).to_broadcast([P, 4, P]), ALU.mult)\
                    .then_inc(ws_masked, 1)
                drain(("wT", l), ws_t)
                for tt in range(NT):
                    drain(("vgT", l, tt), R(b1_vn + tt * S))
                bn = stats[:, 0:24].rearrange("p (t s) -> p t s", t=4)
                mv = stats[:, 24:32].rearrange("p (t s) -> p t s", t=4)
                rs = stats[:, 32:36]
                taken(dve, ("vgT", l, 3))
                for tt in range(NT):
                    own.step(v.bn_stats(bn[:, tt, :], R(b1_vn + tt * S)))
                own.settle()
                for tt in range(NT):
                    own.step(v.bn_aggr(mv[:, tt, :], bn[:, tt, :]))
                own.settle()
                v.tensor_copy(rs, mv[:, :, 1]).then_inc(var_ready, 1)
                two("u", 1)
                n = one_sum()
                for name in ("v", "k"):
                    pace((name, l))
                ada_drain(n)
                stds[0] += 1
                dve.wait_ge(std_ready, stds[0])
                own.step(v.reciprocal(rs, rs))
                own.settle()
                for tt in range(NT):
                    v.tensor_scalar(R(b1_vn + tt * S), R(b1_vn + tt * S), mv[:, tt, 0:1], rs[:, tt:tt + 1],
                                    ALU.subtract, ALU.mult).then_inc(vn_norm, 1)
                two("za", 0)
                two("za", 1)
                drain(("vT", l), R(b1_v))
                two("zg", 0)
                two("zg", 1)

                def query(t):
                    if l == 0 and t == 0:
                        dve.wait_ge(bias_out, 16)
                    c = vec_a(l, "q", t)
                    o = full(dve, ("q", l, t))
                    v.tensor_scalar(R(b1_q + t * S), o, cols[:, c:c + 1], -HD ** -0.5, ALU.add, ALU.mult)\
                        .then_inc(dve_drained, 1)

                two("q", 0, query)
                two("q", 1, query)
                for g in range(4):
                    o = full(dve, ("sp", l, g))
                    tmp = R(b1_z + (g % 2) * S)
                    bs = bs_row[:, g * P:(g + 1) * P].unsqueeze(1).to_broadcast([P, 4, P])
                    v.tensor_tensor(tmp.rearrange("p (b t) -> p b t", b=4), o.rearrange("p (b t) -> p b t", b=4),
                                    bs, ALU.add).then_inc(dve_drained, 1)
                    dve.wait_ge(dve_drained, u[("sp", l, g)].drained)
                    dve.wait_ge(uz_ready, 4 * l + g + 1)
                    zg = R(b1_zg + g * S)
                    own.step(v.tensor_tensor(zg, zg, tmp, ALU.mult))
                    both_parts(zg, tile(u_hi, g), tile(zg_lo, g)).then_inc(yg_ready, 1)
                jobs = pl.swa[l]
                biased(jobs[0])
                biased(jobs[1])
                normalise(jobs[0])
                for s in range(9):
                    if s + 2 < 8:
                        biased(jobs[s + 2])
                    if s + 1 < 8:
                        normalise(jobs[s + 1])
                    if s < 8:
                        two("g", s)
                        drain_t(jobs[s])
                    if s >= 1:
                        outputs(jobs[s - 1])
                for t in range(KT):
                    dve.wait_ge(sig_ready, 8 * l + 2 * (t // 2) + 2)
                    pace(("ba", l, t))
                    o = full(dve, ("ba", l, t))
                    v.tensor_tensor(ga(t), ga(t), o, ALU.mult).then_inc(dve_drained, 1)
                    pace(("bg", l, t))
                    o = full(dve, ("bg", l, t))
                    v.tensor_tensor(ga(8 + t), ga(8 + t), o, ALU.mult).then_inc(dve_drained, 1)
                    taken(dve, ("bg", l, t))
                    own.step(v.tensor_tensor(ga(t), ga(t), ga(8 + t), ALU.add))
                    dve.wait_ge(res_scaled, 8 * l + t + 1)
                    both_parts(ga(t), tile(hi_r, t), tile(ga_lo, t)).then_inc(merged, 1)
                if l == 1:
                    modulations(0)
                for t in range(KT):
                    pace(("out", l, t))
                    o = full(dve, ("out", l, t))
                    v.tensor_tensor(X(t), X(t), o, ALU.add).then_inc(dve_drained, 1)
                layer_norm(l)
                if l == 0:
                    for t in range(KT):
                        dve.wait_ge(hi_ready, 8 + t + 1)
                        v.tensor_tensor(tile(x_lo, t), X(t), HI(t), ALU.subtract).then_inc(op_ready, 1)

            rest_tiles(2, H, lo_r)
            for key in ("lat", "ik", "misc"):
                pace(key)
            drain("latT", A(e_ckv))
            taken(dve, "latT")
            dve.wait_ge(mask_in, 32)
            for tt in range(NT):
                own.step(v.tensor_tensor_reduce(out=R(PT_AT + 1200, P), in0=A(e_ckv + tt * P, P),
                                                in1=A(e_ckv + tt * P, P), scale=1.0, scalar=0.0, op0=ALU.mult,
                                                op1=ALU.add, accum_out=stats[:, tt:tt + 1]))
                own.settle()
            v.tensor_scalar(stats[:, 0:4], stats[:, 0:4], 1.0 / P, None, ALU.mult).then_inc(var_ready, 1)
            pace(("iq", 0))
            pace(("iq", 1))
            o = full(dve, "miscT").rearrange("p (b f) -> p b f", b=4)
            v.tensor_scalar(iw.rearrange("p (b f) -> p b f", b=4), o[:, :, 120:128], 8 ** -0.5 * 64 ** -0.5, None,
                            ALU.mult).then_inc(iw_ready, 1)
            v.tensor_copy(gates.rearrange("p (b f) -> p b f", b=4), o[:, :, 0:24]).then_inc(dve_drained, 1)
            pace(("iq", 2))
            pace(("iq", 3))
            stds[0] += 1
            dve.wait_ge(std_ready, stds[0])
            own.step(v.reciprocal(stats[:, 0:4], stats[:, 0:4]))
            own.settle()
            for tt in range(NT):
                c = A(e_ckv + tt * P, P)
                v.scalar_tensor_tensor(c, c, stats[:, tt:tt + 1], kvnorm, ALU.mult, ALU.mult).then_inc(lat_done, 1)
            drain("ckvT", A(e_ckvT))
            taken(dve, "ckvT")
            i = 0
            for qb in range(1, 4):
                n = (qb + 1) * P
                for j in range(8):
                    dve.wait_ge(act_drained, u[("I", qb, j)].drained)
                    c = relu_at + (i % 2) * S
                    relu = mix[:, c:c + n]
                    w = iw[:, 8 * qb + j:8 * qb + j + 1]
                    if j == 0:
                        v.tensor_scalar(work(qb), relu, w, None, ALU.mult).then_inc(isc_used, 1)
                    else:
                        dve.wait_ge(isc_used, i)
                        v.scalar_tensor_tensor(work(qb), relu, w, work(qb), ALU.mult, ALU.add).then_inc(isc_used, 1)
                    i += 1
                    if qb < 3 and j % 4 == 3:
                        pace(("dq", (qb - 1) * 2 + j // 4))
                dve.wait_ge(isc_used, i)
                diag = work(qb)[:, n - P:n]
                v.tensor_tensor(diag, diag, future, ALU.add).then_inc(future_used, 1)
            dve.wait_ge(future_used, 3)
            ahead = ["kc", "vc", "vs", "ks", "vw", "kw", "ukT"] + [("nq", t) for t in range(4)]

            def one_ahead(key):
                if key == "ukT":
                    drain("ukT", ukT)
                else:
                    pace(key)

            for r in range(TOPK // 8):
                own.settle()
                for qb in range(1, 4):
                    own.step(v.max(m8[:, 8 * qb - 8:8 * qb], work(qb)))
                own.settle()
                for qb in range(1, 4):
                    own.step(v.match_replace(work(qb), m8[:, 8 * qb - 8:8 * qb], work(qb), -HUGE))
                if r and ahead:
                    one_ahead(ahead.pop(0))
            own.settle()
            for key in ahead:
                one_ahead(key)
            dve.wait_ge(r_in, 128)
            dve.wait_ge(e_in, 16 * N_E)
            for kind in range(2):
                c = rp_at + kind * 992
                rp = mix[:, c:c + 992].rearrange("p (j g n) -> p j g n", j=16, g=2)
                for g in range(2):
                    src = tile(mix, 2 * kind + g).rearrange("p (n r) -> p r n", r=16)
                    for half in range(2):
                        pe_ = peT[:, 16 * kind + 8 * half:16 * kind + 8 * half + 8]
                        v.tensor_tensor(rp[:, 8 * half:8 * half + 8, g, :], src[:, 0:16:2, half:half + NCMP],
                                        pe_.unsqueeze(2).to_broadcast([P, 8, NCMP]), ALU.add).then_inc(rp_ready, 1)
            dve.wait_ge(psum_full, u[("nq", 3)].full)
            for qb in range(1, 4):
                v.tensor_scalar(selm(qb), work(qb), -0.5 * HUGE, MASKED, ALU.is_gt, ALU.mult).then_inc(selm_ready, 1)
            dve.wait_ge(selm_ready, 3)
            attention(pl.even)

            def after_attention(i):
                limit[0] = pl.phase[1] if i == 0 else len(pl.parts)
                feed(pl.phase[i] + SPLITS)

            def residual(key, n, gate, first):
                for t in range(KT):
                    if t % 2 == 0 and key == ("m2", 0, 0):
                        ada_sum(32 + t)
                        ada_sum(33 + t)
                    if key[0] == "mo":
                        pace(key + (t,))
                    elif t % 2 == 0:
                        last = pl.part_of[key + (t + 1,)]
                        for q in range(last - 3, last + 1):
                            feed(q + 1 + SPLITS)
                    o = full(dve, key + (t,))
                    if first:
                        dve.wait_ge(res_scaled, 8 * n + t + 1)
                    v.scalar_tensor_tensor(X(t), o, adac[:, gate + t:gate + t + 1], X(t), ALU.mult, ALU.add)\
                        .then_inc(dve_drained, 1)
                    if t % 2 and key == ("m2", 0, 0):
                        ada_drain(31 + t)
                        ada_drain(32 + t)

            def mlp_dve(i):
                for half in range(2):
                    for t in range(16):
                        if i == 0 and t % 2 == 0:
                            ada_sum(24 + 16 * half + t // 2)
                        pace(("m1", i, 16 * half + t))
                        taken(dve, ("m1", i, 16 * half + t))
                        h = M(t % 8)
                        own.step(v.tensor_tensor(h, h, h, ALU.mult))
                        both_parts(h, tile(hid_hi, t), tile(hid_lo, t)).then_inc(hidden_ready, 1)
                        if i == 0 and t % 2:
                            ada_drain(24 + 16 * half + t // 2)
                    residual(("m2", i, half), 3 + 2 * i, 48 * i + ADA["g2"], half == 0)
                if i == 0:
                    modulations(1)
                layer_norm(3 + 2 * i)

            after_attention(0)
            rest_tiles(3, M, lo_r)
            residual(("mo", 0), 2, ADA["g1"], True)
            layer_norm(2)
            rest_tiles(4, H, lo_r)
            mlp_dve(0)
            rest_tiles(5, H, lo_r)

            dve.wait_ge(ada_ready, 4)
            for name in ("oq", "ok", "ov"):
                for t in range(KT):
                    pace((name, t))
                    if name == "ov" and t:
                        drain(("ovT", t - 1), A(o_v + (t - 1) * S))
            drain(("ovT", 7), A(o_v + 7 * S))
            dve.wait_ge(lam_sem, 16)
            for i in range(2):
                v.tensor_tensor_reduce(out=lam_tmp[:, i * HD:(i + 1) * HD],
                                       in0=lam_in[:, 2 * i * HD:(2 * i + 1) * HD],
                                       in1=lam_in[:, (2 * i + 1) * HD:(2 * i + 2) * HD], scale=1.0, scalar=0.0,
                                       op0=ALU.mult, op1=ALU.add, accum_out=lamc[:, i:i + 1]).then_inc(lam_dots, 1)
            c = vec_b(0, "subln")
            own.step(v.tensor_scalar(small[:, 7:8], cols[:, c:c + 1], 1.0 - LAMBDA_INIT, None, ALU.mult))
            own.settle()
            dve.wait_ge(lam_ready, 1)
            own.step(v.tensor_tensor(small[:, 6:7], lamc[:, 3:4], lamc[:, 2:3], ALU.subtract))
            own.settle()
            own.step(v.tensor_scalar(small[:, 6:7], small[:, 6:7], -LAMBDA_INIT, None, ALU.add))
            own.settle()
            attention(pl.odd)
            for h in range(HEADS):
                head_norm(h)
            after_attention(1)
            rest_tiles(6, M, lo_r)
            residual(("mo", 1), 4, 48 + ADA["g1"], True)
            layer_norm(4)
            rest_tiles(7, H, lo_r)
            mlp_dve(1)
            for tt in range(NT):
                drain(("y", tt, 0), hi32[:, tt * D:tt * D + S])

        @block.gpsimd
        def _(pool):
            g = nc.gpsimd

            def prescale(n):
                c = 32 * (n - 1) + 16
                for t in range(KT):
                    pool.wait_ge(h_ready, 8 * (n - 1) + t + 1)
                    g.tensor_scalar(X(t), X(t), ccols[:, c + t:c + t + 1], ccols[:, c + 8 + t:c + 9 + t],
                                    ALU.mult, ALU.add).then_inc(res_scaled, 1)

            def column_products(n):
                i, j = divmod(n - 1, 2)
                gain, offset = (vec_a(1, "ln_g"), vec_a(1, "ln_b")) if n == 1 else (vec_b(n - 2, "ln_g"), vec_b(n - 2, "ln_b"))
                gain, offset = cols[:, gain:gain + 8], cols[:, offset:offset + 8]
                sc, sh = (48 * i + ADA[k] for k in (("sc1", "sh1") if j == 0 else ("sc2", "sh2")))
                c = 32 * (n - 1)
                scale, shift = adac[:, sc:sc + 8], adac[:, sh:sh + 8]
                pool.wait_ge(ada_ready, 2 * i + 2)
                g.tensor_tensor(ccols[:, c:c + 8], gain, scale, ALU.mult).then_inc(ccols_ready, 1)
                g.tensor_tensor(ccols[:, c + 8:c + 16], offset, scale, ALU.mult).then_inc(pool_own, 1)
                pool.wait_ge(pool_own, 8 + n)
                g.tensor_tensor(ccols[:, c + 8:c + 16], ccols[:, c + 8:c + 16], shift, ALU.add).then_inc(ccols_ready, 1)
                g.tensor_scalar(ccols[:, c + 16:c + 24], gain, ALPHA, None, ALU.mult).then_inc(ccols_ready, 1)
                g.tensor_scalar(ccols[:, c + 24:c + 32], offset, ALPHA, None, ALU.mult).then_inc(ccols_ready, 1)

            g.memset(mean_w[:, :], 1.0 / D).then_inc(memsets, 1)
            g.memset(head_w[:, :], 1.0 / P).then_inc(memsets, 1)
            g.memset(eps[:, :], EPS).then_inc(memsets, 1)
            g.memset(ones[:, :], 1.0).then_inc(memsets, 1)
            pool.wait_ge(memsets, 4)
            g.memset(mix[BUCKETS:BUCKETS + 1, 384:400], -MASKED).then_inc(memsets, 1)
            pool.wait_ge(memsets, 5)
            for l in range(DEPTH):
                for tt in range(NT):
                    vn = R(b1_vn + tt * S)
                    pool.wait_ge(vn_norm, 4 * l + tt + 1)
                    g.tensor_tensor(vn, vn, lng_row, ALU.mult).then_inc(pool_own, 1)
                for tt in range(NT):
                    vn = R(b1_vn + tt * S)
                    pool.wait_ge(pool_own, 4 * l + tt + 1)
                    g.tensor_tensor(vn, vn, lnb_row, ALU.add).then_inc(vn_ready, 1)
                for t in range(4):
                    taken(pool, ("zg", l, t))
                    zg = R(b1_zg + t * S)
                    g.tensor_tensor(zg, zg, ug[:, t * S:(t + 1) * S], ALU.mult).then_inc(uz_ready, 1)
                pool.wait_ge(psum_full, u[("g", l, 15)].full)
                for t in range(KT):
                    g.tensor_tensor(X(t), tile(x_lo, t).bitcast(F32), HI(t), ALU.add).then_inc(x_whole, 1)
                for t in range(KT):
                    c = vec_a(l, "b_out", t)
                    pool.wait_ge(x_whole, 8 * l + t + 1)
                    g.tensor_scalar(X(t), X(t), ALPHA, cols[:, c:c + 1], ALU.mult, ALU.add).then_inc(res_scaled, 1)
                if l == 1:
                    column_products(1)
                    column_products(2)
            prescale(1)
            pool.wait_ge(res_scaled, 24)
            g.memset(tab_full[BUCKETS:BUCKETS + 1, :], -MASKED).then_inc(memsets, 1)
            pool.wait_ge(memsets, 6)
            prescale(2)
            column_products(3)
            column_products(4)
            prescale(3)
            pool.wait_ge(psum_full, u[("oq", 0)].full)
            pool.dma_start(lam_in, bcast(a["diff_lam_2"], 256)).then_inc(lam_sem, 16)
            prescale(4)


_INS = ["x", "w_in", "b_in", "attn_sinks", "gmlp_ln_g", "gmlp_ln_b", "w_spatial", "b_spatial", "w_branch_attn",
        "w_branch_gmlp", "w_out", "b_out", "ln_g", "ln_b", "c_2", "rel_bias_2", "ada_w_2", "ada_b_2", "ln_g_2",
        "ln_b_2", "ev_w_in_2", "ev_w_out_2", "nsa_pe_k_2", "nsa_pe_v_2", "nsa_w1_k_2", "nsa_w2_k_2", "nsa_w1_v_2",
        "nsa_w2_v_2", "dsa_kv_norm_2", "dsa_w_uk_2", "dsa_w_uv_2", "od_w_in_2", "od_w_out_2", "diff_lam_2",
        "diff_subln_2", "mlp_w1_2", "mlp_w2_2"]


def kernel(**inputs):
    import concourse.bacc as bacc
    from concourse.bass_utils import run_bass_kernel_spmd

    nc = bacc.Bacc("TRN2", target_bir_lowering=False, num_devices=1)
    given = {name: np.ascontiguousarray(inputs[name]) for name in _INS}
    given.update(shape_constants())
    arrays, a = {}, {}
    for name, value in given.items():
        arrays[f"in_{name}"] = value
        a[name] = nc.dram_tensor(f"in_{name}", value.shape, mybir.dt.from_np(value.dtype), kind="ExternalInput").ap()
    out = nc.dram_tensor("out_0", (1, S, D), F32, kind="ExternalOutput").ap()
    two_blocks(nc, a, out)
    r = run_bass_kernel_spmd(nc, [arrays], core_ids=[0])
    return r.results[0]["out_0"]
```

```python
from contextlib import ExitStack
import math

import numpy as np
import concourse.bass as bass
from concourse import mybir

ALU = mybir.AluOpType
ACT = mybir.ActivationFunctionType
F32 = mybir.dt.float32
F32R = mybir.dt.float32r
AX_X = mybir.AxisListType.X

P = 128
S = 512
NT = S // P
D = 1024
KT = D // P
DEPTH = 2
HEADS = 8
HD = 64
W1 = 4864
EVEN_IN = 2528
ODD_IN = 3072
DFF = 4096
ALPHA = float(np.float32((2 * DEPTH) ** 0.25))
EPS = 1e-5
MASKED = 1e30
HUGE = 3e38
TOPK = 128
BUCKETS = 32
NCMP = 31
CHUNK = 8 * 256
RING = 4
PART = 8 * 128
SPLITS = 3
BANKS = 6
TW = 640
LAMBDA_INIT = 0.8 - 0.6 * math.exp(-0.3)
EARLY_HEADS = 5
ADAS = 12
ZSLOTS = 6
AHEAD = 3
ORDER = (0, 2, 1, 3)
ZOFF = (0, 128, 384, 768)
KOFF = (0, 512, 896, 1152)


def buckets_of(dist):
    n = np.maximum(dist, 0)
    exact = BUCKETS // 2
    nf = np.maximum(n, 1).astype(np.float32)
    large = exact + (np.log(nf / exact) / math.log(128 / exact) * (BUCKETS - exact)).astype(np.int32)
    return np.where(n < exact, n, np.minimum(large, BUCKETS - 1))


def one_hot(dist):
    out = np.zeros((BUCKETS + 1, len(dist)), np.float32)
    b = buckets_of(dist)
    for i, d in enumerate(dist):
        if d >= 0:
            out[b[i], i] = 1.0
        else:
            out[BUCKETS, i] = 1.0
    return out


def shape_constants():
    ident = np.eye(P, dtype=np.float32)
    s, t = np.arange(P)[:, None], np.arange(P)[None, :]
    tril = (t <= s).astype(np.float32)
    dist = np.arange(P)[:, None] + P - np.arange(2 * P)[None, :]
    valid = (dist >= 0) & (dist < P)
    alibi = np.stack([np.where(valid, np.float32(2.0 ** -(h + 1)) * dist, MASKED) for h in range(HEADS)], 1)
    future = np.where(t <= s, 0.0, -1e30)
    wide = one_hot(511 - np.arange(TW))
    return {
        "ident": ident, "tril": tril, "alibi": alibi.astype(np.float32).reshape(P, HEADS * 2 * P),
        "future": future.astype(np.float32), "hot_rev": wide,
    }


class Unit:
    def __init__(self, index, who, drained):
        self.index, self.who, self.drained = index, who, drained
        self.bank, self.full = index % BANKS, index + 1


class Job:
    pass


class Plan:

    def __init__(self):
        self.units, self.order, self.count = {}, [], {"act": 0, "dve": 0, "z": 0}
        self.chunks, self.parts, self.part_of, self.used = [], [], {}, 0
        self.jobs = []
        self.cur = {"z": 0, "p": 0, "s": 0, "m": 0, "r": 0, "pt": 0, "o": 0}

    def unit(self, key, who, n=1):
        self.count[who] += n
        u = Unit(len(self.order), who, self.count[who])
        assert key not in self.units, key
        self.units[key] = u
        self.order.append(u)
        return u

    def load(self, name, free):
        self.chunks.append([name, free])

    def part(self, chunk, key, src=("plain", 0), kt=KT, used=None):
        self.parts.append((chunk, src, kt, ("unit", key) if used is None else ("used", used)))
        for c in self.chunks:
            if c[0] == chunk:
                c[1] = ("split", len(self.parts))
        self.part_of[key] = len(self.parts) - 1

    def dense(self, key, who, chunk, src=("plain", 0), kt=KT):
        self.unit(key, who)
        self.part(chunk, key, src, kt)

    def job(self, kind, h, l=0, m=0):
        j = Job()
        j.kind, j.h, j.l, j.m, j.J = kind, h, l, m, len(self.jobs)
        j.slot = j.J % 4 if kind == "swa" else (j.J - 2 * HEADS) % ZSLOTS
        j.key = (kind, l, h, m)
        n = 1 if kind == "cmp" else 4
        j.z0, j.p0, j.s0 = self.cur["z"], self.cur["p"], self.cur["s"]
        self.cur["z"] += n
        self.cur["p"] += n
        self.cur["s"] += n
        self.cur["r"] += 1
        self.cur["m"] += kind in ("swa", "cmp")
        j.before = None
        j.mr = self.cur["m"]
        j.r_count = self.cur["r"]
        j.z, j.p, j.s = self.cur["z"], self.cur["p"], self.cur["s"]
        j.has_pt = not (kind == "diff" and m == 0)
        if j.has_pt:
            j.pt = self.cur["pt"]
            self.cur["pt"] += 1
            j.pv = self.cur["pt"]
            if kind == "swa":
                j.first_o, j.last_o = True, h >= 4
                new_o = h < 4
            elif kind in ("cmp", "sel", "win"):
                new_o = kind == "cmp" and h < 4
                j.first_o, j.last_o = kind == "cmp", kind == "win" and h >= 4
            else:
                new_o, j.first_o, j.last_o = True, True, True
            j.new_o = new_o
            if new_o:
                self.cur["o"] += 1
            j.o = self.cur["o"] - 1
        self.jobs.append(j)
        return j

    def s_units(self, j):
        if j.kind == "swa":
            for i in range(2):
                self.unit(("S", j.J, i), "z", 2)
        elif j.kind == "cmp":
            self.unit(("S", j.J, 0), "z", 1)
        else:
            for i, n in enumerate((2, 1, 1)):
                self.unit(("S", j.J, i), "z", n)

    def t_units(self, j):
        if not j.has_pt:
            return
        if j.kind == "swa":
            whos = ("act", "dve")
        elif j.kind == "cmp":
            whos = ("act",)
        else:
            whos = ("act", "act" if j.kind in ("dsa", "diff") else "dve", "act")
        for i, who in enumerate(whos):
            self.unit(("T", j.J, i), who)
        j.ptn = len(whos)


PAIRS = (0, 4, 1, 5, 2, 6, 3, 7)


def make_plan():
    pl = Plan()
    U, DN = pl.unit, pl.dense
    for k in range(KT):
        U(("xT", k), "dve")

    pl.swa = []
    for l in range(DEPTH):
        a = [ADAS * l]

        def next_ada():
            if a[0] < ADAS * (l + 1):
                ada(pl, a[0])
                a[0] += 1

        def two(name, c, who="act", paired=False):
            pl.load((name, l, c), None)
            for t in (2 * c, 2 * c + 1):
                DN((name, l, t), who, (name, l, c), ("paired" if paired else "plain", t % 2))
            if (name, l, c) == ("vg", 0, 0):
                for i in range(3):
                    U(("vec", i), "dve")
            else:
                next_ada()

        two("vg", 0)
        two("vg", 1)
        if l == 0:
            for i in range(2):
                U(("bias", i), "act")
        two("u", 0)
        for tt in range(4):
            U(("vgT", l, tt), "dve")
        U(("wT", l), "dve")
        two("u", 1)
        pl.load(("kv", l, 0), None)
        DN(("v", l), "act", ("kv", l, 0), ("plain", 1))
        DN(("k", l), "act", ("kv", l, 0), ("plain", 0))
        next_ada()
        two("za", 0, paired=True)
        two("za", 1, paired=True)
        U(("vT", l), "dve")
        two("zg", 0)
        two("zg", 1)
        two("q", 0, "dve", True)
        two("q", 1, "dve", True)
        for g in range(4):
            U(("sp", l, g), "dve")
        jobs = [pl.job("swa", h, l) for h in PAIRS]
        pl.swa.append(jobs)
        pl.s_units(jobs[0])
        pl.s_units(jobs[1])
        for s in range(8):
            if s + 2 < 8:
                pl.s_units(jobs[s + 2])
            two("g", s)
            pl.t_units(jobs[s])
        for c in range(2):
            pl.load(("ba", l, c), None)
            pl.load(("bg", l, c), None)
            for t in range(4 * c, 4 * c + 4):
                DN(("ba", l, t), "dve", ("ba", l, c), ("plain", t % 4), 4)
                DN(("bg", l, t), "dve", ("bg", l, c), ("plain", t % 4), 4)
        for c in range(4):
            pl.load(("out", l, c), None)
            for t in (2 * c, 2 * c + 1):
                DN(("out", l, t), "dve", ("out", l, c), ("plain", t % 2))

    pl.load("lat", None)
    DN("lat", "act", "lat", ("plain", 0))
    DN("ik", "act", "lat", ("twice", 2))
    pl.load("misc", None)
    DN("misc", "act", "misc", ("plain", 0))
    U("latT", "dve")
    for c in range(2):
        pl.load(("iq", c), None)
        for t in (2 * c, 2 * c + 1):
            DN(("iq", t), "act", ("iq", c), ("plain", t % 2))
        if c == 0:
            U("miscT", "dve")
    U("ckvT", "dve")
    pl.load(("dq", 0), None)
    pl.load(("dq", 1), None)
    for qb in range(1, 4):
        for j in range(8):
            U(("I", qb, j), "act")
            if qb < 3 and j % 4 == 3:
                t = (qb - 1) * 2 + j // 4
                DN(("dq", t), "act", ("dq", t // 2), ("plain", t % 2))
    for name, one, two_ in (("c", "kc", "vc"), ("s", "vs", "ks"), ("w", "vw", "kw")):
        pl.load(("kv2", name), None)
        DN(one, "act", ("kv2", name), ("plain", 1 if name != "c" else 0))
        DN(two_, "act", ("kv2", name), ("plain", 0 if name != "c" else 1))
        if name != "c":
            U(one + "T", "act")
    U("ukT", "dve")
    for c in range(2):
        pl.load(("nq", c), None)
        for t in (2 * c, 2 * c + 1):
            DN(("nq", t), "act", ("nq", c), ("paired", t % 2))
    for h in range(8):
        U(("ql", h), "act")
    pl.phase = [len(pl.parts)]
    for kind in range(2):
        pl.used += 1
        pl.load(("w1", kind, 0), ("used", pl.used))
        pl.load(("w1", kind, 1), ("unit", ("hid", kind)))
        U(("hid", kind), "act")
    for kind in range(2):
        U(("hidT", kind), "act")
    U("kcT", "act")
    U("vct", "act")
    jobs = [pl.job(kind, h) for h in PAIRS for kind in ("cmp", "sel", "win")]
    jobs += [pl.job("dsa", h) for h in range(8)]
    pl.even = jobs
    steps(pl, jobs)
    mixer_out(pl, 0)
    mlp(pl, 0)
    for name in ("oq", "ok", "ov"):
        for c in range(4):
            pl.load((name, c), None)
            for t in (2 * c, 2 * c + 1):
                DN((name, t), "act", (name, c), ("plain", t % 2))
                if name == "ov" and t:
                    U(("ovT", t - 1), "dve")
    U(("ovT", 7), "dve")
    pl.phase.append(len(pl.parts))
    jobs = [pl.job("diff", h, m=m) for h in range(8) for m in range(2)]
    pl.odd = jobs
    steps(pl, jobs)
    mixer_out(pl, 1)
    mlp(pl, 1)
    for c in range(2):
        for tt in range(NT):
            U(("y", tt, c), "act" if c else "dve")
    return pl


def ada(pl, n):
    pl.load(("ada", n), ("acc", n + 1))
    pl.unit(("ada", n), "dve")


def spread_after(j):
    return {("diff", 6, 0): range(3), ("diff", 6, 1): range(3, EARLY_HEADS)}.get((j.kind, j.h, j.m), ())


def steps(pl, jobs):
    n = len(jobs)
    for i, j in enumerate(jobs):
        j.before = None
        if i >= ZSLOTS:
            j.before = jobs[i - ZSLOTS] if jobs[i - ZSLOTS].has_pt else jobs[i - ZSLOTS + 1]
    for i in range(AHEAD):
        pl.s_units(jobs[i])
    for s in range(n + 2):
        if s + AHEAD < n:
            pl.s_units(jobs[s + AHEAD])
        if s < n:
            pl.t_units(jobs[s])
        if 0 <= s - 2 < n:
            j = jobs[s - 2]
            if j.kind == "dsa":
                pl.unit(("uv", j.h), "act")
            if (j.kind, j.h, j.m) == ("diff", EARLY_HEADS - 1, 1):
                pl.unit("msA", "act")
            for h in spread_after(j):
                pl.unit(("rb", h), "dve")
    if jobs[0].kind == "diff":
        pl.unit("msB", "act")
        for h in range(EARLY_HEADS, HEADS):
            pl.unit(("rb", h), "dve")


def mixer_out(pl, i):
    for c in range(4):
        pl.load(("mo", i, c), None)
        for t in (2 * c, 2 * c + 1):
            pl.dense(("mo", i, t), "dve", ("mo", i, c), ("plain", t % 2))


def mlp(pl, i):
    for half in range(2):
        for c in range(8 * half, 8 * half + 8):
            pl.load(("m1", i, c), None)
            for t in (2 * c, 2 * c + 1):
                pl.dense(("m1", i, t), "act", ("m1", i, c), ("plain", t % 2))
            if i == 0:
                ada(pl, 24 + 8 * half + c)
        for c in range(4):
            for t in (2 * c, 2 * c + 1):
                pl.unit(("m2", i, half, t), "dve")
            for kc in range(2):
                name = ("m2", i, half, c, kc)
                pl.load(name, None)
                for t in (2 * c, 2 * c + 1):
                    key = ("m2", i, half, t)
                    if kc == 0:
                        pl.used += 1
                    pl.part(name, key, ("plain", t % 2), used=pl.used if kc == 0 else None)
            if i == 0 and half == 0:
                ada(pl, 32 + 2 * c)
                ada(pl, 33 + 2 * c)


N_VEC, N_E = 19, 5

N_A, N_B, N_C = 124, 128, 41


def vec_a(l, name, t=0):
    at = {"q": 0, "k": 4, "v": 5, "za": 6, "u": 10, "vg": 14, "zg": 18, "g": 22,
          "b_out": 38, "ln_g": 46, "ln_b": 54}[name]
    return 62 * l + at + t


def vec_b(i, name, t=0):
    if name == "ada_b":
        return N_A + 48 * i + t
    if name == "ln_g":
        return N_A + 96 + 8 * i + t
    if name == "ln_b":
        return N_A + N_B + 8 * i + t
    return N_A + N_B + {"subln": 32, "c": 33}[name] + t


ADA = {"sh1": 0, "sc1": 8, "g1": 16, "sh2": 24, "sc2": 32, "g2": 40}


class Steps:

    def __init__(self, eng, sem):
        self.eng, self.sem, self.n = eng, sem, 0

    def step(self, ins):
        self.n += 1
        return ins.then_inc(self.sem, 1)

    def settle(self):
        self.eng.wait_ge(self.sem, self.n)


def two_blocks(nc, a, out):
    pl = make_plan()
    u = pl.units
    bias_rows = nc.dram_tensor("bias_rows", (16, P, TW), F32, kind="Internal").ap()

    with ExitStack() as ctx:
        def sb(name, cols):
            return ctx.enter_context(nc.sbuf_tensor(name, [P, cols], F32))

        def sem(name):
            return ctx.enter_context(nc.semaphore(name))

        cols = sb("cols", N_A + N_B + N_C)
        adac = sb("adac", 2 * 48)
        ident = sb("ident", P)
        mean_w = sb("mean_w", P)
        head_w = sb("head_w", 15)
        tril = sb("tril", P)
        negm = sb("negm", 4 * ZSLOTS)
        sums = sb("sums", 4 * ZSLOTS)
        recips = sb("recips", 4 * ZSLOTS)
        esink = sb("esink", 4 * ZSLOTS)
        sinks = sb("sinks", 2 * HEADS)
        nsinks = sb("nsinks", 2 * HEADS)
        stats = sb("stats", 4 * 6 + 4 * 2 + 4)
        cact = sb("cact", KT)
        ones = sb("ones", 1)
        ccols = sb("ccols", 4 * 32)
        small = sb("small", 8)
        eps = sb("eps", 1)
        base = -(-nc.sbuf_base // 64) * 64

        def at(name, off, n, dt=F32):
            return nc.alloc_sbuf_tensor_at(name, [P, n], dt, offset=base + 4 * off)

        X0, HH0, HL0, MIX0, RAW0, W0 = 0, 4096, 8192, 12288, 16384, 24576
        REST = W0 + 2 * SPLITS * PART
        raw = at("raw", RAW0, RING * CHUNK)
        w_hi = at("w_hi", W0, SPLITS * PART, F32R)
        w_lo = at("w_lo", W0 + SPLITS * PART, SPLITS * PART, F32R)
        zarea = at("zarea", W0, 4 * 1280)
        x = at("x", X0, KT * S)
        x_lo = at("x_lo", X0, KT * S, F32R)
        hi32, hi_r = at("hi32", HH0, KT * S), at("hi_r", HH0, KT * S, F32R)
        lo32, lo_r = at("lo32", HL0, KT * S), at("lo_r", HL0, KT * S, F32R)
        mix = at("mix", MIX0, KT * S)
        rest = at("rest", REST, 21248)
        psum = ctx.enter_context(nc.psum_tensor("psum", [P, 8, 512], F32))

        def tile(t, i, n=S):
            return t[:, i * n:(i + 1) * n]

        def X(t):
            return tile(x, t)

        def H(t):
            return tile(lo32, t)

        def stat_row():
            return R(acc_at)

        def dev_row():
            return M(7)

        def HI(t):
            return tile(hi_r, t).bitcast(F32)

        def M(t):
            return tile(mix, t)

        def R(off, n=S):
            return rest[:, off:off + n]

        alibi = R(0, 2048)
        lng_row, lnb_row, bs_row = R(5632), R(6144), R(6656)
        ws_raw, ws_t = R(7168), R(7680)
        b1_z, b1_pt, acc_at, b1_vn, b1_zg, b1_q = 2048, 8704, 20480, 8704, 10752, 12800
        b1_k, b1_v, b1_ga, b1_vT = 14848, 15360, 15872, 19968
        za, ug = mix[:, 0:2048], mix[:, 2048:4096]
        za_lo = at("za_lo", MIX0, 4 * S, F32R)
        q_hi = at("q_hi", REST + b1_q, 4 * S, F32R)
        u_hi = at("u_hi", MIX0 + 2048, 4 * S, F32R)
        zg_lo = at("zg_lo", REST + b1_zg, 4 * S, F32R)
        ga_lo = at("ga_lo", REST + b1_ga, KT * S, F32R)
        SWA_Z = 896

        def ga(i):
            return R(b1_ga + i * S) if i < 8 else H(i - 8)

        T_AT, PT_AT, A0 = 0, 1536, 5088
        biasc = R(4096, 4 * 8 * NCMP)

        def A(off, n=S):
            return R(A0 + off, n)

        e_q, e_dq, e_ql, e_ks, e_vs, e_kw, e_vw = 0, 2048, 4096, 8192, 8704, 9216, 9728
        e_ckv, e_ckvT, e_ik, e_kc, e_vc, e_iq = 10240, 10752, 11264, 11776, 12288, 6144
        small0 = 12800
        kcT = A(small0, NCMP)
        vct = A(small0 + 32, P)
        hid = A(small0 + 160, 248)
        gates = A(small0 + 416, 96)
        iw = A(small0 + 512, 32)
        w2kv = A(small0 + 544, 256)
        kvnorm = A(small0 + 800, P)
        ukT = A(small0 + 928, S)
        peT = A(small0 + 1440, 32)
        m8 = A(small0 + 1472, 24)
        e_tmp = small0 + 1504
        e_olat, w_uv = 2048, A(3072, S)
        uk_raw, future = A(1040, 512), A(1552, P)
        rp_at, relu_at = 2048, 2048
        o_q, o_k, o_v, o_sel = 0, 4096, 8192, 12288
        o_tmp = 13312
        sel = A(o_sel, 8 * P)[0:HEADS, :]
        head_rms = [A(o_tmp + i * S)[0:HEADS, :] for i in range(2)]
        lam_in = A(14336, 256)
        lam_tmp = A(14592, 128)
        lamc = small[:, 0:4]
        work_at = {1: PT_AT, 2: PT_AT + 256, 3: PT_AT + 640}
        selm_at = {1: 2560, 2: 2816, 3: 3200}
        hid_hi = at("hid_hi", REST + PT_AT, 16 * S, F32R)
        hid_lo = at("hid_lo", REST + PT_AT + 16 * S, 16 * S, F32R)

        def hid_rows(kind):
            return A(e_tmp + kind * 256, 256)[0:62, :]

        def work(qb):
            return R(work_at[qb], (qb + 1) * P)

        def selm(qb):
            return lo32[:, selm_at[qb]:selm_at[qb] + (qb + 1) * P]

        def zbuf(j):
            if j.kind == "swa":
                return R(b1_z + j.slot * SWA_Z, SWA_Z)
            if j.slot >= 4:
                return hi32[:, (j.slot - 4) * 1280:(j.slot - 3) * 1280]
            return zarea[:, j.slot * 1280:(j.slot + 1) * 1280]

        def ptbuf(j):
            n, at_ = (SWA_Z, b1_pt) if j.kind == "swa" else (1280, PT_AT)
            return R(at_ + (j.pt % 2) * n, n)

        def stat4(t, j, i=None):
            return t[:, 4 * j.slot:4 * j.slot + 4] if i is None else t[:, 4 * j.slot + i:4 * j.slot + i + 1]

        def tbuf(ti):
            return R(T_AT + (ti % 3) * S)

        def operand(hi, lo):
            return (lambda k: tile(hi, k)), (lambda k: tile(lo, k))

        tables = [h for h in PAIRS] + [8 + h for h in range(8)] + list(range(16))
        for i, j in enumerate(pl.even):
            j.ti = i // 3 if j.kind != "dsa" else 8 + j.h
            j.t_last = j.kind in ("win", "dsa")
        for i, j in enumerate(pl.odd):
            j.ti, j.t_last = 16 + i, True

        psum_full = sem("psum_full")
        act_drained = sem("act_drained")
        dve_drained = sem("dve_drained")
        z_ready = sem("z_ready")
        m_ready = sem("m_ready")
        p_ready = sem("p_ready")
        sink_ready = sem("sink_ready")
        s_ready = sem("s_ready")
        pv_done = sem("pv_done")
        o_drained = sem("o_drained")
        landed = [sem(f"landed{i}") for i in range(RING)]
        part_used = sem("part_used")
        w_hi_ready = sem("w_hi_ready")
        w_lo_ready = sem("w_lo_ready")
        hi_ready = sem("hi_ready")
        op_ready = sem("op_ready")
        acc_ready = sem("acc_ready")
        const_in, x_in, rows_in = sem("const_in"), sem("x_in"), sem("rows_in")
        vec_in, tab_in = sem("vec_in"), sem("tab_in")
        e_in, r_in, uv_in, lam_sem = sem("e_in"), sem("r_in"), sem("uv_in"), sem("lam_sem")
        t_in = [sem(f"t_in{i}") for i in range(3)]
        memsets, bias_out = sem("memsets"), sem("bias_out")
        c_ready, ada_ready = sem("c_ready"), sem("ada_ready")
        ws_masked = sem("ws_masked")
        vg_gelu, vn_norm, vn_ready = sem("vg_gelu"), sem("vn_norm"), sem("vn_ready")
        uz_ready, yg_ready = sem("uz_ready"), sem("yg_ready")
        sig_ready, merged = sem("sig_ready"), sem("merged")
        res_scaled = sem("res_scaled")
        ln_centered, ln_squared, stat_full = sem("ln_centered"), sem("ln_squared"), sem("stat_full")
        ln_scaled, x_ready = sem("ln_scaled"), sem("x_ready")
        sum_ready = sem("sum_ready")
        mean_copied = sem("mean_copied")
        d_squared, d_copied = sem("d_squared"), sem("d_copied")
        var_taken, ln_shifted, x_normed = sem("var_taken"), sem("ln_shifted"), sem("x_normed")
        bc_ready = sem("bc_ready")
        nsink_ready = sem("nsink_ready")
        std_ready, var_ready = sem("std_ready"), sem("var_ready")
        lat_done, relu_ready, isc_used = sem("lat_done"), sem("relu_ready"), sem("isc_used")
        future_used, iw_ready, gates_ready = sem("future_used"), sem("iw_ready"), sem("gates_ready")
        mask_in, x_whole = sem("mask_in"), sem("x_whole")
        warm = sem("warm")
        ya_ready, ccols_ready = sem("ya_ready"), sem("ccols_ready")
        selm_ready, rp_ready = sem("selm_ready"), sem("rp_ready")
        hidden_ready = sem("hidden_ready")
        sq_ready, rms_ready, sel_ready = sem("sq_ready"), sem("rms_ready"), sem("sel_ready")
        lam_ready, lam_dots = sem("lam_ready"), sem("lam_dots")
        y_out = sem("y_out")
        dve_own, pool_own = sem("dve_own"), sem("pool_own")
        drained_by = {"act": act_drained, "dve": dve_drained, "z": z_ready}

        def freed(eng, token):
            kind, n = token
            if kind == "unit":
                eng.wait_ge(psum_full, u[n].full)
            else:
                eng.wait_ge({"used": part_used, "split": w_lo_ready, "acc": acc_ready}[kind], n)

        def bcast(ap, n, off=0):
            return bass.AP(tensor=ap.tensor, offset=ap.offset + off, ap=[[0, P], [1, n]])

        def full(eng, key):
            eng.wait_ge(psum_full, u[key].full)
            return psum[:, u[key].bank, :]

        def taken(eng, key):
            eng.wait_ge(drained_by[u[key].who], u[key].drained)

        def norm_key(n):
            return (("out", 0), ("out", 1), ("mo", 0), ("m2", 0, 1), ("mo", 1), ("m2", 1, 1))[n]

        block = ctx.enter_context(nc.Block())

        ev = a["ev_w_in_2"][0]
        at1 = {"q": 0, "kv": 512, "za": 768, "u": 1280, "vg": 1792, "zg": 2304, "g": 2816}
        ate = {"iq": 1944, "dq": 1304, "nq": 0, "c": 512, "s": 768, "w": 1024}

        def pieces(name):
            kind = name[0] if isinstance(name, tuple) else name
            every, ks = slice(0, P), slice(0, KT)

            def plain(w, c0, n, kt=KT):
                return (kt, n), [(every, slice(0, kt), slice(0, n),
                                  w.rearrange("(k p) n -> p k n", p=P)[:, :, c0:c0 + n])]

            def joined(w, parts):
                loads, c = [], 0
                for c0, n in parts:
                    loads.append((every, ks, slice(c, c + n), w.rearrange("(k p) n -> p k n", p=P)[:, :, c0:c0 + n]))
                    c += n
                return (KT, c), loads

            def split(w, c0, n, kt):
                loads = []
                for hf in range(2):
                    src = w[hf * 256:hf * 256 + 256, c0:c0 + n].rearrange("(t d) n -> d t n", d=HD)
                    loads.append((slice(hf * HD, hf * HD + HD), slice(0, 4), slice(0, n), src))
                if kt > 4:
                    loads.append((every, slice(4, kt), slice(0, n),
                                  w[512:1024, c0:c0 + n].rearrange("(k p) n -> p k n", p=P)))
                return (kt, n), loads

            if kind == "ada":
                l, c = divmod(name[1], 24)
                return plain(a["ada_w_2"][l], 256 * c, 256)
            if kind in ("q", "za"):
                c0 = at1[kind] + P * name[2]
                return joined(a["w_in"][name[1]], ((c0, P), (c0 + 256, P)))
            if kind in at1:
                return plain(a["w_in"][name[1]], at1[kind] + 256 * name[2], 256)
            if kind == "ba":
                return split(a["w_branch_attn"][name[1]], 512 * name[2], 512, 4)
            if kind == "bg":
                return plain(a["w_branch_gmlp"][name[1]], 512 * name[2], 512, 4)
            if kind == "out":
                return plain(a["w_out"][name[1]], 256 * name[2], 256)
            if kind == "lat":
                return joined(ev, ((1816, 128), (2456, 64)))
            if kind == "misc":
                return joined(ev, ((1280, 96), (2496, 32)))
            if kind == "nq":
                return joined(ev, ((P * name[1], P), (P * name[1] + 256, P)))
            if kind in ("iq", "dq"):
                return plain(ev, ate[kind] + 256 * name[1], 256)
            if kind == "kv2":
                return plain(ev, ate[name[1]], 256)
            if kind == "w1":
                w = (a["nsa_w1_k_2"], a["nsa_w1_v_2"])[name[1]][0]
                return plain(w[name[2] * D:(name[2] + 1) * D, :], 0, 256)
            if kind == "mo":
                if name[1] == 0:
                    return split(a["ev_w_out_2"][0], 256 * name[2], 256, 8)
                return plain(a["od_w_out_2"][0], 256 * name[2], 256)
            if kind in ("oq", "ok", "ov"):
                return plain(a["od_w_in_2"][0], 1024 * ("oq", "ok", "ov").index(kind) + 256 * name[1], 256)
            if kind == "m1":
                return plain(a["mlp_w1_2"][name[1]], 256 * name[2], 256)
            if kind == "m2":
                _, i, half, c, kc = name
                r0 = (2 * half + kc) * D
                return plain(a["mlp_w2_2"][i][r0:r0 + D, :], 256 * c, 256)
            raise KeyError(name)

        def slot_view(i, shape):
            kt, n = shape
            return raw[:, (i % RING) * CHUNK:(i % RING) * CHUNK + kt * n].rearrange("p (k n) -> p k n", k=kt)

        arrival, reached = {}, [0] * RING
        for i, (name, _) in enumerate(pl.chunks):
            reached[i % RING] += 16 * len(pieces(name)[1])
            arrival[name] = (i, reached[i % RING])

        def arrived(eng, name):
            i, n = arrival[name]
            eng.wait_ge(landed[i % RING], n)
            return slot_view(i, pieces(name)[0])

        def part_source(view, src):
            how, c = src
            if how == "plain":
                return view[:, :, c * P:(c + 1) * P]
            if how == "paired":
                return view.rearrange("p k (b t d) -> p k b t d", b=2, d=HD)[:, :, :, c, :]
            return view[:, :, c * HD:(c + 1) * HD].unsqueeze(2).to_broadcast([P, view.shape[1], 2, HD])

        def part_view(ring, q):
            _, src, kt, _ = pl.parts[q]
            v = ring[:, (q % SPLITS) * PART:(q % SPLITS) * PART + kt * P]
            if src[0] == "plain":
                return v.rearrange("p (k n) -> p k n", k=kt)
            return v.rearrange("p (k b d) -> p k b d", k=kt, b=2)

        @block.sync
        def _(sp):
            def rows(ap, off, n):
                return bass.AP(tensor=ap.tensor, offset=ap.offset + off, ap=[[P, n], [1, P]])

            def paired_rows(ap, off):
                return bass.AP(tensor=ap.tensor, offset=ap.offset + off, ap=[[HD, 4], [256, 2], [1, HD]])

            vecs = []
            for l in range(DEPTH):
                r, b = 62 * l, l * W1
                for row, off in ((r, b), (r + 6, b + 768)):
                    vecs.append((mix[row:row + 4, 0:P].rearrange("p (b d) -> p b d", b=2), paired_rows(a["b_in"], off)))
                vecs.append((mix[r + 4:r + 6, 0:P], rows(a["b_in"], b + 512, 2)))
                vecs.append((mix[r + 10:r + 38, 0:P], rows(a["b_in"], b + 1280, 28)))
                for i, name in enumerate(("b_out", "ln_g", "ln_b")):
                    vecs.append((mix[r + 38 + 8 * i:r + 46 + 8 * i, 0:P], rows(a[name], l * D, 8)))
            vecs.append((mix[0:96, P:2 * P], rows(a["ada_b_2"], 0, 96)))
            vecs.append((mix[96:128, P:2 * P], rows(a["ln_g_2"], 0, 32)))
            vecs.append((mix[0:32, 2 * P:3 * P], rows(a["ln_b_2"], 0, 32)))
            vecs.append((mix[32:33, 2 * P:3 * P], rows(a["diff_subln_2"], 0, 1)))
            vecs.append((mix[33:41, 2 * P:3 * P], rows(a["c_2"], 0, 8)))
            assert len(vecs) == N_VEC

            def vectors():
                for dst, src in vecs:
                    sp.dma_start(dst, src).then_inc(vec_in, 16)
                sp.dma_start(mix[0:BUCKETS, 384:400], a["rel_bias_2"]).then_inc(tab_in, 16)
                sp.dma_start(mix[0:BUCKETS + 1, 512:512 + TW], a["hot_rev"]).then_inc(tab_in, 16)

            for tt in (2, 3):
                sp.dma_start(lo32[:, tt * D:(tt + 1) * D], a["x"][0, tt * P:(tt + 1) * P, :]).then_inc(x_in, 16)
            for i, (name, _) in enumerate(pl.chunks):
                if i == 2:
                    vectors()
                if i >= RING:
                    freed(sp, pl.chunks[i - RING][1])
                shape, loads = pieces(name)
                v = slot_view(i, shape)
                for ps, ks, ns, src in loads:
                    sp.dma_start(v[ps, ks, ns], src).then_inc(landed[i % RING], 16)
            for c in range(2):
                for tt in range(NT):
                    taken(sp, ("y", tt, c))
                    sp.dma_start(out[0, tt * P:(tt + 1) * P, c * S:(c + 1) * S],
                                 hi32[:, tt * D + c * S:tt * D + (c + 1) * S]).then_inc(y_out, 16)
            sp.wait_ge(y_out, 16 * 2 * NT)

        @block.tensor
        def _(pe):
            made = [0]

            def begin(key):
                unit = u[key]
                assert unit.index == made[0], (key, unit.index, made[0])
                made[0] += 1
                if unit.index >= BANKS:
                    before = pl.order[unit.index - BANKS]
                    pe.wait_ge(drained_by[before.who], before.drained)
                return psum[:, unit.bank, :]

            part = [0]

            def multiply(o, chunk, op, first=True, last=True, inside=None):
                q = part[0]
                part[0] += 1
                name, _, kt, token = pl.parts[q]
                assert name == chunk, (name, chunk)
                pe.wait_ge(w_lo_ready, q + 1)
                hi, lo = (r[:, (q % SPLITS) * PART:(q % SPLITS + 1) * PART] for r in (w_hi, w_lo))
                for k in range(kt):
                    if k == 6 and inside:
                        inside()
                    w = slice(k * P, (k + 1) * P)
                    nc.tensor.matmul(o, hi[:, w], op[0](k), start=first and k == 0, stop=False, skip_group_check=True)
                    nc.tensor.matmul(o, hi[:, w], op[1](k), start=False, stop=False, skip_group_check=True)
                    mm = nc.tensor.matmul(o, lo[:, w], op[0](k), start=False, stop=last and k == kt - 1,
                                          skip_group_check=True)
                mm.then_inc(psum_full if token[0] == "unit" else part_used, 1)

            def dense(key, chunk, op, inside=None):
                multiply(begin(key), chunk, op, inside=inside)

            def ada(n):
                o = begin(("ada", n))
                pe.wait_ge(acc_ready, n + 1)
                acc = R(acc_at + (n % 2) * 256, 256)
                for t in range(2):
                    mm = nc.tensor.matmul(o[:, t:t + 1], acc[:, t * P:(t + 1) * P], ones[:, :], start=True, stop=True)
                mm.then_inc(psum_full, 1)

            def dense_pair(keys, chunks, op, i, between=None):
                banks = [begin(key) for key in keys]
                q = part[0]
                part[0] += 2
                assert [pl.parts[q + j][0] for j in range(2)] == chunks
                if between == "merged":
                    ready, before = merged, 8 * i
                elif i:
                    ready, before = op_ready, 8 * (i - 1)
                else:
                    ready, before = dve_drained, 0
                for k in range(KT):
                    if k == EARLY_HEADS and between not in (None, "merged"):
                        between()
                    pe.wait_ge(ready, before + k + 1)
                    for j in range(2):
                        if k == 0:
                            pe.wait_ge(w_lo_ready, q + j + 1)
                        c = ((q + j) % SPLITS) * PART + k * P
                        hi, lo = w_hi[:, c:c + P], w_lo[:, c:c + P]
                        nc.tensor.matmul(banks[j], hi, op[0](k), start=k == 0, stop=False, skip_group_check=True)
                        nc.tensor.matmul(banks[j], hi, op[1](k), start=False, stop=False, skip_group_check=True)
                        mm = nc.tensor.matmul(banks[j], lo, op[0](k), start=False, stop=k == KT - 1,
                                              skip_group_check=True)
                        if k == KT - 1:
                            mm.then_inc(psum_full, 1)

            def turn(key, src):
                o = begin(key)
                for tt in range(NT):
                    mm = nc.tensor.transpose(o[:, tt * P:(tt + 1) * P], src[:, tt * P:(tt + 1) * P], ident[:, :])
                mm.then_inc(psum_full, 1)

            def scores(j):
                def emit(o, c, lhs, rhs, n):
                    return nc.tensor.matmul(o[:, c:c + n], lhs, rhs, start=True, stop=True)

                hf = slice((j.h >= 4) * HD, (j.h >= 4) * HD + HD)
                t = j.h % 4
                if j.kind == "swa":
                    q, k = R(b1_q + t * S)[hf, :], R(b1_k)[hf, :]
                    for i in range(2):
                        o = begin(("S", j.J, i))
                        c = 0
                        for qb in (2 * i, 2 * i + 1):
                            k0 = max(0, qb - 1) * P
                            n = (qb + 1) * P - k0
                            mm = emit(o, c, q[:, qb * P:(qb + 1) * P], k[:, k0:k0 + n], n)
                            c += n
                        mm.then_inc(psum_full, 1)
                elif j.kind == "cmp":
                    o = begin(("S", j.J, 0))
                    q = A(e_q + t * S)[hf, :]
                    for qb in range(4):
                        mm = emit(o, qb * NCMP, q[:, qb * P:(qb + 1) * P], kcT[hf, :], NCMP)
                    mm.then_inc(psum_full, 1)
                else:
                    if j.kind in ("sel", "win"):
                        q = A(e_q + t * S)[hf, :]
                        k = A(e_ks if j.kind == "sel" else e_kw)[hf, :]
                    elif j.kind == "dsa":
                        q, k = A(e_ql + j.h * S), A(e_ckvT)
                    else:
                        q, k = A(o_q + j.h * S)[j.m * HD:(j.m + 1) * HD, :], A(o_k + j.h * S)[j.m * HD:(j.m + 1) * HD, :]
                    for i, qbs in enumerate(((0, 2), (1,), (3,))):
                        o = begin(("S", j.J, i))
                        c = 0
                        for qb in qbs:
                            n = (qb + 1) * P
                            mm = emit(o, c, q[:, qb * P:(qb + 1) * P], k[:, 0:n], n)
                            c += n
                        mm.then_inc(psum_full, 1)

            def transposes(j):
                if not j.has_pt:
                    return
                pe.wait_ge(s_ready, j.s)
                z = zbuf(j)
                if j.kind == "swa":
                    plan = [[(768 * 0 + (0 if qb == 0 else 256 * qb), qb * P) for qb in range(4)],
                            [(256 * qb - 128, (qb - 1) * P) for qb in range(1, 4)]]
                elif j.kind == "cmp":
                    plan = [[(qb * NCMP, qb * P) for qb in range(4)]]
                else:
                    plan = [[(ZOFF[qb], qb * P) for qb in range(4)],
                            [(ZOFF[qb] + P, (qb - 1) * P) for qb in range(1, 4)],
                            [(ZOFF[2] + 2 * P, 0), (ZOFF[3] + 2 * P, P), (ZOFF[3] + 3 * P, 2 * P)]]
                for i, moves in enumerate(plan):
                    o = begin(("T", j.J, i))
                    for src, dst in moves:
                        n = NCMP if j.kind == "cmp" else P
                        mm = nc.tensor.transpose(o[0:n, dst:dst + P], z[:, src:src + n], ident[:, :])
                    mm.then_inc(psum_full, 1)

            def values(j):
                if not j.has_pt:
                    return
                if j.new_o and j.o >= 2:
                    pe.wait_ge(o_drained, j.o - 1)
                for i in range(j.ptn):
                    taken(pe, ("T", j.J, i))
                pt = ptbuf(j)
                bank = psum[:, 6 + j.o % 2, :]
                hf = slice((j.h >= 4) * HD, (j.h >= 4) * HD + HD)
                if j.kind == "swa":
                    v = R(b1_v).rearrange("p (b f) -> p b f", b=4)
                    for qb in range(4):
                        mm = nc.tensor.matmul(bank[hf, qb * P:(qb + 1) * P], v[:, qb, hf], pt[:, qb * P:(qb + 1) * P],
                                              start=True, stop=qb == 0)
                        if qb:
                            mm = nc.tensor.matmul(bank[hf, qb * P:(qb + 1) * P], v[:, qb - 1, hf],
                                                  pt[:, 512 + (qb - 1) * P:512 + qb * P], start=False, stop=True)
                elif j.kind == "cmp":
                    mm = nc.tensor.matmul(bank[hf, :], vct[0:NCMP, hf], pt[0:NCMP, 0:512], start=True, stop=False,
                                          skip_group_check=True)
                else:
                    for kb in range(4):
                        n = (4 - kb) * P
                        if j.kind in ("sel", "win"):
                            v = A(e_vs if j.kind == "sel" else e_vw).rearrange("p (b f) -> p b f", b=4)[:, kb, hf]
                            o = bank[hf, kb * P:512]
                            start, stop = False, j.kind == "win" and kb == 3
                        elif j.kind == "dsa":
                            v = A(e_ckv).rearrange("p (b f) -> p b f", b=4)[:, kb, :]
                            o, start, stop = bank[:, kb * P:512], kb == 0, kb == 3
                        else:
                            v = A(o_v + j.h * S + kb * P, P)
                            o, start, stop = bank[:, kb * P:512], kb == 0, kb == 3
                        mm = nc.tensor.matmul(o, v, pt[:, KOFF[kb]:KOFF[kb] + n], start=start, stop=stop,
                                              skip_group_check=True)
                mm.then_inc(pv_done, 1)

            def after(j):
                if j.kind == "dsa":
                    pe.wait_ge(o_drained, j.o + 1)
                    pe.wait_ge(uv_in, 16)
                    o = begin(("uv", j.h))
                    hf = (j.h % 2) * HD
                    nc.tensor.matmul(o[hf:hf + HD, :], w_uv[:, j.h * HD:(j.h + 1) * HD], A(e_olat + (j.h % 2) * S),
                                     start=True, stop=True).then_inc(psum_full, 1)
                if (j.kind, j.h, j.m) == ("diff", EARLY_HEADS - 1, 1):
                    mean_squares("msA", range(EARLY_HEADS))
                for h in spread_after(j):
                    spread(h)

            def mean_squares(key, heads):
                o = begin(key)
                for h in heads:
                    pe.wait_ge(sq_ready, h + 1)
                    mm = nc.tensor.matmul(o[0:HEADS, :], head_w[:, 7 - h:15 - h], H(h), start=h == heads[0],
                                          stop=h == heads[-1])
                mm.then_inc(psum_full, 1)

            def spread(h, o=None):
                if o is None:
                    o = begin(("rb", h))
                pe.wait_ge(rms_ready, 2 if h >= EARLY_HEADS else 1)
                nc.tensor.matmul(o, sel[:, h * P:(h + 1) * P], head_rms[h >= EARLY_HEADS], start=True, stop=True)\
                    .then_inc(psum_full, 1)

            def attention(jobs):
                for j in jobs[:AHEAD]:
                    scores(j)
                for s in range(len(jobs) + 2):
                    if s + AHEAD < len(jobs):
                        scores(jobs[s + AHEAD])
                    if s < len(jobs):
                        transposes(jobs[s])
                    if 0 <= s - 1 < len(jobs):
                        values(jobs[s - 1])
                    if 0 <= s - 2 < len(jobs):
                        after(jobs[s - 2])

            def average(bank, tile_, start, stop):
                return nc.tensor.matmul(psum[:, bank, :], mean_w[:, :], tile_, start=start, stop=stop,
                                        skip_group_check=True)

            def first_mean(n):
                pe.wait_ge(sum_ready, 9 * n + 3)
                average(6, M(7), True, True).then_inc(stat_full, 1)

            def early_squares(n):
                pe.wait_ge(sum_ready, 9 * n + 6)
                average(7, M(0), True, False)

            def last_stats(n):
                pe.wait_ge(sum_ready, 9 * n + 9)
                average(6, M(1), True, False)
                average(7, M(4), False, False)
                taken(pe, norm_key(n) + (7,))
                average(6, X(7), False, True).then_inc(stat_full, 1)
                pe.wait_ge(ln_squared, 8 * n + 7)
                average(7, M(6), False, False)
                pe.wait_ge(ln_squared, 8 * n + 8)
                average(7, M(7), False, True).then_inc(stat_full, 1)

            def last_dense(key, n, op, i, between=None):
                dense_pair([key + (0,), key + (1,)], [key + (0,)] * 2, op, i, between)
                for t in range(2, KT):
                    dense(key + (t,), key + (t // 2,), op, (lambda: early_squares(n)) if t == 7 else None)
                    if t == 5:
                        first_mean(n)
                last_stats(n)

            pe.wait_ge(x_in, 80)
            for k in range(KT):
                o = begin(("xT", k))
                for tt in range(NT):
                    mm = nc.tensor.transpose(o[:, tt * P:(tt + 1) * P],
                                             lo32[:, tt * D + k * P:tt * D + (k + 1) * P], ident[:, :])
                mm.then_inc(psum_full, 1)
            def vectors():
                pe.wait_ge(memsets, 5)
                pe.wait_ge(vec_in, 16 * N_VEC)
                for i, n in enumerate((N_A, N_B, N_C)):
                    o = begin(("vec", i))
                    nc.tensor.transpose(o[:, 0:n], mix[0:n, i * P:(i + 1) * P], ident[0:n, 0:n]).then_inc(psum_full, 1)

            def bias_rows_products():
                pe.wait_ge(tab_in, 32)
                tab, hot = mix[0:BUCKETS + 1, 384:400], mix[0:BUCKETS + 1, 512:512 + TW]
                for i, (c, n) in enumerate(((0, 512), (512, 128))):
                    o = begin(("bias", i))
                    nc.tensor.matmul(o[0:16, 0:n], tab, hot[:, c:c + n], start=True, stop=True).then_inc(psum_full, 1)

            X_OP, H_OP = operand(hi_r, x_lo), operand(hi_r, lo_r)
            for l in range(DEPTH):
                next_ada = [ADAS * l]

                def one_ada():
                    if next_ada[0] < ADAS * (l + 1):
                        ada(next_ada[0])
                        next_ada[0] += 1

                def two(name, c):
                    if name == "vg" and c == 0:
                        dense_pair([(name, l, 0), (name, l, 1)], [(name, l, 0)] * 2, X_OP, l)
                        if l == 0:
                            vectors()
                    else:
                        for t in (2 * c, 2 * c + 1):
                            dense((name, l, t), (name, l, c), X_OP)
                    if (name, l, c) != ("vg", 0, 0):
                        one_ada()

                two("vg", 0)
                two("vg", 1)
                if l == 0:
                    bias_rows_products()
                two("u", 0)
                pe.wait_ge(act_drained, u[("vg", l, 3)].drained)
                for tt in range(NT):
                    o = begin(("vgT", l, tt))
                    for t in range(4):
                        mm = nc.tensor.transpose(o[:, t * P:(t + 1) * P], ga(t)[:, tt * P:(tt + 1) * P], ident[:, :])
                    mm.then_inc(psum_full, 1)
                pe.wait_ge(ws_masked, l + 1)
                o = begin(("wT", l))
                for g in range(4):
                    mm = nc.tensor.transpose(o[:, g * P:(g + 1) * P], ws_raw[:, g * P:(g + 1) * P], ident[:, :])
                mm.then_inc(psum_full, 1)
                two("u", 1)
                for name in ("v", "k"):
                    dense((name, l), ("kv", l, 0), X_OP)
                one_ada()
                two("za", 0)
                two("za", 1)
                taken(pe, ("v", l))
                turn(("vT", l), R(b1_vT))
                for name in ("zg", "q"):
                    two(name, 0)
                    two(name, 1)
                pe.wait_ge(vn_ready, 4 * l + 4)
                taken(pe, ("wT", l))
                for g in range(4):
                    o = begin(("sp", l, g))
                    for c in range(NT):
                        vn = R(b1_vn + c * S)
                        mm = nc.tensor.matmul(o[:, c * P:(c + 1) * P], vn[:, g * P:(g + 1) * P],
                                              ws_t[:, g * P:(g + 1) * P], start=True, stop=True)
                    mm.then_inc(psum_full, 1)
                jobs = pl.swa[l]
                taken(pe, ("k", l))
                taken(pe, ("vT", l))
                taken(pe, ("q", l, 3))
                scores(jobs[0])
                scores(jobs[1])
                for s in range(9):
                    if s + 2 < 8:
                        scores(jobs[s + 2])
                    if s < 8:
                        two("g", s)
                        transposes(jobs[s])
                    if s >= 1:
                        values(jobs[s - 1])
                pe.wait_ge(yg_ready, 4 * l + 4)
                pe.wait_ge(ya_ready, 4 * l + 4)
                for t in range(KT):
                    dense(("ba", l, t), ("ba", l, t // 4), operand(q_hi, za_lo))
                    dense(("bg", l, t), ("bg", l, t // 4), operand(u_hi, zg_lo))
                last_dense(("out", l), l, operand(hi_r, ga_lo), l, "merged")

            def mlp_pe(i, op):
                for half in range(2):
                    for t in range(16 * half, 16 * half + 16):
                        if t == 0:
                            dense_pair([("m1", i, 0), ("m1", i, 1)], [("m1", i, 0)] * 2, H_OP, op)
                        elif t > 1:
                            dense(("m1", i, t), ("m1", i, t // 2), H_OP)
                        if i == 0 and t % 2:
                            ada(24 + 8 * half + t // 2)
                    for c in range(4):
                        banks = [begin(("m2", i, half, t)) for t in (2 * c, 2 * c + 1)]
                        for kc in range(2):
                            if c == 0:
                                pe.wait_ge(hidden_ready, 32 * i + 16 * half + 8 * kc + 8)
                            op_ = [lambda k, r=r: tile(r, 8 * kc + k) for r in (hid_hi, hid_lo)]
                            for bank in banks:
                                multiply(bank, ("m2", i, half, c, kc), op_, first=kc == 0, last=kc == 1)
                            if half and c == 3 and kc == 0:
                                early_squares(3 + 2 * i)
                        if half and c == 2:
                            first_mean(3 + 2 * i)
                        if i == 0 and half == 0:
                            ada(32 + 2 * c)
                            ada(33 + 2 * c)
                last_stats(3 + 2 * i)

            dense_pair(["lat", "ik"], ["lat"] * 2, H_OP, 2)
            dense("misc", "misc", H_OP)
            taken(pe, "lat")
            turn("latT", A(e_tmp))
            for t in range(4):
                dense(("iq", t), ("iq", t // 2), H_OP)
                if t == 1:
                    taken(pe, "misc")
                    turn("miscT", A(e_tmp + S))
            pe.wait_ge(lat_done, 4)
            turn("ckvT", A(e_ckv))
            taken(pe, ("iq", 3))
            for qb in range(1, 4):
                for j in range(8):
                    hf = slice((j % 2) * HD, (j % 2) * HD + HD)
                    n = (qb + 1) * P
                    o = begin(("I", qb, j))
                    nc.tensor.matmul(o[:, 0:n], A(e_iq + (j // 2) * S)[hf, qb * P:(qb + 1) * P], A(e_ik)[hf, 0:n],
                                     start=True, stop=True).then_inc(psum_full, 1)
                    if qb < 3 and j % 4 == 3:
                        t = (qb - 1) * 2 + j // 4
                        dense(("dq", t), ("dq", t // 2), H_OP)
            dense("kc", ("kv2", "c"), H_OP)
            dense("vc", ("kv2", "c"), H_OP)
            for name, v_, k_, tmp in (("s", "vs", "ks", e_tmp), ("w", "vw", "kw", e_tmp + S)):
                dense(v_, ("kv2", name), H_OP)
                dense(k_, ("kv2", name), H_OP)
                taken(pe, v_)
                turn(v_ + "T", A(tmp))
            pe.wait_ge(e_in, 16 * N_E)
            turn("ukT", uk_raw)
            for t in range(4):
                dense(("nq", t), ("nq", t // 2), H_OP)
            taken(pe, "ukT")
            taken(pe, ("dq", 3))
            for h in range(8):
                hf = slice((h % 2) * HD, (h % 2) * HD + HD)
                o = begin(("ql", h))
                nc.tensor.matmul(o, ukT[hf, (h // 2) * P:(h // 2 + 1) * P], A(e_dq + (h // 2) * S)[hf, :],
                                 start=True, stop=True).then_inc(psum_full, 1)
            pe.wait_ge(rp_ready, 8)
            for kind in range(2):
                o = begin(("hid", kind))
                for kc in range(2):
                    w = arrived(pe, ("w1", kind, kc))
                    for k in range(KT):
                        c = rp_at + kind * 992 + (8 * kc + k) * 62
                        mm = nc.tensor.matmul(o[0:62, 0:256], mix[:, c:c + 62], w[:, k, :],
                                              start=kc == 0 and k == 0, stop=kc == 1 and k == KT - 1)
                    mm.then_inc(psum_full if kc else part_used, 1)
            for kind in range(2):
                taken(pe, ("hid", kind))
                o = begin(("hidT", kind))
                for half in range(2):
                    mm = nc.tensor.transpose(o[:, half * 62:(half + 1) * 62],
                                             hid_rows(kind)[:, half * P:(half + 1) * P], ident[0:62, 0:62])
                mm.then_inc(psum_full, 1)
            taken(pe, ("hidT", 1))
            o = begin("kcT")
            for g in range(2):
                for half in range(2):
                    mm = nc.tensor.matmul(o[g * HD:(g + 1) * HD, 0:NCMP], w2kv[:, half * HD:(half + 1) * HD],
                                          hid[:, half * 62 + g * NCMP:half * 62 + (g + 1) * NCMP],
                                          start=half == 0, stop=half == 1)
            mm.then_inc(psum_full, 1)
            o = begin("vct")
            for g in range(2):
                for half in range(2):
                    mm = nc.tensor.matmul(o[0:NCMP, g * HD:(g + 1) * HD],
                                          hid[:, 124 + half * 62 + g * NCMP:124 + half * 62 + (g + 1) * NCMP],
                                          w2kv[:, 128 + half * HD:128 + (half + 1) * HD],
                                          start=half == 0, stop=half == 1)
            mm.then_inc(psum_full, 1)
            taken(pe, "vct")
            taken(pe, "ckvT")
            attention(pl.even)
            last_dense(("mo", 0), 2, H_OP, 3)
            mlp_pe(0, 4)

            dense_pair([("oq", 0), ("oq", 1)], [("oq", 0)] * 2, H_OP, 5)
            for name in ("oq", "ok", "ov"):
                for t in range(2 if name == "oq" else 0, KT):
                    dense((name, t), (name, t // 2), H_OP)
                    if name == "ov" and t:
                        taken(pe, ("ov", t - 1))
                        turn(("ovT", t - 1), A(o_tmp + ((t - 1) % 2) * S))
            taken(pe, ("ov", 7))
            turn(("ovT", 7), A(o_tmp + S))
            taken(pe, ("ovT", 7))
            pe.wait_ge(memsets, 6)
            pe.wait_ge(sel_ready, 1)
            attention(pl.odd)
            mean_squares("msB", range(EARLY_HEADS, HEADS))

            last_banks = [begin(("rb", h)) for h in range(EARLY_HEADS, HEADS)]

            def last_heads():
                for h, bank in zip(range(EARLY_HEADS, HEADS), last_banks):
                    spread(h, bank)

            last_dense(("mo", 1), 4, H_OP, 6, last_heads)
            mlp_pe(1, 7)
            for c in range(2):
                for k in range(4 * c, 4 * c + 4):
                    pe.wait_ge(x_ready, k + 1)
                for tt in range(NT):
                    o = begin(("y", tt, c))
                    for k in range(4):
                        mm = nc.tensor.transpose(o[:, k * P:(k + 1) * P], X(4 * c + k)[:, tt * P:(tt + 1) * P], ident[:, :])
                    mm.then_inc(psum_full, 1)
            assert made[0] == len(pl.order) and part[0] == len(pl.parts)

        def load_rows(eng, l):
            for dst, src in ((lng_row, bcast(a["gmlp_ln_g"], 512, l * 512)),
                             (lnb_row, bcast(a["gmlp_ln_b"], 512, l * 512)),
                             (bs_row, bcast(a["b_spatial"], 512, l * 512))):
                eng.dma_start(dst, src).then_inc(rows_in, 16)
            eng.dma_start(ws_raw.rearrange("p (g s) -> p g s", g=4), a["w_spatial"][l].rearrange("g t s -> t g s"))\
                .then_inc(rows_in, 16)

        @block.scalar
        def _(act):

            def sqrt(out_, in_, bias):
                nc.scalar.activation(out_, in_, ACT.Sqrt, bias=bias).then_inc(std_ready, 1)

            def drain(key, dst, func=ACT.Copy, bias=0.0, scale=1.0, m=slice(0, P), n=slice(0, S)):
                o = full(act, key)
                nc.scalar.activation(dst, o[m, n], func, bias=bias, scale=scale).then_inc(act_drained, 1)

            fed = [0]

            def feed(upto, limit):
                while fed[0] < min(upto, limit, len(pl.parts)):
                    q = fed[0]
                    name, src, _, _ = pl.parts[q]
                    view = arrived(act, name)
                    if q >= SPLITS:
                        freed(act, pl.parts[q - SPLITS][3])
                    nc.scalar.activation(part_view(w_hi, q), part_source(view, src), ACT.Copy).then_inc(w_hi_ready, 1)
                    fed[0] += 1

            limit = [pl.phase[0]]

            def pace(key):
                feed(pl.part_of[key] + 1 + SPLITS, limit[0])

            def dense(key, dst, func=ACT.Copy, bias=0.0, scale=1.0):
                pace(key)
                drain(key, dst, func, bias, scale)

            def round_tiles(src, tiles=range(KT), ready=None):
                for t in tiles:
                    if ready:
                        ready(t)
                    nc.scalar.activation(tile(hi_r, t), src(t), ACT.Copy).then_inc(hi_ready, 1)

            act.dma_start(ident[:, :], a["ident"]).then_inc(x_in, 16)
            for tt in (0, 1):
                act.dma_start(lo32[:, tt * D:(tt + 1) * D], a["x"][0, tt * P:(tt + 1) * P, :]).then_inc(x_in, 16)
            for dst, src in ((tril[:, :], a["tril"]), (sinks[:, :], bcast(a["attn_sinks"], 2 * HEADS)),
                             (alibi, a["alibi"])):
                act.dma_start(dst, src).then_inc(const_in, 16)
            load_rows(act, 0)
            for k in range(KT):
                o = full(act, ("xT", k))
                nc.scalar.activation(tile(hi_r, k), o, ACT.Copy).then_inc(hi_ready, 1)
                if k in (1, 3, 5):
                    feed(k // 2 + 1, limit[0])
            act.wait_ge(memsets, 4)

            taken(act, ("vec", 2))
            c0 = vec_b(0, "c")
            nc.scalar.activation(cact[:, :], cols[:, c0:c0 + KT], ACT.Silu).then_inc(c_ready, 1)

            def load_table(ti):
                h = tables[ti]
                src = bass.AP(tensor=bias_rows.tensor, offset=bias_rows.offset + h * P * TW + P - 1,
                              ap=[[TW - 1, P], [1, S]])
                act.dma_start(tbuf(ti), src).then_inc(t_in[ti % 3], 16)

            def exps(j):
                z = zbuf(j)
                if j is pl.even[0]:
                    taken(act, "miscT")
                    nc.scalar.activation(gates, gates, ACT.Sigmoid).then_inc(gates_ready, 1)
                if j.kind == "cmp":
                    act.wait_ge(m_ready, j.mr)
                    nc.scalar.activation(z[:, 0:4 * NCMP], z[:, 0:4 * NCMP], ACT.Exp, scale=-1.0).then_inc(p_ready, 1)
                    return
                if j.kind == "swa":
                    act.wait_ge(m_ready, j.mr)
                    spans = [(qb, (0, 128, 384, 640)[qb], 256 if qb else 128) for qb in range(4)]
                else:
                    spans = [(qb, ZOFF[qb], (qb + 1) * P) for qb in ORDER]
                for i, (qb, c, n) in enumerate(spans):
                    if j.kind != "swa":
                        act.wait_ge(z_ready, j.z0 + i + 1)
                    nc.scalar.activation(z[:, c:c + n], z[:, c:c + n], ACT.Exp, bias=stat4(negm, j, qb), scale=-1.0,
                                         accum_out=stat4(sums, j, qb)).then_inc(p_ready, 1)
                if j.kind == "swa":
                    h = HEADS * j.l + j.h
                    nc.scalar.activation(stat4(esink, j), stat4(negm, j), ACT.Exp, bias=sinks[:, h:h + 1])\
                        .then_inc(sink_ready, 1)
                if j.kind not in ("swa", "cmp") and j.t_last and j.ti + 3 < len(tables):
                    load_table(j.ti + 3)

            def drain_t(j):
                if not j.has_pt:
                    return
                pt = ptbuf(j)
                if j.pt >= 2:
                    act.wait_ge(pv_done, j.pt - 1)
                if j.kind == "cmp":
                    drain(("T", j.J, 0), pt[0:NCMP, 0:512], m=slice(0, NCMP))
                else:
                    drain(("T", j.J, 0), pt[:, 0:512])
                    if j.kind != "swa":
                        if j.kind in ("dsa", "diff"):
                            drain(("T", j.J, 1), pt[:, 512:896], n=slice(0, 384))
                        drain(("T", j.J, 2), pt[:, 896:1280], n=slice(0, 384))

            def warm_up():
                nc.scalar.activation(small[:, 4:5], eps[:, :], ACT.Sqrt).then_inc(warm, 1)

            def mean_copy(n):
                act.wait_ge(stat_full, 3 * n + 1)
                nc.scalar.activation(stat_row(), psum[:, 6, :], ACT.Copy, scale=2.0).then_inc(mean_copied, 1)

            def squares(n, tiles):
                for t in tiles:
                    if t < 6:
                        act.wait_ge(ln_centered, 6 * n + t + 1)
                    else:
                        taken(act, norm_key(n) + (t,))
                    nc.scalar.activation(M(t), X(t), ACT.Square).then_inc(ln_squared, 1)

            def offset_d(n):
                act.wait_ge(stat_full, 3 * n + 2)
                nc.scalar.activation(M(3), psum[:, 6, :], ACT.Square).then_inc(d_squared, 1)
                nc.scalar.activation(stat_row(), psum[:, 6, :], ACT.Copy).then_inc(d_copied, 1)

            def deviation(n):
                act.wait_ge(var_taken, n + 1)
                sqrt(dev_row(), dev_row(), eps[:, :])

            def last_dense(key, n):
                for t in range(6):
                    pace(key + (t,))
                warm_up()
                mean_copy(n)
                squares(n, range(6))
                pace(key + (6,))
                squares(n, (6,))
                pace(key + (7,))
                squares(n, (7,))
                offset_d(n)

            def offset_tiles(n):
                c = vec_a(0, "ln_b") if n == 0 else 32 * (n - 1) + 8
                if n:
                    act.wait_ge(ccols_ready, 4 * n)
                for t in range(KT):
                    act.wait_ge(ln_scaled, 8 * n + t + 1)
                    src, b = (H(t), ccols) if n else (X(t), cols)
                    nc.scalar.activation(tile(hi_r, t), src, ACT.Identity, bias=b[:, c + t:c + t + 1])\
                        .then_inc(hi_ready, 1)

            def block_2_loads():
                for dst, src in ((kvnorm, bcast(a["dsa_kv_norm_2"], P)), (future, a["future"])):
                    act.dma_start(dst, src).then_inc(mask_in, 16)
                e_loads = [(uk_raw, a["dsa_w_uk_2"][0].rearrange("r h d -> r (h d)"))]
                for i, name in enumerate(("nsa_w2_k_2", "nsa_w2_v_2")):
                    e_loads.append((w2kv[:, 128 * i:128 * i + 128].rearrange("p (k n) -> p k n", k=2),
                                    a[name][0].rearrange("(k p) n -> p k n", p=P)))
                for dst, src in e_loads:
                    act.dma_start(dst, src).then_inc(e_in, 16)
                with nc.allow_non_contiguous_dma("positional embeddings of 16 KB"):
                    for i, name in enumerate(("nsa_pe_k_2", "nsa_pe_v_2")):
                        src = bass.AP(tensor=a[name].tensor, offset=a[name].offset, ap=[[1, P], [P, 16]])
                        act.dma_start(peT[:, 16 * i:16 * i + 16], src).then_inc(e_in, 16)
                act.wait_ge(bias_out, 16)
                for ti in range(3):
                    load_table(ti)

            def bias_vectors():
                bias_sb = R(b1_q, TW)[0:16, :]
                drain(("bias", 0), bias_sb[:, 0:512], scale=-1.0, m=slice(0, 16))
                drain(("bias", 1), bias_sb[:, 512:TW], scale=-1.0, m=slice(0, 16), n=slice(0, TW - 512))
                taken(act, ("bias", 1))
                act.dma_start(bias_rows, bias_sb.unsqueeze(1).to_broadcast([16, P, TW])).then_inc(bias_out, 16)

            for l in range(DEPTH):
                def biased_tile(name, t, dst, func):
                    c = vec_a(l, name, t)
                    dense((name, l, t) if name not in ("k", "v") else (name, l), dst, func, bias=cols[:, c:c + 1])

                for t in range(4):
                    biased_tile("vg", t, ga(t), ACT.Gelu)
                if l == 0:
                    bias_vectors()
                for t in range(4):
                    biased_tile("u", t, ug[:, t * S:(t + 1) * S], ACT.Gelu)
                biased_tile("v", 0, R(b1_vT), ACT.Identity)
                biased_tile("k", 0, R(b1_k), ACT.Identity)
                act.wait_ge(var_ready, l + 1)
                sqrt(stats[:, 32:36], stats[:, 32:36], eps[:, :])
                for t in range(4):
                    biased_tile("za", t, za[:, t * S:(t + 1) * S], ACT.Silu)
                for t in range(4):
                    biased_tile("zg", t, R(b1_zg + t * S), ACT.Silu)
                for t in range(4):
                    pace(("q", l, t))
                jobs = pl.swa[l]
                exps(jobs[0])
                exps(jobs[1])
                for s in range(8):
                    for t in range(2 * s, 2 * s + 2):
                        biased_tile("g", t, ga(t), ACT.Identity)
                    if s + 2 < 8:
                        exps(jobs[s + 2])
                    drain_t(jobs[s])
                act.wait_ge(act_drained, u[("T", jobs[7].J, 0)].drained)
                for i in range(4):
                    for v in (R(b1_ga + 2 * i * S, 2 * S), lo32[:, 2 * i * S:2 * (i + 1) * S]):
                        nc.scalar.activation(v, v, ACT.Sigmoid).then_inc(sig_ready, 1)
                if l + 1 < DEPTH:
                    taken(act, ("sp", l, 3))
                    load_rows(act, l + 1)
                for t in range(KT):
                    pace(("ba", l, t))
                    pace(("bg", l, t))
                last_dense(("out", l), l)
                if l == 1:
                    block_2_loads()
                deviation(l)
                offset_tiles(l)

            dense("lat", A(e_tmp))
            dense("ik", A(e_ik))
            dense("misc", A(e_tmp + S))
            for t in range(4):
                dense(("iq", t), A(e_iq + t * S))
            act.wait_ge(var_ready, DEPTH + 1)
            sqrt(stats[:, 0:4], stats[:, 0:4], eps[:, :])
            i = 0
            for qb in range(1, 4):
                n = (qb + 1) * P
                for j in range(8):
                    if i >= 2:
                        act.wait_ge(isc_used, i - 1)
                    c = relu_at + (i % 2) * S
                    drain(("I", qb, j), mix[:, c:c + n], ACT.Relu, n=slice(0, n))
                    if qb < 3 and j % 4 == 3:
                        t = (qb - 1) * 2 + j // 4
                        dense(("dq", t), A(e_dq + t * S), scale=-HD ** -0.5)
                    i += 1
            dense("kc", A(e_kc))
            dense("vc", A(e_vc))
            act.wait_ge(act_drained, u["vc"].drained)
            for kind, at_ in enumerate((e_kc, e_vc)):
                for g in range(2):
                    dst = tile(mix, 2 * kind + g)
                    src = A(at_)[g * HD:(g + 1) * HD, :]
                    act.dma_start(dst[0:HD, :], src).then_inc(r_in, 16)
                    act.dma_start(dst[HD:P, 0:S - 1], src[:, 1:S]).then_inc(r_in, 16)
            for v_, k_, tmp, at_v, at_k in (("vs", "ks", e_tmp, e_vs, e_ks), ("vw", "kw", e_tmp + S, e_vw, e_kw)):
                dense(v_, A(tmp))
                dense(k_, A(at_k))
                drain(v_ + "T", A(at_v))
            act.wait_ge(future_used, 3)
            for t in range(4):
                dense(("nq", t), A(e_q + t * S), scale=-HD ** -0.5)
            for h in range(8):
                drain(("ql", h), A(e_ql + h * S))
            act.wait_ge(psum_full, u[("ql", 7)].full)
            act.dma_start(w_uv, a["dsa_w_uv_2"][0].rearrange("r h d -> r (h d)")).then_inc(uv_in, 16)
            for kind in range(2):
                drain(("hid", kind), hid_rows(kind), ACT.Gelu_apprx_tanh, m=slice(0, 62), n=slice(0, 256))
            for kind in range(2):
                drain(("hidT", kind), hid[:, 124 * kind:124 * kind + 124], n=slice(0, 124))
            drain("kcT", kcT, n=slice(0, NCMP))
            drain("vct", vct[0:NCMP, :], m=slice(0, NCMP), n=slice(0, P))

            def root(key, i):
                o = full(act, key)
                nc.scalar.activation(head_rms[i], o[0:HEADS, :], ACT.Sqrt, bias=eps[0:HEADS, :])\
                    .then_inc(act_drained, 1)

            def closing(i, last_job):
                act.wait_ge(psum_full, u[("T", last_job.J, last_job.ptn - 1)].full)
                limit[0] = pl.phase[1] if i == 0 else len(pl.parts)
                feed(pl.phase[i] + SPLITS, limit[0])
                if i == 0:
                    for t in range(4):
                        act.wait_ge(o_drained, pl.even[6 * t + 5].o + 1)
                    round_tiles(M, range(4))

            def attention(jobs):
                for j in jobs[:AHEAD]:
                    exps(j)
                for s in range(len(jobs) + 2):
                    if s < len(jobs):
                        drain_t(jobs[s])
                    if s + AHEAD < len(jobs):
                        exps(jobs[s + AHEAD])
                    if 0 <= s - 1 < len(jobs) and jobs[s - 1].kind == "diff" and jobs[s - 1].m:
                        h = jobs[s - 1].h
                        act.wait_ge(o_drained, jobs[s - 1].o + 1)
                        nc.scalar.activation(H(h), M(h), ACT.Square).then_inc(sq_ready, 1)
                    if 0 <= s - 2 < len(jobs) and jobs[s - 2].kind == "dsa":
                        h = jobs[s - 2].h
                        m = slice((h % 2) * HD, (h % 2) * HD + HD)
                        drain(("uv", h), M(4 + h // 2)[m, :], m=m)
                    if s == 2 * EARLY_HEADS + 2 and jobs[s].kind == "diff":
                        root("msA", 0)
                    if s == len(jobs) - 1:
                        closing(int(jobs[s].kind == "diff"), jobs[s])

            attention(pl.even)

            def mixed(i):
                if i == 0:
                    taken(act, ("uv", 7))
                    round_tiles(M, range(4, KT))
                else:
                    for t in range(KT):
                        if t == 2:
                            root("msB", 1)
                        taken(act, ("rb", t))
                        round_tiles(M, (t,))
                last_dense(("mo", i), 2 + 2 * i)
                deviation(2 + 2 * i)
                offset_tiles(2 + 2 * i)

            def mlp_act(i):
                for half in range(2):
                    for t in range(16 * half, 16 * half + 16):
                        pace(("m1", i, t))
                        if t >= 8:
                            act.wait_ge(hidden_ready, 32 * i + t - 7)
                        if t == 7:
                            act.wait_ge(x_normed, 8 * (2 * i + 1) + 8)
                        drain(("m1", i, t), M(t % 8), ACT.Relu)
                    for t in range(0, 6 if half else 8, 2):
                        last = pl.part_of[("m2", i, half, t + 1)]
                        for q in range(last - 3, last + 1):
                            feed(q + 1 + SPLITS, limit[0])
                n, last = 3 + 2 * i, pl.part_of[("m2", i, 1, 7)]
                warm_up()
                mean_copy(n)
                squares(n, range(3))
                feed(last + 1, limit[0])
                squares(n, range(3, 6))
                feed(last + 2, limit[0])
                squares(n, (6,))
                feed(last + 3, limit[0])
                squares(n, (7,))
                offset_d(n)
                feed(last + 4, limit[0])
                deviation(n)

            mixed(0)
            mlp_act(0)
            offset_tiles(3)
            for i, at_ in ((0, o_q), (1, o_k), (2, o_v)):
                name = ("oq", "ok", "ov")[i]
                for t in range(KT):
                    if name == "ov" and t >= 2:
                        act.wait_ge(psum_full, u[("ovT", t - 2)].full)
                    dst = A(at_ + t * S) if name != "ov" else A(o_tmp + (t % 2) * S)
                    dense((name, t), dst, scale=-HD ** -0.5 if i == 0 else 1.0)
            act.wait_ge(lam_dots, 2)
            nc.scalar.activation(lamc[:, 2:4], lamc[:, 0:2], ACT.Exp).then_inc(lam_ready, 1)
            attention(pl.odd)
            mixed(1)
            mlp_act(1)
            for t in range(KT):
                act.wait_ge(ln_scaled, 8 * 5 + t + 1)
                c = vec_b(3, "ln_b", t)
                nc.scalar.activation(X(t), X(t), ACT.Identity, bias=cols[:, c:c + 1]).then_inc(x_ready, 1)
            for tt in range(NT):
                drain(("y", tt, 1), hi32[:, tt * D + S:(tt + 1) * D])

        @block.vector
        def _(dve):
            own = Steps(dve, dve_own)
            v = nc.vector
            stds = [0]

            def drain(key, dst, m=slice(0, P), n=slice(0, S)):
                o = full(dve, key)
                v.tensor_copy(dst, o[m, n]).then_inc(dve_drained, 1)

            def ada_sum(n):
                w = arrived(dve, ("ada", n))
                if n >= 2:
                    dve.wait_ge(psum_full, u[("ada", n - 2)].full)
                acc = R(acc_at + (n % 2) * 256, 256)
                own.step(v.tensor_scalar(acc, w[:, 0, :], cact[:, 0:1], None, ALU.mult))
                for k in range(1, KT):
                    own.settle()
                    ins = v.scalar_tensor_tensor(acc, w[:, k, :], cact[:, k:k + 1], acc, ALU.mult, ALU.add)
                    if k < KT - 1:
                        own.step(ins)
                    else:
                        ins.then_inc(acc_ready, 1)

            def ada_drain(n):
                o = full(dve, ("ada", n))
                b = N_A + 2 * n
                v.tensor_tensor(adac[:, 2 * n:2 * n + 2], o[:, 0:2], cols[:, b:b + 2], ALU.add).then_inc(dve_drained, 1)

            def modulations(i):
                taken(dve, ("ada", 24 * i + 23))
                for c in (ADA["sc1"], ADA["sc2"]):
                    one = adac[:, 48 * i + c:48 * i + c + 16]
                    v.tensor_scalar(one, one, 1.0, None, ALU.add).then_inc(ada_ready, 1)

            fed = [0]
            limit = [pl.phase[0]]

            def feed(upto):
                while fed[0] < min(upto, limit[0], len(pl.parts)):
                    q = fed[0]
                    name, src, _, _ = pl.parts[q]
                    i, _ = arrival[name]
                    view = slot_view(i, pieces(name)[0])
                    dve.wait_ge(w_hi_ready, q + 1)
                    v.tensor_tensor(part_view(w_lo, q), part_source(view, src), part_view(w_hi, q).bitcast(F32),
                                    ALU.subtract).then_inc(w_lo_ready, 1)
                    fed[0] += 1

            def pace(key):
                feed(pl.part_of[key] + 1 + SPLITS)

            def rest_tiles(i, src, dst, tiles=range(KT)):
                for t in tiles:
                    dve.wait_ge(hi_ready, 8 * i + t + 1)
                    v.tensor_tensor(tile(dst, t), src(t), HI(t), ALU.subtract).then_inc(op_ready, 1)

            def both_parts(src, hi, lo):
                own.settle()
                own.step(v.tensor_copy(hi, src))
                own.settle()
                return v.tensor_tensor(lo, src, hi.bitcast(F32), ALU.subtract)

            def biased(j):
                z = zbuf(j)
                before = pl.jobs[j.J - 4] if j.kind == "swa" and j.J >= 4 else j.before
                if before:
                    dve.wait_ge(psum_full, u[("T", before.J, before.ptn - 1)].full)
                if j.kind == "cmp":
                    dve.wait_ge(bc_ready, 4 * j.ti + 4)
                    o = full(dve, ("S", j.J, 0))[:, 0:4 * NCMP].rearrange("p (b n) -> p b n", b=4)
                    zz = z[:, 0:4 * NCMP].rearrange("p (b n) -> p b n", b=4)
                    bias = biasc.rearrange("p (h b n) -> p h b n", b=4, h=8)[:, j.h, :, :]
                    v.tensor_tensor(zz, o, bias, ALU.add).then_inc(z_ready, 1)
                    dve.wait_ge(z_ready, j.z)
                    own.step(v.tensor_reduce(stat4(negm, j), zz, AX_X, ALU.min))
                    own.settle()
                    own.step(v.tensor_scalar(stat4(negm, j), stat4(negm, j), 0.1 * MASKED, None, ALU.min))
                    own.settle()
                    v.tensor_tensor(zz, zz, stat4(negm, j).unsqueeze(2).to_broadcast([P, 4, NCMP]),
                                    ALU.subtract).then_inc(m_ready, 1)
                    return
                if j.kind == "swa":
                    for i in range(2):
                        o = full(dve, ("S", j.J, i))
                        c = 0
                        for qb in (2 * i, 2 * i + 1):
                            n = 256 if qb else 128
                            at = (0, 128, 384, 640)[qb]
                            v.tensor_tensor_reduce(
                                out=z[:, at:at + n], in0=o[:, c:c + n],
                                in1=alibi[:, j.h * 256 + 256 - n:(j.h + 1) * 256], scale=1.0, scalar=HUGE,
                                op0=ALU.add, op1=ALU.min, accum_out=stat4(negm, j, qb)).then_inc(z_ready, 1)
                            c += n
                    dve.wait_ge(z_ready, j.z)
                    h = HEADS * j.l + j.h
                    v.tensor_scalar(stat4(negm, j), stat4(negm, j), nsinks[:, h:h + 1], None, ALU.min)\
                        .then_inc(m_ready, 1)
                    return
                dve.wait_ge(t_in[j.ti % 3], 16 * (j.ti // 3 + 1))
                table = tbuf(j.ti)
                for i, qbs in enumerate(((0, 2), (1,), (3,))):
                    o = full(dve, ("S", j.J, i))
                    c = 0
                    for qb in qbs:
                        n, at = (qb + 1) * P, ZOFF[qb]
                        zz, bias = z[:, at:at + n], table[:, S - n:S]
                        first, second = o[:, c:c + n], bias
                        if j.kind == "dsa" and qb:
                            own.step(v.tensor_tensor(zz, o[:, c:c + n], bias, ALU.add))
                            own.settle()
                            first, second = zz, selm(qb)
                        v.tensor_tensor_reduce(out=zz, in0=first, in1=second, scale=1.0, scalar=HUGE,
                                               op0=ALU.add, op1=ALU.min, accum_out=stat4(negm, j, qb))\
                            .then_inc(z_ready, 1)
                        c += n

            def normalise(j):
                dve.wait_ge(p_ready, j.p)
                z, den, r = zbuf(j), stat4(sums, j), stat4(recips, j)
                cmp = z[:, 0:4 * NCMP].rearrange("p (b n) -> p b n", b=4)
                if j.kind == "swa":
                    dve.wait_ge(sink_ready, HEADS * j.l + pl.swa[j.l].index(j) + 1)
                    own.step(v.tensor_tensor(den, den, stat4(esink, j), ALU.add))
                else:
                    if j.kind == "cmp":
                        own.step(v.tensor_reduce(den, cmp, AX_X, ALU.add))
                        own.settle()
                    own.step(v.tensor_scalar(den, den, 1e-30, None, ALU.max))
                own.settle()
                own.step(v.reciprocal(r, den))
                own.settle()
                if j.kind == "diff" and j.m:
                    own.step(v.tensor_scalar(r, r, small[:, 6:7], None, ALU.mult))
                    own.settle()
                elif j.kind in ("cmp", "sel", "win"):
                    i = ("cmp", "sel", "win").index(j.kind)
                    dve.wait_ge(gates_ready, 1)
                    g = gates.rearrange("p (b f) -> p b f", b=4)[:, :, 3 * j.h + i]
                    own.step(v.tensor_tensor(r, r, g, ALU.mult))
                    own.settle()
                if j.kind == "cmp":
                    v.tensor_tensor(cmp, cmp, r.unsqueeze(2).to_broadcast([P, 4, NCMP]), ALU.mult)\
                        .then_inc(s_ready, 1)
                    return
                if j.kind == "swa":
                    spans = [(qb, (0, 128, 384, 640)[qb], 256 if qb else 128) for qb in range(4)]
                else:
                    spans = [(qb, ZOFF[qb], (qb + 1) * P) for qb in range(4)]
                if j.kind == "diff" and j.m:
                    dve.wait_ge(s_ready, j.s0)
                for qb, c, n in spans:
                    zz, rr = z[:, c:c + n], stat4(recips, j, qb)
                    if j.kind == "diff" and j.m:
                        z0 = zbuf(pl.jobs[j.J - 1])[:, c:c + n]
                        v.scalar_tensor_tensor(zz, zz, rr, z0, ALU.mult, ALU.add).then_inc(s_ready, 1)
                    else:
                        v.tensor_scalar(zz, zz, rr, None, ALU.mult).then_inc(s_ready, 1)

            def drain_t(j):
                if not j.has_pt or j.kind in ("cmp", "dsa", "diff"):
                    return
                if j.pt >= 2:
                    dve.wait_ge(pv_done, j.pt - 1)
                drain(("T", j.J, 1), ptbuf(j)[:, 512:896], n=slice(0, 384))

            def outputs(j):
                if not (j.has_pt and j.last_o):
                    return
                dve.wait_ge(pv_done, j.pv)
                bank = psum[:, 6 + j.o % 2, :]
                if j.kind == "swa":
                    t = j.h % 4
                    zt = za[:, t * S:(t + 1) * S]
                    v.tensor_tensor(zt, zt, bank, ALU.mult).then_inc(o_drained, 1)
                    dve.wait_ge(o_drained, j.o + 1)
                    both_parts(zt, tile(q_hi, t), tile(za_lo, t)).then_inc(ya_ready, 1)
                elif j.kind == "win":
                    v.tensor_copy(M(j.h % 4), bank).then_inc(o_drained, 1)
                elif j.kind == "dsa":
                    if j.h >= 2:
                        dve.wait_ge(psum_full, u[("uv", j.h - 2)].full)
                    v.tensor_copy(A(e_olat + (j.h % 2) * S), bank).then_inc(o_drained, 1)
                else:
                    v.tensor_copy(M(j.h), bank).then_inc(o_drained, 1)

            def invert(key, i):
                taken(dve, key)
                v.reciprocal(head_rms[i], head_rms[i]).then_inc(rms_ready, 1)

            def head_norm(h):
                o = full(dve, ("rb", h))
                v.scalar_tensor_tensor(M(h), M(h), small[:, 7:8], o, ALU.mult, ALU.mult).then_inc(dve_drained, 1)

            def attention(jobs):
                biased(jobs[0])
                for i in range(1, AHEAD):
                    biased(jobs[i])
                    normalise(jobs[i - 1])
                for s in range(len(jobs) + 2):
                    if s + AHEAD < len(jobs):
                        biased(jobs[s + AHEAD])
                    if s + AHEAD - 1 < len(jobs):
                        normalise(jobs[s + AHEAD - 1])
                    if s < len(jobs):
                        drain_t(jobs[s])
                    if 0 <= s - 1 < len(jobs):
                        outputs(jobs[s - 1])
                    if jobs[0].kind == "diff":
                        if s == 2 * EARLY_HEADS + 2:
                            invert("msA", 0)
                        for h in spread_after(jobs[s - 2]) if s >= 2 else ():
                            head_norm(h)

            def centre(n):
                dve.wait_ge(mean_copied, n + 1)
                for t in range(6):
                    v.tensor_tensor(X(t), X(t), stat_row(), ALU.subtract).then_inc(ln_centered, 1)
                for t in (6, 7):
                    own.step(v.tensor_tensor(X(t), X(t), stat_row(), ALU.subtract))

            def layer_norm(n, operand_at=None):
                dve.wait_ge(d_squared, n + 1)
                dve.wait_ge(stat_full, 3 * n + 3)
                v.tensor_tensor(dev_row(), psum[:, 7, :], M(3), ALU.subtract).then_inc(var_taken, 1)
                dve.wait_ge(d_copied, n + 1)
                for t in (6, 7):
                    own.step(v.tensor_tensor(X(t), X(t), stat_row(), ALU.subtract))
                stds[0] += 1
                dve.wait_ge(std_ready, stds[0])
                own.step(v.reciprocal(dev_row(), dev_row()))
                own.settle()
                if n == 0:
                    gain, off, b = cols, vec_a(0, "ln_g"), (cols, vec_a(0, "ln_b"))
                elif n == 5:
                    gain, off = cols, vec_b(3, "ln_g")
                else:
                    dve.wait_ge(ccols_ready, 4 * n)
                    gain, off, b = ccols, 32 * (n - 1), (ccols, 32 * (n - 1) + 8)
                dst = H if 0 < n < 5 else X
                for t in range(KT + 1):
                    if t < KT:
                        if t < 6:
                            dve.wait_ge(ln_shifted, 6 * n + t + 1)
                        v.scalar_tensor_tensor(dst(t), X(t), gain[:, off + t:off + t + 1], dev_row(),
                                               ALU.mult, ALU.mult).then_inc(ln_scaled, 1)
                    if n < 5 and t:
                        i = 8 * (operand_at[0]) + t
                        dve.wait_ge(hi_ready, i)
                        v.scalar_tensor_tensor(tile(operand_at[1], t - 1), dst(t - 1),
                                               b[0][:, b[1] + t - 1:b[1] + t], HI(t - 1),
                                               ALU.add, ALU.subtract).then_inc(op_ready, 1)

            for k in range(KT):
                o = full(dve, ("xT", k))
                dve.wait_ge(hi_ready, k + 1)
                v.tensor_tensor(tile(x_lo, k), o, HI(k), ALU.subtract).then_inc(dve_drained, 1)
                if k in (1, 3, 5):
                    feed(k // 2 + 1)
            for i, (c, n) in enumerate(((0, N_A), (N_A, N_B), (N_A + N_B, N_C))):
                drain(("vec", i), cols[:, c:c + n], n=slice(0, n))
            dve.wait_ge(const_in, 48)
            v.tensor_scalar(nsinks[:, :], sinks[:, :], -1.0, None, ALU.mult).then_inc(nsink_ready, 1)
            dve.wait_ge(nsink_ready, 1)

            for l in range(DEPTH):
                next_ada = [ADAS * l]

                def one_sum():
                    if next_ada[0] < ADAS * (l + 1):
                        ada_sum(next_ada[0])
                        next_ada[0] += 1
                        return next_ada[0] - 1
                    return None

                def two(name, c, act=None):
                    if (name, l, c) == ("vg", 0, 1):
                        dve.wait_ge(c_ready, 1)
                    n = one_sum() if (name, l, c) != ("vg", 0, 0) else None
                    for t in (2 * c, 2 * c + 1):
                        pace((name, l, t))
                        if act:
                            act(t)
                    if n is not None:
                        ada_drain(n)

                two("vg", 0)
                two("vg", 1)
                dve.wait_ge(rows_in, 64 * (l + 1))
                if l:
                    dve.wait_ge(psum_full, u[("wT", l - 1)].full)
                ws3 = ws_raw.rearrange("p (g s) -> p g s", g=4)
                v.tensor_tensor(ws3, ws3, tril[:, :].unsqueeze(1).to_broadcast([P, 4, P]), ALU.mult)\
                    .then_inc(ws_masked, 1)
                two("u", 0)
                for tt in range(NT):
                    drain(("vgT", l, tt), R(b1_vn + tt * S))
                drain(("wT", l), ws_t)
                bn = stats[:, 0:24].rearrange("p (t s) -> p t s", t=4)
                mv = stats[:, 24:32].rearrange("p (t s) -> p t s", t=4)
                rs = stats[:, 32:36]
                taken(dve, ("vgT", l, 3))
                for tt in range(NT):
                    own.step(v.bn_stats(bn[:, tt, :], R(b1_vn + tt * S)))
                own.settle()
                for tt in range(NT):
                    own.step(v.bn_aggr(mv[:, tt, :], bn[:, tt, :]))
                own.settle()
                v.tensor_copy(rs, mv[:, :, 1]).then_inc(var_ready, 1)
                two("u", 1)
                n = one_sum()
                for name in ("v", "k"):
                    pace((name, l))
                ada_drain(n)
                stds[0] += 1
                dve.wait_ge(std_ready, stds[0])
                own.step(v.reciprocal(rs, rs))
                own.settle()
                for tt in range(NT):
                    v.tensor_scalar(R(b1_vn + tt * S), R(b1_vn + tt * S), mv[:, tt, 0:1], rs[:, tt:tt + 1],
                                    ALU.subtract, ALU.mult).then_inc(vn_norm, 1)
                two("za", 0)
                two("za", 1)
                drain(("vT", l), R(b1_v))
                two("zg", 0)
                two("zg", 1)

                def query(t):
                    if l == 0 and t == 0:
                        dve.wait_ge(bias_out, 16)
                    c = vec_a(l, "q", t)
                    o = full(dve, ("q", l, t))
                    v.tensor_scalar(R(b1_q + t * S), o, cols[:, c:c + 1], -HD ** -0.5, ALU.add, ALU.mult)\
                        .then_inc(dve_drained, 1)

                two("q", 0, query)
                two("q", 1, query)
                for g in range(4):
                    o = full(dve, ("sp", l, g))
                    tmp = R(b1_z + (g % 2) * S)
                    bs = bs_row[:, g * P:(g + 1) * P].unsqueeze(1).to_broadcast([P, 4, P])
                    v.tensor_tensor(tmp.rearrange("p (b t) -> p b t", b=4), o.rearrange("p (b t) -> p b t", b=4),
                                    bs, ALU.add).then_inc(dve_drained, 1)
                    dve.wait_ge(dve_drained, u[("sp", l, g)].drained)
                    dve.wait_ge(uz_ready, 4 * l + g + 1)
                    zg = R(b1_zg + g * S)
                    own.step(v.tensor_tensor(zg, zg, tmp, ALU.mult))
                    both_parts(zg, tile(u_hi, g), tile(zg_lo, g)).then_inc(yg_ready, 1)
                jobs = pl.swa[l]
                biased(jobs[0])
                biased(jobs[1])
                normalise(jobs[0])
                for s in range(9):
                    if s + 2 < 8:
                        biased(jobs[s + 2])
                    if s + 1 < 8:
                        normalise(jobs[s + 1])
                    if s < 8:
                        two("g", s)
                        drain_t(jobs[s])
                    if s >= 1:
                        outputs(jobs[s - 1])
                for t in range(KT):
                    dve.wait_ge(sig_ready, 8 * l + 2 * (t // 2) + 2)
                    pace(("ba", l, t))
                    o = full(dve, ("ba", l, t))
                    v.tensor_tensor(ga(t), ga(t), o, ALU.mult).then_inc(dve_drained, 1)
                    pace(("bg", l, t))
                    o = full(dve, ("bg", l, t))
                    v.tensor_tensor(ga(8 + t), ga(8 + t), o, ALU.mult).then_inc(dve_drained, 1)
                    taken(dve, ("bg", l, t))
                    own.step(v.tensor_tensor(ga(t), ga(t), ga(8 + t), ALU.add))
                    dve.wait_ge(res_scaled, 8 * l + t + 1)
                    both_parts(ga(t), tile(hi_r, t), tile(ga_lo, t)).then_inc(merged, 1)
                if l == 1:
                    modulations(0)
                for t in range(KT):
                    if t < 6:
                        pace(("out", l, t))
                    o = full(dve, ("out", l, t))
                    if t == 6:
                        own.settle()
                    v.tensor_tensor(X(t), X(t), o, ALU.add).then_inc(dve_drained, 1)
                    if t == 5:
                        taken(dve, ("out", l, t))
                        centre(l)
                    if t >= 6:
                        pace(("out", l, t))
                layer_norm(l, (1 + l, x_lo if l == 0 else lo_r))

            for key in ("lat", "ik", "misc"):
                pace(key)
            drain("latT", A(e_ckv))
            taken(dve, "latT")
            dve.wait_ge(mask_in, 32)
            for tt in range(NT):
                own.step(v.tensor_tensor_reduce(out=R(PT_AT + 1200, P), in0=A(e_ckv + tt * P, P),
                                                in1=A(e_ckv + tt * P, P), scale=1.0, scalar=0.0, op0=ALU.mult,
                                                op1=ALU.add, accum_out=stats[:, tt:tt + 1]))
                own.settle()
            v.tensor_scalar(stats[:, 0:4], stats[:, 0:4], 1.0 / P, None, ALU.mult).then_inc(var_ready, 1)
            pace(("iq", 0))
            pace(("iq", 1))
            o = full(dve, "miscT").rearrange("p (b f) -> p b f", b=4)
            v.tensor_scalar(iw.rearrange("p (b f) -> p b f", b=4), o[:, :, 120:128], 8 ** -0.5 * 64 ** -0.5, None,
                            ALU.mult).then_inc(iw_ready, 1)
            v.tensor_copy(gates.rearrange("p (b f) -> p b f", b=4), o[:, :, 0:24]).then_inc(dve_drained, 1)
            pace(("iq", 2))
            pace(("iq", 3))
            stds[0] += 1
            dve.wait_ge(std_ready, stds[0])
            own.step(v.reciprocal(stats[:, 0:4], stats[:, 0:4]))
            own.settle()
            for tt in range(NT):
                c = A(e_ckv + tt * P, P)
                v.scalar_tensor_tensor(c, c, stats[:, tt:tt + 1], kvnorm, ALU.mult, ALU.mult).then_inc(lat_done, 1)
            drain("ckvT", A(e_ckvT))
            taken(dve, "ckvT")
            i = 0
            for qb in range(1, 4):
                n = (qb + 1) * P
                for j in range(8):
                    dve.wait_ge(act_drained, u[("I", qb, j)].drained)
                    c = relu_at + (i % 2) * S
                    relu = mix[:, c:c + n]
                    w = iw[:, 8 * qb + j:8 * qb + j + 1]
                    if j == 0:
                        v.tensor_scalar(work(qb), relu, w, None, ALU.mult).then_inc(isc_used, 1)
                    else:
                        dve.wait_ge(isc_used, i)
                        v.scalar_tensor_tensor(work(qb), relu, w, work(qb), ALU.mult, ALU.add).then_inc(isc_used, 1)
                    i += 1
                    if qb < 3 and j % 4 == 3:
                        pace(("dq", (qb - 1) * 2 + j // 4))
                dve.wait_ge(isc_used, i)
                diag = work(qb)[:, n - P:n]
                v.tensor_tensor(diag, diag, future, ALU.add).then_inc(future_used, 1)
            dve.wait_ge(future_used, 3)
            ahead = ["kc", "vc", "vs", "ks", "vw", "kw", "ukT"] + [("nq", t) for t in range(4)]

            def windows():
                dve.wait_ge(r_in, 128)
                dve.wait_ge(x_normed, 8)
                dve.wait_ge(e_in, 16 * N_E)
                for kind in range(2):
                    c = rp_at + kind * 992
                    rp = mix[:, c:c + 992].rearrange("p (j g n) -> p j g n", j=16, g=2)
                    for g in range(2):
                        src = tile(mix, 2 * kind + g).rearrange("p (n r) -> p r n", r=16)
                        for half in range(2):
                            pe_ = peT[:, 16 * kind + 8 * half:16 * kind + 8 * half + 8]
                            v.tensor_tensor(rp[:, 8 * half:8 * half + 8, g, :], src[:, 0:16:2, half:half + NCMP],
                                            pe_.unsqueeze(2).to_broadcast([P, 8, NCMP]), ALU.add).then_inc(rp_ready, 1)

            def one_ahead(key):
                if key == "ukT":
                    drain("ukT", ukT)
                else:
                    pace(key)

            for r in range(TOPK // 8):
                own.settle()
                for qb in range(1, 4):
                    own.step(v.max(m8[:, 8 * qb - 8:8 * qb], work(qb)))
                own.settle()
                for qb in range(1, 4):
                    own.step(v.match_replace(work(qb), m8[:, 8 * qb - 8:8 * qb], work(qb), -HUGE))
                if r and ahead:
                    one_ahead(ahead.pop(0))
                if r == 11:
                    windows()
            own.settle()
            for key in ahead:
                one_ahead(key)
            dve.wait_ge(psum_full, u[("nq", 3)].full)
            for qb in range(1, 4):
                v.tensor_scalar(selm(qb), work(qb), -0.5 * HUGE, MASKED, ALU.is_gt, ALU.mult).then_inc(selm_ready, 1)
            dve.wait_ge(selm_ready, 3)
            attention(pl.even)

            def after_attention(i):
                limit[0] = pl.phase[1] if i == 0 else len(pl.parts)
                feed(pl.phase[i] + SPLITS)

            def residual(key, n, gate, first, norm=None):
                for t in range(KT):
                    late = norm is not None and t >= 6
                    if t % 2 == 0 and key == ("m2", 0, 0):
                        ada_sum(32 + t)
                        ada_sum(33 + t)
                    if key[0] == "mo":
                        if not late:
                            pace(key + (t,))
                    elif t % 2 == 0:
                        last = pl.part_of[key + (t + 1,)]
                        if late:
                            feed(last + 2)
                        else:
                            for q in range(last - 3, last + 1):
                                feed(q + 1 + SPLITS)
                    o = full(dve, key + (t,))
                    if first:
                        dve.wait_ge(res_scaled, 8 * n + 8 if norm is not None and t >= 5 else 8 * n + t + 1)
                    if norm is not None and t == 6:
                        own.settle()
                    v.scalar_tensor_tensor(X(t), o, adac[:, gate + t:gate + t + 1], X(t), ALU.mult, ALU.add)\
                        .then_inc(dve_drained, 1)
                    if norm is not None and t == 5:
                        taken(dve, key + (t,))
                        centre(norm)
                    if late:
                        if key[0] == "mo":
                            pace(key + (t,))
                        else:
                            feed(last + t - 3)
                    if t % 2 and key == ("m2", 0, 0):
                        ada_drain(31 + t)
                        ada_drain(32 + t)

            def mlp_dve(i):
                for half in range(2):
                    for t in range(16):
                        if i == 0 and t % 2 == 0:
                            ada_sum(24 + 16 * half + t // 2)
                        pace(("m1", i, 16 * half + t))
                        taken(dve, ("m1", i, 16 * half + t))
                        h = M(t % 8)
                        own.step(v.tensor_tensor(h, h, h, ALU.mult))
                        both_parts(h, tile(hid_hi, t), tile(hid_lo, t)).then_inc(hidden_ready, 1)
                        if i == 0 and t % 2:
                            ada_drain(24 + 16 * half + t // 2)
                    if i == 0 and half:
                        modulations(1)
                    residual(("m2", i, half), 3 + 2 * i, 48 * i + ADA["g2"], half == 0, 3 + 2 * i if half else None)
                if i:
                    layer_norm(5)
                else:
                    layer_norm(3, (5, lo_r))

            after_attention(0)
            rest_tiles(3, M, lo_r)
            residual(("mo", 0), 2, ADA["g1"], True, 2)
            layer_norm(2, (4, lo_r))
            mlp_dve(0)

            dve.wait_ge(ada_ready, 4)
            for name in ("oq", "ok", "ov"):
                for t in range(KT):
                    pace((name, t))
                    if name == "ov" and t:
                        drain(("ovT", t - 1), A(o_v + (t - 1) * S))
            drain(("ovT", 7), A(o_v + 7 * S))
            dve.wait_ge(lam_sem, 16)
            for i in range(2):
                v.tensor_tensor_reduce(out=lam_tmp[:, i * HD:(i + 1) * HD],
                                       in0=lam_in[:, 2 * i * HD:(2 * i + 1) * HD],
                                       in1=lam_in[:, (2 * i + 1) * HD:(2 * i + 2) * HD], scale=1.0, scalar=0.0,
                                       op0=ALU.mult, op1=ALU.add, accum_out=lamc[:, i:i + 1]).then_inc(lam_dots, 1)
            v.tensor_copy(sel.rearrange("p (h m) -> p h m", h=HEADS),
                          ident[0:HEADS, 0:HEADS].unsqueeze(2).to_broadcast([HEADS, HEADS, P])).then_inc(sel_ready, 1)
            c = vec_b(0, "subln")
            own.step(v.tensor_scalar(small[:, 7:8], cols[:, c:c + 1], 1.0 - LAMBDA_INIT, None, ALU.mult))
            own.settle()
            dve.wait_ge(lam_ready, 1)
            own.step(v.tensor_tensor(small[:, 6:7], lamc[:, 3:4], lamc[:, 2:3], ALU.subtract))
            own.settle()
            own.step(v.tensor_scalar(small[:, 6:7], small[:, 6:7], -LAMBDA_INIT, None, ALU.add))
            own.settle()
            dve.wait_ge(x_normed, 24)
            attention(pl.odd)
            after_attention(1)
            rest_tiles(6, M, lo_r, range(2))
            invert("msB", 1)
            rest_tiles(6, M, lo_r, range(2, EARLY_HEADS))
            for h in range(EARLY_HEADS, HEADS):
                head_norm(h)
            rest_tiles(6, M, lo_r, range(EARLY_HEADS, HEADS))
            residual(("mo", 1), 4, 48 + ADA["g1"], True, 4)
            layer_norm(4, (7, lo_r))
            mlp_dve(1)
            for tt in range(NT):
                drain(("y", tt, 0), hi32[:, tt * D:tt * D + S])

        @block.gpsimd
        def _(pool):
            g = nc.gpsimd

            def norm_sums(n, key):
                def add(dst, x0, x1, after):
                    if after:
                        pool.wait_ge(sum_ready, after)
                    g.tensor_tensor(dst, x0, x1, ALU.add).then_inc(sum_ready, 1)

                for t in range(4):
                    taken(pool, key + (t,))
                    if t:
                        add(M(7), X(0) if t == 1 else M(7), X(t), 9 * n + t - 1)
                pool.wait_ge(ln_squared, 8 * n + 2)
                add(M(0), M(0), M(1), None)
                pool.wait_ge(ln_squared, 8 * n + 4)
                add(M(2), M(2), M(3), None)
                add(M(0), M(0), M(2), 9 * n + 5)
                pool.wait_ge(ln_centered, 6 * n + 6)
                add(M(1), X(4), X(5), None)
                pool.wait_ge(ln_squared, 8 * n + 6)
                add(M(4), M(4), M(5), None)
                taken(pool, norm_key(n) + (6,))
                add(M(1), M(1), X(6), 9 * n + 7)
                pool.wait_ge(d_copied, n + 1)
                for t in range(6):
                    g.tensor_tensor(X(t), X(t), stat_row(), ALU.subtract).then_inc(ln_shifted, 1)

            def prescale(n):
                c = 32 * (n - 1) + 16
                for t in range(KT):
                    pool.wait_ge(ln_scaled, 8 * n + t + 1)
                    g.tensor_tensor(X(t), X(t), dev_row(), ALU.mult).then_inc(x_normed, 1)
                for t in range(KT):
                    pool.wait_ge(x_normed, 8 * (n - 1) + t + 1)
                    g.tensor_scalar(X(t), X(t), ccols[:, c + t:c + t + 1], ccols[:, c + 8 + t:c + 9 + t],
                                    ALU.mult, ALU.add).then_inc(res_scaled, 1)

            def column_products(n):
                i, j = divmod(n - 1, 2)
                gain, offset = (vec_a(1, "ln_g"), vec_a(1, "ln_b")) if n == 1 else (vec_b(n - 2, "ln_g"), vec_b(n - 2, "ln_b"))
                gain, offset = cols[:, gain:gain + 8], cols[:, offset:offset + 8]
                sc, sh = (48 * i + ADA[k] for k in (("sc1", "sh1") if j == 0 else ("sc2", "sh2")))
                c = 32 * (n - 1)
                scale, shift = adac[:, sc:sc + 8], adac[:, sh:sh + 8]
                pool.wait_ge(ada_ready, 2 * i + 2)
                g.tensor_tensor(ccols[:, c:c + 8], gain, scale, ALU.mult).then_inc(ccols_ready, 1)
                g.tensor_tensor(ccols[:, c + 8:c + 16], offset, scale, ALU.mult).then_inc(pool_own, 1)
                pool.wait_ge(pool_own, 8 + n)
                g.tensor_tensor(ccols[:, c + 8:c + 16], ccols[:, c + 8:c + 16], shift, ALU.add).then_inc(ccols_ready, 1)
                g.tensor_scalar(ccols[:, c + 16:c + 24], gain, ALPHA, None, ALU.mult).then_inc(ccols_ready, 1)
                g.tensor_scalar(ccols[:, c + 24:c + 32], offset, ALPHA, None, ALU.mult).then_inc(ccols_ready, 1)

            g.memset(mean_w[:, :], 1.0 / D).then_inc(memsets, 1)
            g.memset(head_w[:, :], 0.0).then_inc(memsets, 1)
            g.memset(eps[:, :], EPS).then_inc(memsets, 1)
            g.memset(ones[:, :], 1.0).then_inc(memsets, 1)
            pool.wait_ge(memsets, 4)
            g.memset(mix[BUCKETS:BUCKETS + 1, 384:400], -MASKED).then_inc(memsets, 1)
            pool.wait_ge(memsets, 5)
            g.memset(head_w[:, 7:8], 1.0 / P).then_inc(memsets, 1)
            for l in range(DEPTH):
                for tt in range(NT):
                    vn = R(b1_vn + tt * S)
                    pool.wait_ge(vn_norm, 4 * l + tt + 1)
                    g.tensor_tensor(vn, vn, lng_row, ALU.mult).then_inc(pool_own, 1)
                for tt in range(NT):
                    vn = R(b1_vn + tt * S)
                    pool.wait_ge(pool_own, 4 * l + tt + 1)
                    g.tensor_tensor(vn, vn, lnb_row, ALU.add).then_inc(vn_ready, 1)
                for t in range(4):
                    taken(pool, ("zg", l, t))
                    zg = R(b1_zg + t * S)
                    g.tensor_tensor(zg, zg, ug[:, t * S:(t + 1) * S], ALU.mult).then_inc(uz_ready, 1)
                pool.wait_ge(psum_full, u[("g", l, 15)].full)
                for t in range(KT):
                    g.tensor_tensor(X(t), tile(x_lo, t).bitcast(F32), HI(t), ALU.add).then_inc(x_whole, 1)
                for t in range(KT):
                    c = vec_a(l, "b_out", t)
                    pool.wait_ge(x_whole, 8 * l + t + 1)
                    g.tensor_scalar(X(t), X(t), ALPHA, cols[:, c:c + 1], ALU.mult, ALU.add).then_inc(res_scaled, 1)
                if l == 1:
                    column_products(1)
                    column_products(2)
                norm_sums(l, ("out", l))
            prescale(1)
            g.memset(biasc, MASKED).then_inc(memsets, 1)
            pool.wait_ge(memsets, 7)
            for ti in range(HEADS):
                pool.wait_ge(t_in[ti % 3], 16 * (ti // 3 + 1))
                for qb in range(NT):
                    n, c = (8 * (qb + 1)) - 1, S - (qb + 1) * P + 31
                    at_ = (tables[ti] * 4 + qb) * NCMP
                    g.tensor_copy(biasc[:, at_:at_ + n], tbuf(ti)[:, c:c + 16 * (n - 1) + 1:16]).then_inc(bc_ready, 1)
            norm_sums(2, ("mo", 0))
            prescale(2)
            column_products(3)
            column_products(4)
            norm_sums(3, ("m2", 0, 1))
            prescale(3)
            pool.wait_ge(psum_full, u[("oq", 0)].full)
            pool.dma_start(lam_in, bcast(a["diff_lam_2"], 256)).then_inc(lam_sem, 16)
            norm_sums(4, ("mo", 1))
            prescale(4)
            norm_sums(5, ("m2", 1, 1))


_INS = ["x", "w_in", "b_in", "attn_sinks", "gmlp_ln_g", "gmlp_ln_b", "w_spatial", "b_spatial", "w_branch_attn",
        "w_branch_gmlp", "w_out", "b_out", "ln_g", "ln_b", "c_2", "rel_bias_2", "ada_w_2", "ada_b_2", "ln_g_2",
        "ln_b_2", "ev_w_in_2", "ev_w_out_2", "nsa_pe_k_2", "nsa_pe_v_2", "nsa_w1_k_2", "nsa_w2_k_2", "nsa_w1_v_2",
        "nsa_w2_v_2", "dsa_kv_norm_2", "dsa_w_uk_2", "dsa_w_uv_2", "od_w_in_2", "od_w_out_2", "diff_lam_2",
        "diff_subln_2", "mlp_w1_2", "mlp_w2_2"]


def kernel(**inputs):
    import concourse.bacc as bacc
    from concourse.bass_utils import run_bass_kernel_spmd

    nc = bacc.Bacc("TRN2", target_bir_lowering=False, num_devices=1)
    given = {name: np.ascontiguousarray(inputs[name]) for name in _INS}
    given.update(shape_constants())
    arrays, a = {}, {}
    for name, value in given.items():
        arrays[f"in_{name}"] = value
        a[name] = nc.dram_tensor(f"in_{name}", value.shape, mybir.dt.from_np(value.dtype), kind="ExternalInput").ap()
    out = nc.dram_tensor("out_0", (1, S, D), F32, kind="ExternalOutput").ap()
    two_blocks(nc, a, out)
    r = run_bass_kernel_spmd(nc, [arrays], core_ids=[0])
    return r.results[0]["out_0"]
```
